# Optimizing a Trainium2 kernel written in Bass

```python
import math
import jax, jax.numpy as jnp
from jax import lax
import numpy as np

D_MODEL = 2048
BATCH = 1
SEQ = 256
DEPTH = 1

CHUNK = 64
EPS = 1e-5
HEAD_DIM = 64
N_HEADS = 32
N_KV = 8
GQ = N_HEADS // N_KV
WINDOW = 128
WIN_CHUNKS = WINDOW // CHUNK
Q_DIM = N_HEADS * HEAD_DIM
KV_DIM = N_KV * HEAD_DIM
SSD_EXPAND = 2
D_INNER = SSD_EXPAND * D_MODEL
SSD_HEAD_DIM = 64
SSD_HEADS = D_INNER // SSD_HEAD_DIM
SSD_GROUPS = 8
D_STATE = 128
CONV_K = 4
CONV_DIM = D_INNER + 2 * SSD_GROUPS * D_STATE
SSD_CHUNK = CHUNK
D_FF = 4 * D_MODEL
N_BRANCH = 2
SPLIT_SIZES = (Q_DIM, KV_DIM, KV_DIM, D_INNER, CONV_DIM, SSD_HEADS, N_BRANCH * D_MODEL)
SPLIT_IDX = tuple(int(i) for i in np.cumsum(SPLIT_SIZES)[:-1])
D_IN_PROJ = int(sum(SPLIT_SIZES))

kernel_name = "hybrid_swa_sink_alibi_ssd_gated_merge"

def rms_norm(x, w):
    xf = x.astype(jnp.float32)
    y = xf * lax.rsqrt(jnp.mean(xf * xf, axis=-1, keepdims=True) + EPS)
    return (y * w.astype(jnp.float32)).astype(x.dtype)

def alibi_slopes(n_heads):
    return 2.0 ** (-8.0 * jnp.arange(1, n_heads + 1, dtype=jnp.float32) / n_heads)

def sliding_window_attention(q, k, v, sinks):
    b, s = q.shape[:2]
    nc = s // CHUNK
    qc = q.reshape(b, nc, CHUNK, N_KV, GQ, HEAD_DIM)
    kc = k.reshape(b, nc, CHUNK, N_KV, HEAD_DIM)
    vc = v.reshape(b, nc, CHUNK, N_KV, HEAD_DIM)

    def band(t):
        tp = jnp.pad(t, ((0, 0), (WIN_CHUNKS - 1, 0), (0, 0), (0, 0), (0, 0)))
        return jnp.concatenate([tp[:, i:i + nc] for i in range(WIN_CHUNKS)], axis=2)

    kb, vb = band(kc), band(vc)
    scale = 1.0 / math.sqrt(HEAD_DIM)
    scores = jnp.einsum('bcqkgd,bcskd->bckgqs', qc, kb).astype(jnp.float32) * scale
    qi = jnp.arange(CHUNK)
    kj = jnp.arange(WIN_CHUNKS * CHUNK)
    dist = jnp.abs((WIN_CHUNKS - 1) * CHUNK + qi[:, None] - kj[None, :]).astype(jnp.float32)
    slopes = alibi_slopes(N_HEADS).reshape(N_KV, GQ)
    scores = scores - slopes[:, :, None, None] * dist
    key_chunk = jnp.arange(nc)[:, None] - (WIN_CHUNKS - 1) + kj[None, :] // CHUNK
    valid = key_chunk >= 0
    scores = jnp.where(valid[None, :, None, None, None, :], scores, -jnp.inf)
    sink = sinks.astype(jnp.float32).reshape(1, 1, N_KV, GQ, 1, 1)
    mx = jnp.maximum(jnp.max(scores, axis=-1, keepdims=True), sink)
    p = jnp.exp(scores - mx)
    probs = p / (jnp.sum(p, axis=-1, keepdims=True) + jnp.exp(sink - mx))
    out = jnp.einsum('bckgqs,bcskd->bcqkgd', probs.astype(v.dtype), vb)
    return out.reshape(b, s, Q_DIM)

def causal_dwconv(u, w, bias):
    y = lax.conv_general_dilated(
        u, w[:, None, :].astype(u.dtype), window_strides=(1,), padding=[(CONV_K - 1, 0)],
        dimension_numbers=('NWC', 'WIO', 'NWC'), feature_group_count=u.shape[-1])
    return y + bias.astype(u.dtype)

def ssd_chunked(xh, dt, A, Bm, Cm):
    b, s, h, p = xh.shape
    g, n = Bm.shape[2], Bm.shape[3]
    r = h // g
    nc = s // SSD_CHUNK
    L = SSD_CHUNK
    X = (xh * dt.astype(xh.dtype)[..., None]).reshape(b, nc, L, g, r, p)
    a = (dt * A).reshape(b, nc, L, g, r).transpose(0, 1, 3, 4, 2)
    Bc = Bm.reshape(b, nc, L, g, n)
    Cc = Cm.reshape(b, nc, L, g, n)
    a_cs = jnp.cumsum(a, axis=-1)
    causal = jnp.tril(jnp.ones((L, L), dtype=bool))
    seg = a_cs[..., :, None] - a_cs[..., None, :]
    Lmat = jnp.where(causal, jnp.exp(jnp.where(causal, seg, 0.0)), 0.0).astype(X.dtype)
    CB = jnp.einsum('bclgn,bcsgn->bcgls', Cc, Bc)
    y_diag = jnp.einsum('bcgls,bcgrls,bcsgrp->bclgrp', CB, Lmat, X)
    decay = jnp.exp(a_cs[..., -1:] - a_cs).astype(X.dtype)
    states = jnp.einsum('bclgn,bcgrl,bclgrp->bcgrpn', Bc, decay, X).astype(jnp.float32)
    chunk_decay = jnp.exp(a_cs[..., -1])

    def step(carry, inp):
        st, dec = inp
        return carry * dec[..., None, None] + st, carry

    init = jnp.zeros((b, g, r, p, n), jnp.float32)
    _, prev = lax.scan(step, init, (states.transpose(1, 0, 2, 3, 4, 5), chunk_decay.transpose(1, 0, 2, 3)))
    prev = prev.transpose(1, 0, 2, 3, 4, 5).astype(X.dtype)
    y_off = jnp.einsum('bclgn,bcgrpn,bcgrl->bclgrp', Cc, prev, jnp.exp(a_cs).astype(X.dtype))
    return (y_diag + y_off).reshape(b, s, h, p)

def gated_group_rmsnorm(y, z, w):
    yz = (y * jax.nn.silu(z)).astype(jnp.float32)
    sh = yz.shape
    yg = yz.reshape(sh[:-1] + (SSD_GROUPS, sh[-1] // SSD_GROUPS))
    yg = yg * lax.rsqrt(jnp.mean(yg * yg, axis=-1, keepdims=True) + EPS)
    return (yg.reshape(sh) * w.astype(jnp.float32)).astype(y.dtype)

def setup_inputs(seed: int = 0) -> dict:
    key = jax.random.key(seed)
    ks = jax.random.split(key, 20)
    f32 = jnp.float32
    nrm = lambda k, shape, s: jax.random.normal(k, shape, f32) * s
    dt0 = jnp.exp(jax.random.uniform(ks[8], (SSD_HEADS,), f32) * (math.log(0.1) - math.log(0.001)) + math.log(0.001))
    return {
        "x": nrm(ks[0], (BATCH, SEQ, D_MODEL), 1.0),
        "norm1_w": 1.0 + nrm(ks[1], (D_MODEL,), 0.02),
        "w_in": nrm(ks[2], (D_MODEL, D_IN_PROJ), D_MODEL ** -0.5),
        "gate_bias": nrm(ks[3], (N_BRANCH * D_MODEL,), 0.02),
        "attn_sinks": nrm(ks[4], (N_HEADS,), 1.0),
        "w_o_attn": nrm(ks[5], (Q_DIM, D_MODEL), Q_DIM ** -0.5),
        "conv_w": nrm(ks[6], (CONV_K, CONV_DIM), CONV_K ** -0.5),
        "conv_b": nrm(ks[7], (CONV_DIM,), 0.02),
        "dt_bias": dt0 + jnp.log(-jnp.expm1(-dt0)),
        "a_log": jnp.log(jax.random.uniform(ks[9], (SSD_HEADS,), f32, 1.0, 16.0)),
        "d_skip": 1.0 + nrm(ks[10], (SSD_HEADS,), 0.02),
        "ssd_norm_w": 1.0 + nrm(ks[11], (D_INNER,), 0.02),
        "w_o_ssd": nrm(ks[12], (D_INNER, D_MODEL), D_INNER ** -0.5),
        "w_out": nrm(ks[13], (D_MODEL, D_MODEL), D_MODEL ** -0.5),
        "norm2_w": 1.0 + nrm(ks[14], (D_MODEL,), 0.02),
        "w_up": nrm(ks[15], (D_MODEL, D_FF), D_MODEL ** -0.5),
        "w_down": nrm(ks[16], (D_FF, D_MODEL), D_FF ** -0.5),
        "norm_final_w": 1.0 + nrm(ks[17], (D_MODEL,), 0.02),
    }

def reference(x, norm1_w, w_in, gate_bias, attn_sinks, w_o_attn, conv_w, conv_b, dt_bias, a_log,
              d_skip, ssd_norm_w, w_o_ssd, w_out, norm2_w, w_up, w_down, norm_final_w):
    b, s, _ = x.shape
    for _layer in range(DEPTH):
        h = rms_norm(x, norm1_w)
        proj = h @ w_in
        q, k, v, z, xbc, dt_raw, gate_raw = jnp.split(proj, SPLIT_IDX, axis=-1)
        y_a = sliding_window_attention(q, k, v, attn_sinks) @ w_o_attn
        xbc = jax.nn.silu(causal_dwconv(xbc, conv_w, conv_b))
        xs, Bm, Cm = jnp.split(xbc, (D_INNER, D_INNER + SSD_GROUPS * D_STATE), axis=-1)
        xs = xs.reshape(b, s, SSD_HEADS, SSD_HEAD_DIM)
        Bm = Bm.reshape(b, s, SSD_GROUPS, D_STATE)
        Cm = Cm.reshape(b, s, SSD_GROUPS, D_STATE)
        dt = jax.nn.softplus(dt_raw.astype(jnp.float32) + dt_bias.astype(jnp.float32))
        A = -jnp.exp(a_log.astype(jnp.float32))
        y_s = ssd_chunked(xs, dt, A, Bm, Cm) + xs * d_skip.astype(xs.dtype)[:, None]
        y_s = gated_group_rmsnorm(y_s.reshape(b, s, D_INNER), z, ssd_norm_w) @ w_o_ssd
        g_a, g_s = jnp.split(jax.nn.sigmoid(gate_raw + gate_bias), N_BRANCH, axis=-1)
        x = x + (g_a * y_a + g_s * y_s) @ w_out
        u = rms_norm(x, norm2_w) @ w_up
        x = x + jnp.square(jax.nn.relu(u)) @ w_down
    return rms_norm(x, norm_final_w)


_drawn_inputs = setup_inputs


def setup_inputs(seed=0):
    import zlib

    import numpy as np

    out = dict(_drawn_inputs(seed))
    spreads = {}
    factors = {'norm1_w': 3.313,
     'gate_bias': 8.0,
     'attn_sinks': 29.536,
     'conv_b': 3.928,
     'd_skip': 200.0,
     'ssd_norm_w': 16.241,
     'norm2_w': 10.053,
     'norm_final_w': 22.412}
    for name, (base, spread) in spreads.items():
        noise = np.random.default_rng([zlib.crc32(name.encode()), seed]).standard_normal(out[name].shape)
        drawn = base * np.exp(spread * noise) if base else spread * noise
        out[name] = __import__('jax').numpy.asarray(drawn.astype(out[name].dtype))
    for name, factor in factors.items():
        out[name] = (out[name] * factor).astype(out[name].dtype)
    return out
```

```python
from contextlib import ExitStack

import concourse.bass as bass
from concourse import mybir

F32 = mybir.dt.float32
F32R = mybir.dt.float32r
ALU = mybir.AluOpType
ACT = mybir.ActivationFunctionType
AX = mybir.AxisListType.X

P = 128
T = 256
TT = T // P
D = 2048
KD = D // P
CHUNK = 64
N_CHUNKS = T // CHUNK
HD = 64
N_HEADS, N_KV = 32, 8
GQ = N_HEADS // N_KV
D_INNER = 2 * D
GROUPS = 8
HPG = D_INNER // HD // GROUPS
GW = D_INNER // GROUPS
SSD_HEADS = GROUPS * HPG
STATE = 128
CONV_K = 4
D_FF = 4 * D
EPS = 1e-5

Q0 = 0
K0 = Q0 + N_HEADS * HD
V0 = K0 + N_KV * HD
Z0 = V0 + N_KV * HD
X0 = Z0 + D_INNER
B0 = X0 + D_INNER
C0 = B0 + GROUPS * STATE
DT0 = C0 + GROUPS * STATE
G0 = DT0 + SSD_HEADS
D_IN = G0 + 2 * D

RING = 4
SLAB = 1024

V_N1, V_GB, V_CW, V_CB, V_SN, V_N2 = 0, 16, 48, 240, 288, 320
V_COLS = 336
C_ID, C_TRI, C_CUM, C_BLK, C_SLOPE, C_EPS, C_EPS4, C_ONE = 0, 128, 192, 320, 448, 480, 481, 482
C_COLS = 610
C_NEG, NEG_COLS = C_COLS, 3 * P

PHASES = [
    ("kv", 1, [(4, [0]), (4, [1]), (8, [2, 3]), (4, [0, 1])]),
    ("q", N_KV, [(4, [2])]),
    ("gate_a", 4, [(4, [3]), (4, [2])]),
    ("attn_out", 4, [(4, [3]), (4, [2])]),
    ("first_group", 1, [(4, [0]), (4, [1])]),
    ("group", GROUPS - 1, [(4, [0]), (8, [2, 3]), (4, [0]), (4, [1])]),
    ("last_group", 1, [(4, [0]), (8, [2, 3])]),
    ("gate_s", 4, [(4, [0]), (4, [1])]),
    ("ssd_out", 4, [(8, [2]), (8, [3])]),
    ("out", 1, [(8, [0, 1]), (8, [2, 3]), (8, [0, 1]), (8, [2, 3])]),
    ("up_a0", 4, [(4, [0]), (4, [1])]),
    ("up_a1", 4, [(4, [0]), (4, [1])]),
    ("down_a", 2, [(16, [2, 3]), (16, [0, 1])]),
    ("up_b0", 4, [(4, [2]), (4, [3])]),
    ("up_b1", 4, [(4, [2]), (4, [3])]),
    ("down_b", 1, [(16, [0, 1]), (16, [2, 3])]),
    ("down_end", 1, [(16, [0, 1]), (16, [2, 3])]),
]


def make_plan():
    plan, slab, uses = {}, 0, [0] * 4
    for name, iters, jobs in PHASES:
        per = [sum(b in banks for _, banks in jobs) for b in range(4)]
        plan[name] = dict(iters=iters, jobs=jobs, slab0=slab, slabs=sum(n for n, _ in jobs), use0=list(uses), uses=per)
        slab += iters * plan[name]["slabs"]
        uses = [u + iters * p for u, p in zip(uses, per)]
    return plan, slab


PLAN, N_SLABS = make_plan()
DT_SLAB = PLAN["kv"]["slab0"] + 16


def slab_no(phase, i, x):
    return PLAN[phase]["slab0"] + i * PLAN[phase]["slabs"] + x


def slot_round(phase, i, x):
    return PLAN[phase]["slab0"] // RING + i * (PLAN[phase]["slabs"] // RING) + x // RING


def bank_use(phase, i, job, bank):
    p = PLAN[phase]
    return p["use0"][bank] + i * p["uses"][bank] + sum(bank in banks for _, banks in p["jobs"][:job])


def job_end(phase, job):
    return sum(n for n, _ in PLAN[phase]["jobs"][: job + 1]) - 1


def loop(eng, phase, body, peel=0):
    n = PLAN[phase]["iters"]
    for i in range(peel):
        body(i)
    if n - peel == 1:
        body(peel)
    elif n > peel:
        with eng.Fori(peel, n) as i:
            body(i)


def hybrid_block(nc, x, w_in, w_o_attn, w_o_ssd, w_out, w_up, w_down, sinks, dt_bias, a_log, d_skip, norm_final_w,
                 channel_table, shape_table, out):
    with ExitStack() as ctx:
        def sb(name, shape, dt=F32):
            return ctx.enter_context(nc.sbuf_tensor(name, shape, dt))

        def sem(name):
            return ctx.enter_context(nc.semaphore(name))

        ps = [ctx.enter_context(nc.psum_tensor(f"bank{b}", [P, 512], F32)) for b in range(8)]

        raw = sb("raw", [P, RING, SLAB])
        w_hi = sb("w_hi", [P, RING, SLAB], F32R)
        w_lo = sb("w_lo", [P, RING, SLAB], F32R)
        act16 = sb("act16", [P, 16, 2 * T], F32R)
        act32 = sb("act32", [P, 32, 2 * T], F32R)
        xg = sb("xg", [P, 4096])
        ga = sb("ga", [P, 4096])
        scr = sb("scr", [P, 6040])
        chan = sb("chan", [P, V_COLS])
        const = sb("const", [P, C_COLS])
        sink_b = sb("sink_b", [P, N_HEADS])
        dskip_b = sb("dskip_b", [P, SSD_HEADS])
        dt_t = sb("dt_t", [P, TT, SSD_HEADS])
        a_t = sb("a_t", [P, TT, SSD_HEADS])
        acs_t = sb("acs_t", [P, TT, SSD_HEADS])
        ea_t = sb("ea_t", [P, TT, SSD_HEADS])
        dec_t = sb("dec_t", [P, TT, SSD_HEADS])
        cdec = sb("cdec", [P, N_CHUNKS, SSD_HEADS])
        ssq = sb("ssq", [P, TT, 4])
        small = sb("small", [P, 32])

        ident = const[:, C_ID:C_ID + P]
        tri = const[:, C_TRI:C_TRI + CHUNK]
        cum = const[:, C_CUM:C_CUM + P]
        blk = const[:, C_BLK:C_BLK + P]
        ones = const[:, C_ONE:C_ONE + P]
        neg_all = scr[:, 5184:5184 + NEG_COLS]
        negd = [neg_all[:, 0:P], neg_all[:, P:NEG_COLS]]
        x_sb = xg[:, :].rearrange("p (t n) -> p t n", t=TT)
        gs = xg[:, :].rearrange("p (f n) -> p f n", f=KD)
        ga_f = ga[:, :].rearrange("p (f n) -> p f n", f=KD)

        ks = scr[:, 0:2048].rearrange("p (j c t) -> p j c t", j=4, c=2)
        vs = scr[:, 2048:3072].rearrange("p (t n) -> p t n", t=TT)
        qt = scr[:, 3072:3584].rearrange("p (f t) -> p f t", f=2)
        kc = scr[:, 3584:3840]
        vc = scr[:, 3840:3968].rearrange("p (t n) -> p t n", t=TT)
        p0 = scr[:, 3968:4480].rearrange("p (g k) -> p g k", g=GQ)
        sm = scr[:, 4480:4544]
        mx, mm_, negm, es, rsum, den, rden = [sm[:, 8 * n:8 * n + 8] for n in range(7)]
        dt_tmp = scr[:, 4544:4544 + 5 * 128]
        p1 = xg[:, 0:1024].rearrange("p (g k) -> p g k", g=GQ)
        pt = xg[:, 1024:2560].rearrange("p (b n) -> p b n", b=3)
        upad = scr[:, 0:1560].rearrange("p (f n) -> p f n", f=6)
        cv = scr[:, 1560:3096].rearrange("p (f n) -> p f n", f=6)
        th = scr[:, 3096:4632].rearrange("p (f n) -> p f n", f=6)
        prev = scr[:, 3096:4632].rearrange("p (c n) -> p c n", c=3)
        btok = scr[:, 4632:4888].rearrange("p (t n) -> p t n", t=TT)
        mt = scr[:, 4888:5912].rearrange("p (t n) -> p t n", t=TT)
        cbm = scr[:, 5912:6040].rearrange("p (t l) -> p t l", t=TT)
        rs = xg[:, 0:1024].rearrange("p (t n) -> p t n", t=TT)
        sz = rs
        yb = xg[:, 1024:2048].rearrange("p (t n) -> p t n", t=TT)
        xdt = xg[:, 2048:3072].rearrange("p (t n) -> p t n", t=TT)
        xd = xg[:, 3072:4096].rearrange("p (t n) -> p t n", t=TT)
        xdec = scr[:, 1560:2584].rearrange("p (t n) -> p t n", t=TT)
        tu = scr[:, 0:1024].rearrange("p (b n) -> p b n", b=2)
        rrow = scr[:, 1024:1280]
        diag = scr[:, 1280:1536].rearrange("p (t n) -> p t n", t=TT)
        junk = scr[:, 2048:4096]
        wf = ga[:, 0:D]

        names = """x_loaded tables_loaded rows_loaded x_again wf_loaded stored
            hi_ready lo_ready slab_used
            ssq1_ready std1_ready rstd1_ready xn_ready xt_done h_hi h_lo half_ready
            k_kept v_kept dt_v dt_e dt_ready a_ready neg_a cums_done acs_ready tot_copied ea_ready dec_in dec_ready tail_b
            q_kept even_scores kc_ready vc_ready scores_done biased max_done shift_ready es_ready exp_done den_ready rden_ready
            probs_ready pt_done pt_act pt_dve pv_done attn_hi attn_lo
            gate_ready ya_ready
            pad_zero bc_in xa_in xb_in conv_bc conv_xa conv_xb th_bc th_x silu_bc silu_x rs_ready cb_done bt_done seg_out seg_min
            seg_exp btok_ready cbm_ready mt_ready xt_tr xs_used xdec_ready st_done prev1 prev2 prev3 prev_tmp yd0_done yd1_done
            y_part tz_ready sz_ready yo_done y_ready ssq_g std_g rstd_g yn_ready yt_done y_hi y_lo y_tmp
            gs_ready m_sum m_sum2 m_hi m_lo
            x2_ready sq2_ready x2t_done h2_hi h2_lo ssq2_sum std2 rstd2 diag_ready rr_done rr_ready
            u_relu u_hi u_sq u_lo x3_half x3_ready sq3_ready x3_w ssq3_sum std3 rstd3 out_act out_dve""".split()
        S = {n: sem(n) for n in names}
        raw_landed = [sem(f"raw_landed{s}") for s in range(RING)]
        bank_free = [sem(f"bank_free{b}") for b in range(4)]

        class Chain:
            def __init__(self, eng, s):
                self.eng, self.s, self.base, self.n = eng, s, 0, 0

            def at(self, start):
                self.base, self.n = start, 0

            def link(self, ins):
                self.n += 1
                ins.then_inc(self.s, 1)
                self.eng.wait_ge(self.s, self.base + self.n)

        def width_of(n):
            narrow = isinstance(n, int) and DT_SLAB <= n + RING < DT_SLAB + 4
            return 4 * SSD_HEADS if narrow else SLAB

        def raw_count(slot, phase, i, x):
            return (slot_round(phase, i, x) + 2) * 16

        block = ctx.enter_context(nc.Block())

        def feature_src(w, row_tile, col, width=256, kt=4):
            v = w.rearrange("(k p) n -> p k n", p=P)
            return v[:, row_tile:row_tile + kt, bass.ds(col, width)]

        @block.sync
        def _(sp):
            sp.dma_start(x_sb[:, 0, :], x[0, 0:P, :]).then_inc(S["x_loaded"], 16)
            sp.dma_start(x_sb[:, 1, :], x[0, P:T, :]).then_inc(S["x_again"], 16)

            def load(phase, i, xs, src, dst=None):
                n = slab_no(phase, i, xs)
                slot = xs % RING
                if not (isinstance(n, int) and n < RING):
                    sp.wait_ge(S["lo_ready"], n - RING + 1)
                dst = raw[:, slot, :] if dst is None else dst
                sp.dma_start(dst, src).then_inc(raw_landed[slot], 16)

            def feature_job(phase, i, x0, w, col, rows=KD):
                for s in range(rows // 4):
                    load(phase, i, x0 + s, feature_src(w, 4 * s, col),
                         raw[:, (x0 + s) % RING, :].rearrange("p (k n) -> p k n", k=4))

            def token_job(phase, i, x0, w, col, rows=KD, row0=0):
                for s in range(rows // 2):
                    load(phase, i, x0 + s, feature_src(w, row0 + 2 * s, col, 512, 2),
                         raw[:, (x0 + s) % RING, :].rearrange("p (k n) -> p k n", k=2))

            def bc_job(phase, i, x0, g):
                for s in range(4):
                    load(phase, i, x0 + s, feature_src(w_in, 8 * (s % 2), g * STATE + (B0 if s < 2 else C0), STATE, 8),
                         raw[:, (x0 + s) % RING, :].rearrange("p (k n) -> p k n", k=8))

            feature_job("kv", 0, 0, w_in, K0)
            feature_job("kv", 0, 4, w_in, K0 + 256)
            token_job("kv", 0, 8, w_in, V0)
            for s in range(4):
                load("kv", 0, 16 + s, feature_src(w_in, 4 * s, DT0, SSD_HEADS),
                     raw[:, s, 0:4 * SSD_HEADS].rearrange("p (k n) -> p k n", k=4))
            loop(sp, "q", lambda i: feature_job("q", i, 0, w_in, i * 256 + Q0))

            def gate(phase, col):
                def body(i):
                    for k in range(2):
                        feature_job(phase, i, 4 * k, w_in, i * 512 + (col + 256 * k))
                loop(sp, phase, body)

            def rows_out(phase, w, rows, col=0):
                def body(i):
                    for k in range(2):
                        feature_job(phase, i, (rows // 4) * k, w, i * 512 + (col + 256 * k), rows)
                loop(sp, phase, body)

            gate("gate_a", G0)
            rows_out("attn_out", w_o_attn, KD)
            bc_job("first_group", 0, 0, 0)
            feature_job("first_group", 0, 4, w_in, X0)

            def group(phase, g, i, last=False):
                feature_job(phase, i, 0, w_in, g * GW + (X0 + 256))
                token_job(phase, i, 4, w_in, g * GW + Z0)
                if not last:
                    bc_job(phase, i, 12, g + 1)
                    feature_job(phase, i, 16, w_in, g * GW + (X0 + GW))
            loop(sp, "group", lambda i: group("group", i, i))
            group("last_group", GROUPS - 1, 0, last=True)
            gate("gate_s", G0 + D)
            rows_out("ssd_out", w_o_ssd, 2 * KD)
            for n in range(4):
                token_job("out", 0, 8 * n, w_out, 512 * n)
                if n == 0:
                    sp.wait_ge(S["m_sum2"], 8)
                    for t in range(TT):
                        sp.dma_start(x_sb[:, t, :], x[0, t * P:(t + 1) * P, :]).then_inc(S["x_loaded" if t == 0 else "x_again"], 16)
                    sp.wait_ge(S["m_lo"], 8)
                    sp.dma_start(wf, norm_final_w.partition_broadcast(P)).then_inc(S["wf_loaded"], 16)

            def down(phase, i, half, nb0):
                for k in range(2):
                    token_job(phase, i, 16 * k, w_down, i * 1024 + (512 * k + 512 * nb0), 2 * KD, half * 2 * KD)

            for half, name in enumerate("ab"):
                for part in range(2):
                    rows_out(f"up_{name}{part}", w_up, KD, half * (D_FF // 2) + part * D)
                if half == 0:
                    loop(sp, "down_a", lambda i: down("down_a", i, 0, 0))
                else:
                    down("down_b", 0, 1, 0)
                    down("down_end", 0, 1, 2)
            for t, name in ((0, "out_act"), (1, "out_dve")):
                sp.wait_ge(S[name], 1)
                sp.dma_start(out[0, t * P:(t + 1) * P, :], x_sb[:, t, :]).then_inc(S["stored"], 16)
            sp.wait_ge(S["stored"], 32)

        @block.tensor
        def _(pe):
            mm = nc.tensor.matmul

            def split3(out_ap, a_hi, a_lo, b_hi, b_lo, start, stop):
                mm(out_ap, a_hi, b_hi, start=start, stop=False, skip_group_check=True)
                mm(out_ap, a_hi, b_lo, start=False, stop=False, skip_group_check=True)
                return mm(out_ap, a_lo, b_hi, start=False, stop=stop, skip_group_check=True)

            def bank_ready(phase, i, job, bank):
                u = bank_use(phase, i, job, bank)
                if not (isinstance(u, int) and u == 0):
                    pe.wait_ge(bank_free[bank], u)

            def feature_job(phase, i, job, acts, side=None, bc=False):
                n, (bank,) = PLAN[phase]["jobs"][job]
                x0 = job_end(phase, job) - n + 1
                bank_ready(phase, i, job, bank)
                for s in range(n):
                    slot = (x0 + s) % RING
                    pe.wait_ge(S["lo_ready"], slab_no(phase, i, x0 + s) + 1)
                    for c in range(8):
                        col, f, k = (c, s // 2, 8 * (s % 2) + c) if bc else (2 * (c % 4) + c // 4, c // 4, 4 * s + c % 4)
                        w = slice(128 * col, 128 * col + 128)
                        a = acts(k)
                        last = split3(ps[bank][:, f * T:(f + 1) * T], w_hi[:, slot, w], w_lo[:, slot, w],
                                      a[:, 0:T], a[:, T:2 * T], start=(s == 0 and c == 0),
                                      stop=(k == (KD if n == 4 else 2 * KD) - 1))
                    last.then_inc(S["slab_used"], 1)
                    if side:
                        side(x0 + s)

            def token_job(phase, i, job, acts, side=None, narrow=False):
                n, banks = PLAN[phase]["jobs"][job]
                x0 = job_end(phase, job) - n + 1
                kts, width = (4, SSD_HEADS) if narrow else (2, 512)
                for b in banks:
                    bank_ready(phase, i, job, b)
                for s in range(n):
                    slot = (x0 + s) % RING
                    pe.wait_ge(S["lo_ready"], slab_no(phase, i, x0 + s) + 1)
                    for k in range(kts):
                        c = slice(width * k, width * (k + 1))
                        a = acts(kts * s + k)
                        for t in range(TT):
                            last = split3(ps[banks[t]][:, 0:width], a[:, t * P:(t + 1) * P],
                                          a[:, T + t * P:T + (t + 1) * P], w_hi[:, slot, c], w_lo[:, slot, c],
                                          start=(s == 0 and k == 0), stop=(s == n - 1 and k == kts - 1))
                    last.then_inc(S["slab_used"], 1)
                    if side:
                        side(x0 + s)

            h = lambda k: act16[:, k, :]
            a32 = lambda k: act32[:, k, :]

            pe.wait_ge(S["tables_loaded"], 32)
            for r in range(KD // 2):
                pe.wait_ge(S["xn_ready"], 2)
                if r >= 4:
                    pe.wait_ge(S["h_lo"], 2 * (r - 4) + 2)
                for k in range(2):
                    for t in range(TT):
                        last = nc.tensor.transpose(ps[4 + r % 4][:, (2 * k + t) * P:(2 * k + t + 1) * P],
                                                   x_sb[:, t, (2 * r + k) * P:(2 * r + k + 1) * P], ident)
                last.then_inc(S["xt_done"], 1)
            pe.wait_ge(S["h_lo"], KD)

            feature_job("kv", 0, 0, h)
            feature_job("kv", 0, 1, h)
            token_job("kv", 0, 2, h)
            token_job("kv", 0, 3, h, narrow=True)

            def scores(j):
                pe.wait_ge(S["q_kept"], j + 1)
                pe.wait_ge(S["kc_ready"], j + 1)
                order = [(0, 0), (2, 0), (0, 1), (2, 1), (1, 1), (3, 1), (1, 0), (3, 0)]
                for g, t in order:
                    half = slice(64 * (g % 2), 64 * (g % 2) + 64)
                    if t == 0:
                        o, keys = ps[4][:, g * P:(g + 1) * P], P
                    else:
                        o, keys = ps[5 + g % 2][:, (g // 2) * T:(g // 2 + 1) * T], T
                    if (g, t) == (1, 0):
                        pe.wait_ge(S["even_scores"], j + 1)
                    last = mm(o, qt[half, g // 2, t * P:(t + 1) * P], kc[half, 0:keys], start=True, stop=True)
                    if (g, t) == (2, 0):
                        last.then_inc(S["even_scores"], 1)
                last.then_inc(S["scores_done"], 1)

            def probs_t(j):
                pe.wait_ge(S["probs_ready"], j + 1)
                for b in range(3):
                    for g in range(GQ):
                        src = p0[:, g, :] if b == 0 else p1[:, g, (b - 1) * P:b * P]
                        last = nc.tensor.transpose(ps[4 + b][:, g * P:(g + 1) * P], src, ident)
                last.then_inc(S["pt_done"], 1)

            def values(j):
                pe.wait_ge(S["pt_act"], j + 1)
                pe.wait_ge(S["pt_dve"], j + 1)
                pe.wait_ge(S["vc_ready"], j + 1)
                if not (isinstance(j, int) and j == 0):
                    pe.wait_ge(S["attn_lo"], j)
                for g in range(GQ):
                    half = slice(64 * (g % 2), 64 * (g % 2) + 64)
                    for t in range(TT):
                        o = ps[7][half, (g // 2) * T + t * P:(g // 2) * T + (t + 1) * P]
                        for k in range(t + 1):
                            last = mm(o, vc[:, k, :], pt[:, t + k, g * P:(g + 1) * P],
                                      start=(g < 2 and t == 0), stop=(k == t), skip_group_check=True)
                last.then_inc(S["pv_done"], 1)

            def attention(i, x, first=0):
                known = isinstance(i, int)
                if x == 2 and not (known and not 2 <= i < N_KV + 2):
                    probs_t(i - 2)
                if x == 3:
                    if not (known and not 2 <= i < N_KV + 2):
                        values(i - 2)
                    if not (known and not 1 <= i < N_KV + 1):
                        scores(i - 1)

            def cumsums():
                pe.wait_ge(S["a_ready"], 1)
                for t in range(TT):
                    mm(ps[7][:, t * 64:(t + 1) * 64], cum, a_t[:, t, :], start=True, stop=True)
                    mm(ps[7][:, 128 + t * 64:192 + t * 64], blk, a_t[:, t, :], start=True, stop=True)
                for c in (0, 2, 1, 3):
                    rows = slice(64 * (c % 2), 64 * (c % 2) + 64)
                    last = mm(ps[5 + c % 2][:, (c // 2) * 64:(c // 2 + 1) * 64], ones[rows, :], a_t[rows, c // 2, :],
                              start=True, stop=True)
                last.then_inc(S["cums_done"], 1)

            def q_body(i):
                def side(x):
                    if isinstance(i, int) and i == 0 and x == 3:
                        cumsums()
                    if isinstance(i, int) and i == 1 and x == 3:
                        pe.wait_ge(S["dec_ready"], 2)
                    attention(i, x)
                feature_job("q", i, 0, h, side)
            loop(pe, "q", q_body, peel=2)

            def gate_a_body(i):
                for k in range(2):
                    side = (lambda x, k=k: attention(N_KV + k, x - 4 * k)) if isinstance(i, int) and i == 0 else None
                    feature_job("gate_a", i, k, h, side)
            loop(pe, "gate_a", gate_a_body, peel=1)

            pe.wait_ge(S["attn_lo"], N_KV)

            def two_jobs(phase, acts):
                def body(i):
                    for k in range(2):
                        feature_job(phase, i, k, acts)
                return body
            loop(pe, "attn_out", two_jobs("attn_out", a32))

            feature_job("first_group", 0, 0, h, bc=True)
            feature_job("first_group", 0, 1, h)

            def ssd(g, x):
                known0 = isinstance(g, int) and g == 0
                if x == 1:
                    pe.wait_ge(S["rs_ready"], g + 1)
                    if not known0:
                        pe.wait_ge(S["y_part"], g * 4)
                    for t in range(TT):
                        mm(ps[4 + t][:, :], blk, rs[:, t, :], start=True, stop=True)
                    pe.wait_ge(S["silu_bc"], g + 1)
                    if not known0:
                        pe.wait_ge(S["y_lo"], g * 4)
                    for c in range(N_CHUNKS):
                        rows = slice(64 * (c % 2), 64 * (c % 2) + 64)
                        tok = slice(c * CHUNK, (c + 1) * CHUNK)
                        mm(ps[6][rows, (c // 2) * 64:(c // 2 + 1) * 64], cv[:, 4, tok], cv[:, 5, tok], start=True, stop=True)
                    for t in range(TT):
                        last = nc.tensor.transpose(ps[6][:, (1 + t) * P:(2 + t) * P], cv[:, 4, t * P:(t + 1) * P], ident)
                    last.then_inc(S["cb_done"], 1)
                if x == 7:
                    pe.wait_ge(S["silu_x"], g + 1)
                    pe.wait_ge(S["cbm_ready"], g + 1)
                    pe.wait_ge(S["btok_ready"], g + 1)
                    for t in range(TT):
                        for f in range(4):
                            last = nc.tensor.transpose(ps[7 - t][:, f * P:(f + 1) * P], cv[:, f, t * P:(t + 1) * P], ident)
                    last.then_inc(S["xt_tr"], 1)
                if x == 9:
                    pe.wait_ge(S["xdec_ready"], g + 1)
                    pe.wait_ge(S["seg_out"], 2 * g + 2)
                    pe.wait_ge(S["xs_used"], 4 * g + 4)
                    pe.wait_ge(S["mt_ready"], 2 * g + 2)
                    for c in range(3):
                        rows = slice(64 * (c % 2), 64 * (c % 2) + 64)
                        last = mm(ps[4 + c][:, :], btok[rows, c // 2, :], xdec[rows, c // 2, :], start=True, stop=True)
                    last.then_inc(S["st_done"], 1)
                    y_diag(0)
                if x == 13:
                    pe.wait_ge(S["prev3"], g + 1)
                    for c in range(1, N_CHUNKS):
                        rows = slice(64 * (c % 2), 64 * (c % 2) + 64)
                        last = mm(ps[5 + c // 2][rows, :], cv[:, 5, c * CHUNK:(c + 1) * CHUNK], prev[:, c - 1, :],
                                  start=True, stop=True)
                    last.then_inc(S["yo_done"], 1)
                    y_diag(1)
                if x == 19:
                    pe.wait_ge(S["yn_ready"], 2 * g + 2)
                    for f in range(4):
                        for t in range(TT):
                            last = nc.tensor.transpose(ps[6 + f // 2][:, (f % 2) * T + t * P:(f % 2) * T + (t + 1) * P],
                                                       yb[:, t, f * P:(f + 1) * P], ident)
                    last.then_inc(S["yt_done"], 1)

            def y_diag(t):
                for c in (2 * t, 2 * t + 1):
                    rows = slice(64 * (c % 2), 64 * (c % 2) + 64)
                    for r in range(HPG):
                        cols = slice(64 * r, 64 * r + 64)
                        last = mm(ps[7 if t == 0 else 4][rows, cols], mt[rows, t, cols], xdt[rows, t, cols],
                                  start=True, stop=True)
                last.then_inc(S["yd0_done" if t == 0 else "yd1_done"], 1)

            def group(phase, g, i, last=False):
                side = lambda x: ssd(g, x)
                feature_job(phase, i, 0, h, side)
                token_job(phase, i, 1, h, side)
                if not last:
                    feature_job(phase, i, 2, h, side, bc=True)
                    feature_job(phase, i, 3, h, side)
            loop(pe, "group", lambda i: group("group", i, i))
            group("last_group", GROUPS - 1, 0, last=True)

            def gate_s_body(i):
                side = (lambda x: ssd(GROUPS - 1, x + 12)) if isinstance(i, int) and i == 0 else None
                for k in range(2):
                    feature_job("gate_s", i, k, h, side)
            loop(pe, "gate_s", gate_s_body, peel=1)

            pe.wait_ge(S["y_lo"], 4 * GROUPS)
            loop(pe, "ssd_out", two_jobs("ssd_out", a32))

            pe.wait_ge(S["m_lo"], 8)

            def x2_t(nb):
                pe.wait_ge(S["x2_ready"], nb + 1)
                for q in range(2):
                    r = 2 * nb + q
                    if r >= 4:
                        pe.wait_ge(S["h2_lo"], 2 * (r - 4) + 2)
                    for k in range(2):
                        for t in range(TT):
                            last = nc.tensor.transpose(ps[4 + r % 4][:, (2 * k + t) * P:(2 * k + t + 1) * P],
                                                       x_sb[:, t, (2 * r + k) * P:(2 * r + k + 1) * P], ident)
                    last.then_inc(S["x2t_done"], 1)
            for n in range(4):
                token_job("out", 0, n, h, (lambda x, n=n: x2_t(n - 1) if n and x == 8 * n + 1 else None))
            x2_t(3)
            pe.wait_ge(S["h2_lo"], KD)

            def row_of_rstd():
                pe.wait_ge(S["diag_ready"], 1)
                mm(ps[4][:, 0:T], ones, diag[:, :, :], start=True, stop=True).then_inc(S["rr_done"], 1)

            def up_first(i):
                for k in range(2):
                    side = (lambda x: row_of_rstd() if x == 1 else None) if isinstance(i, int) and i == 0 and k == 0 else None
                    feature_job("up_a0", i, k, a32, side)

            def u_act(k):
                return act32[:, 16 + k, :] if k < 16 else act16[:, k - 16, :]

            def down(phase):
                def body(i):
                    for k in range(2):
                        token_job(phase, i, k, u_act)
                return body
            loop(pe, "up_a0", up_first, peel=1)
            loop(pe, "up_a1", two_jobs("up_a1", a32))
            pe.wait_ge(S["u_lo"], 16)
            loop(pe, "down_a", down("down_a"))
            loop(pe, "up_b0", two_jobs("up_b0", a32))
            loop(pe, "up_b1", two_jobs("up_b1", a32))
            pe.wait_ge(S["u_lo"], 32)
            down("down_b")(0)
            down("down_end")(0)

        @block.scalar
        def _(act):
            activation = nc.scalar.activation

            def split(phase, i, x):
                n = slab_no(phase, i, x)
                if isinstance(n, int) and n + RING >= N_SLABS:
                    return
                slot = x % RING
                act.wait_ge(S["slab_used"], n + 1)
                act.wait_ge(raw_landed[slot], raw_count(slot, phase, i, x))
                w = width_of(n)
                activation(w_hi[:, slot, 0:w], raw[:, slot, 0:w], ACT.Copy).then_inc(S["hi_ready"], 1)

            act.dma_start(const[:, :], shape_table[:, 0:C_COLS]).then_inc(S["tables_loaded"], 16)
            act.dma_start(neg_all, shape_table[:, C_NEG:C_NEG + NEG_COLS]).then_inc(S["rows_loaded"], 16)
            act.dma_start(chan[:, :], channel_table).then_inc(S["tables_loaded"], 16)
            act.dma_start(sink_b[:, :], sinks.partition_broadcast(P)).then_inc(S["rows_loaded"], 16)
            act.dma_start(dskip_b[:, :], d_skip.partition_broadcast(P)).then_inc(S["rows_loaded"], 16)
            act.dma_start(dt_tmp[:, 0:64], dt_bias.partition_broadcast(P)).then_inc(S["rows_loaded"], 16)
            act.dma_start(dt_tmp[:, 64:128], a_log.partition_broadcast(P)).then_inc(S["rows_loaded"], 16)

            for t, s in ((0, "x_loaded"), (1, "x_again")):
                act.wait_ge(S[s], 16)
                activation(ga[:, t * D:(t + 1) * D], x_sb[:, t, :], ACT.Square, accum_out=small[:, t:t + 1]).then_inc(S["ssq1_ready"], 1)
            act.wait_ge(S["ssq1_ready"], 2)
            act.wait_ge(S["tables_loaded"], 32)
            activation(small[:, 2:4], small[:, 0:2], ACT.Sqrt, scale=1.0 / D, bias=const[:, C_EPS:C_EPS + 1]) \
                .then_inc(S["std1_ready"], 1)
            for s in range(RING):
                act.wait_ge(raw_landed[s], 16)
                activation(w_hi[:, s, :], raw[:, s, :], ACT.Copy).then_inc(S["hi_ready"], 1)
            for r in range(KD // 2):
                act.wait_ge(S["xt_done"], r + 1)
                for k in (2 * r, 2 * r + 1):
                    activation(act16[:, k, 0:T], ps[4 + r % 4][:, (k % 2) * T:(k % 2 + 1) * T], ACT.Copy,
                               scale=chan[:, V_N1 + k:V_N1 + k + 1]).then_inc(S["h_hi"], 1)

            for x in range(20):
                if x == 15:
                    act.wait_ge(S["slab_used"], 16)
                    for t in range(TT):
                        activation(vs[:, t, :], ps[2 + t][:, :], ACT.Copy).then_inc(bank_free[2 + t], 1)
                if x == 19:
                    act.wait_ge(S["rows_loaded"], 80)
                    activation(dt_tmp[:, 64:128], dt_tmp[:, 64:128], ACT.Exp).then_inc(S["neg_a"], 1)
                    act.wait_ge(S["dt_v"], 1)
                    activation(dt_tmp[:, 256:384], dt_tmp[:, 256:384], ACT.Exp, scale=-1.0).then_inc(S["dt_e"], 1)
                split("kv", 0, x)

            def attention(i, x):
                known = isinstance(i, int)
                if not (known and not 2 <= i < N_KV + 2):
                    j = i - 2
                    if x == 0:
                        act.wait_ge(S["shift_ready"], j + 1)
                        for g in range(GQ):
                            activation(p0[:, g, :], p0[:, g, :], ACT.Exp, scale=0.125, bias=negm[:, g:g + 1],
                                       accum_out=rsum[:, g:g + 1])
                            activation(p1[:, g, :], p1[:, g, :], ACT.Exp, scale=0.125, bias=negm[:, 4 + g:5 + g],
                                       accum_out=rsum[:, 4 + g:5 + g])
                        activation(es, es, ACT.Exp).then_inc(S["exp_done"], 1)
                    if x == 2:
                        act.wait_ge(S["pt_done"], j + 1)
                        activation(pt[:, 0, :], ps[4][:, :], ACT.Copy)
                        activation(pt[:, 2, :], ps[6][:, :], ACT.Copy).then_inc(S["pt_act"], 1)
                    if x == 3:
                        act.wait_ge(S["pv_done"], j + 1)
                        activation(act32[:, bass.ds(2 * j, 2), 0:T], ps[7][:, :].rearrange("p (f t) -> p f t", f=2),
                                   ACT.Copy).then_inc(S["attn_hi"], 1)

            def q_body(i):
                for x in range(4):
                    if x == 3:
                        act.wait_ge(S["slab_used"], slab_no("q", i, 3) + 1)
                        if not (isinstance(i, int) and i == 0):
                            act.wait_ge(S["scores_done"], i)
                        activation(qt[:, :, :], ps[2][:, :].rearrange("p (f t) -> p f t", f=2), ACT.Copy) \
                            .then_inc(S["q_kept"], 1)
                    attention(i, x)
                    if isinstance(i, int) and i == 1 and x == 0:
                        act.wait_ge(S["acs_ready"], 1)
                        activation(ea_t[:, :, :], acs_t[:, :, :], ACT.Exp).then_inc(S["dec_ready"], 1)
                        act.wait_ge(S["dec_in"], 1)
                        activation(dec_t[:, :, :], dec_t[:, :, :], ACT.Exp)
                        for odd in range(2):
                            last = activation(cdec[:, odd::2, :], ps[5 + odd][:, 0:128].rearrange("p (c h) -> p c h", c=2),
                                              ACT.Exp)
                        last.then_inc(S["dec_ready"], 1)
                    split("q", i, x)
            loop(act, "q", q_body, peel=2)

            def gates(phase, dst, col, peel=0, side=None):
                def body(i):
                    for k in range(2):
                        for x in range(4 * k, 4 * k + 4):
                            if side and isinstance(i, int) and i == 0:
                                side(x)
                            if x == 4 * k + 3:
                                bank = PLAN[phase]["jobs"][k][1][0]
                                if phase == "gate_s" and isinstance(i, int):
                                    act.wait_ge(S["y_ready"], 2 * GROUPS)
                                act.wait_ge(S["slab_used"], slab_no(phase, i, x) + 1)
                                for f in range(2):
                                    ft = 4 * i + (2 * k + f)
                                    last = activation(dst[:, bass.ds(ft, 1), :],
                                                      ps[bank][:, f * T:(f + 1) * T].unsqueeze(1), ACT.Tanh, scale=0.5,
                                                      bias=chan[:, bass.ds(ft + col, 1)])
                                last.then_inc(bank_free[bank], 1)
                            split(phase, i, x)
                loop(act, phase, body, peel)
            act.wait_ge(S["half_ready"], 1)
            gates("gate_a", ga_f, V_GB, 1, lambda x: attention(N_KV + x // 4, x % 4))

            def only_split(phase):
                def body(i):
                    for x in range(PLAN[phase]["slabs"]):
                        split(phase, i, x)
                return body
            loop(act, "attn_out", only_split("attn_out"))

            def conv_in(phase, i, x, bank, f0, name):
                act.wait_ge(S["slab_used"], slab_no(phase, i, x) + 1)
                activation(upad[:, f0:f0 + 2, 4:4 + T], ps[bank][:, :].rearrange("p (f t) -> p f t", f=2), ACT.Copy) \
                    .then_inc(S[name], 1)

            act.wait_ge(S["pad_zero"], 1)
            for x in range(8):
                if x == 3:
                    conv_in("first_group", 0, 3, 0, 4, "bc_in")
                if x == 4:
                    act.wait_ge(S["conv_bc"], 8)
                    activation(th[:, 4:6, :], cv[:, 4:6, :], ACT.Tanh).then_inc(S["th_bc"], 1)
                if x == 7:
                    conv_in("first_group", 0, 7, 1, 0, "xa_in")
                split("first_group", 0, x)

            def ssd(g, x, phase, i, last=False):
                if x == 1:
                    act.wait_ge(S["cb_done"], g + 1)
                    activation(btok[:, :, :], ps[6][:, P:P + T].rearrange("p (t n) -> p t n", t=TT), ACT.Copy) \
                        .then_inc(S["btok_ready"], 1)
                if x == 3:
                    conv_in(phase, i, 3, 0, 2, "xb_in")
                    act.wait_ge(S["seg_out"], 2 * g + 2)
                    activation(mt[:, :, :], mt[:, :, :], ACT.Relu, scale=-1.0).then_inc(S["seg_min"], 1)
                    act.wait_ge(S["seg_min"], g + 1)
                    activation(mt[:, :, :], mt[:, :, :], ACT.Exp, scale=-1.0).then_inc(S["seg_exp"], 1)
                if x == 5:
                    act.wait_ge(S["conv_xb"], 8 * g + 8)
                    activation(th[:, 0:4, :], cv[:, 0:4, :], ACT.Tanh).then_inc(S["th_x"], 1)
                if x == 9:
                    act.wait_ge(S["st_done"], g + 1)
                    activation(prev[:, 0, :], ps[4][:, :], ACT.Copy).then_inc(S["prev1"], 1)
                if x == 11:
                    act.wait_ge(S["slab_used"], slab_no(phase, i, 11) + 1)
                    for t in range(TT):
                        activation(sz[:, t, :], ps[2 + t][:, :], ACT.Tanh, scale=0.5).then_inc(S["tz_ready"], 1)
                if x == 15 and not last:
                    conv_in(phase, i, 15, 0, 4, "bc_in")
                if x == 17 and not last:
                    act.wait_ge(S["conv_bc"], 8 * g + 16)
                    activation(th[:, 4:6, :], cv[:, 4:6, :], ACT.Tanh).then_inc(S["th_bc"], 1)
                if x == 16:
                    for t in range(TT):
                        act.wait_ge(S["y_ready"], 2 * g + t + 1)
                        activation(xdt[:, t, :], yb[:, t, :], ACT.Square, accum_out=small[:, 4 + t:5 + t]) \
                            .then_inc(S["ssq_g"], 1)
                    act.wait_ge(S["ssq_g"], 2 * g + 2)
                    activation(small[:, 6:8], small[:, 4:6], ACT.Sqrt, scale=1.0 / GW, bias=const[:, C_EPS4:C_EPS4 + 1]) \
                        .then_inc(S["std_g"], 1)
                if x == 18:
                    act.wait_ge(S["rstd_g"], g + 1)
                    for t in range(TT):
                        activation(yb[:, t, :], yb[:, t, :], ACT.Copy, scale=small[:, 8 + t:9 + t]).then_inc(S["yn_ready"], 1)
                if x == 19:
                    if not last:
                        conv_in(phase, i, 19, 1, 0, "xa_in")
                    act.wait_ge(S["yt_done"], g + 1)
                    for f in range(4):
                        activation(act32[:, bass.ds(4 * g + f, 1), 0:T],
                                   ps[6 + f // 2][:, (f % 2) * T:(f % 2 + 1) * T].unsqueeze(1), ACT.Copy,
                                   scale=chan[:, bass.ds(4 * g + (V_SN + f), 1)]).then_inc(S["y_hi"], 1)

            def group_body(i):
                for x in range(20):
                    ssd(i, x, "group", i)
                    split("group", i, x)
            loop(act, "group", group_body)
            for x in range(12):
                ssd(GROUPS - 1, x, "last_group", 0, last=True)
                split("last_group", 0, x)
            gates("gate_s", gs, V_GB + KD, 1, lambda x: (act.wait_ge(S["y_lo"], 4 * GROUPS - 4) if x == 0 else None,
                                                         ssd(GROUPS - 1, x + 12, None, None, last=True)))

            def ssd_out_body(i):
                for k in range(2):
                    for x in range(8 * k, 8 * k + 8):
                        if x == 8 * k + 7:
                            act.wait_ge(S["m_sum2"], 2 * i + (k + 1))
                            activation(act16[:, bass.ds(4 * i + 2 * k, 2), 0:T], ga_f[:, bass.ds(4 * i + 2 * k, 2), :],
                                       ACT.Copy, scale=0.5).then_inc(S["m_hi"], 1)
                        split("ssd_out", i, x)
            loop(act, "ssd_out", ssd_out_body)

            def x2_side(nb):
                for q in range(2):
                    r = 2 * nb + q
                    act.wait_ge(S["x2t_done"], r + 1)
                    for k in (2 * r, 2 * r + 1):
                        activation(act32[:, k, 0:T], ps[4 + r % 4][:, (k % 2) * T:(k % 2 + 1) * T], ACT.Copy,
                                   scale=chan[:, V_N2 + k:V_N2 + k + 1]).then_inc(S["h2_hi"], 1)

            def squares(nb, ready, done):
                act.wait_ge(S[ready], nb + 1)
                for t in range(TT):
                    n = 2 * nb + t
                    if n >= 4:
                        act.wait_ge(S[done], n - 3)
                    activation(junk[:, (n % 4) * 512:(n % 4 + 1) * 512], x_sb[:, t, nb * 512:(nb + 1) * 512], ACT.Square,
                               accum_out=ssq[:, t, nb:nb + 1]).then_inc(S[done], 1)
            for n in range(4):
                for x in range(8 * n, 8 * n + 8):
                    if n and x == 8 * n + 1:
                        x2_side(n - 1)
                    if x == 8 * n + 7:
                        squares(n, "x2_ready", "sq2_ready")
                    split("out", 0, x)
            x2_side(3)
            act.wait_ge(S["ssq2_sum"], 1)
            activation(small[:, 12:14], small[:, 10:12], ACT.Sqrt, scale=1.0 / D, bias=const[:, C_EPS:C_EPS + 1]) \
                .then_inc(S["std2"], 1)

            def up(phase, n0, dst, ft0):
                def body(i):
                    for k in range(2):
                        for x in range(4 * k, 4 * k + 4):
                            if x == 4 * k + 3:
                                act.wait_ge(S["u_relu"], 2 * i + (n0 + k + 1))
                                activation(dst[:, bass.ds(4 * i + (ft0 + 2 * k), 2), 0:T],
                                           tu[:, k, :].rearrange("p (f t) -> p f t", f=2), ACT.Square) \
                                    .then_inc(S["u_hi"], 1)
                            split(phase, i, x)
                loop(act, phase, body, peel=1 if phase == "up_a0" else 0)
            up("up_a0", 0, act32, 16)
            up("up_a1", 8, act16, 0)
            loop(act, "down_a", only_split("down_a"))
            up("up_b0", 16, act32, 16)
            up("up_b1", 24, act16, 0)
            for phase, nb0 in (("down_b", 0), ("down_end", 2)):
                for k in range(2):
                    for x in range(16 * k, 16 * k + 16):
                        if x == 16 * k + 15:
                            squares(nb0 + k, "x3_ready", "sq3_ready")
                        split(phase, 0, x)
            act.wait_ge(S["ssq3_sum"], 1)
            activation(small[:, 20:22], small[:, 18:20], ACT.Sqrt, scale=1.0 / D, bias=const[:, C_EPS:C_EPS + 1]) \
                .then_inc(S["std3"], 1)
            act.wait_ge(S["rstd3"], 1)
            activation(x_sb[:, 0, :], x_sb[:, 0, :], ACT.Copy, scale=small[:, 22:23]).then_inc(S["out_act"], 1)

        @block.vector
        def _(dve):
            v = nc.vector
            stt = v.scalar_tensor_tensor
            tt = v.tensor_tensor

            def split(phase, i, x):
                n = slab_no(phase, i, x)
                if isinstance(n, int) and n + RING >= N_SLABS:
                    return
                w = width_of(n)
                slot = x % RING
                dve.wait_ge(S["hi_ready"], n + RING + 1)
                tt(w_lo[:, slot, 0:w], raw[:, slot, 0:w], w_hi[:, slot, 0:w].bitcast(F32), ALU.subtract) \
                    .then_inc(S["lo_ready"], 1)

            def f2(ap):
                return ap.rearrange("p (f t) -> p f t", f=2)

            chain = Chain(dve, sem("dve_step"))

            dve.wait_ge(S["std1_ready"], 1)
            v.reciprocal(small[:, 2:4], small[:, 2:4]).then_inc(S["rstd1_ready"], 1)
            dve.wait_ge(S["rstd1_ready"], 1)
            for t in range(TT):
                v.tensor_scalar(x_sb[:, t, :], x_sb[:, t, :], small[:, 2 + t:3 + t], None, ALU.mult).then_inc(S["xn_ready"], 1)
            for s in range(RING):
                dve.wait_ge(S["hi_ready"], s + 1)
                tt(w_lo[:, s, :], raw[:, s, :], w_hi[:, s, :].bitcast(F32), ALU.subtract).then_inc(S["lo_ready"], 1)
            for k in range(KD):
                dve.wait_ge(S["h_hi"], 2 * (k // 2) + 2)
                stt(out=act16[:, k, T:2 * T], in0=ps[4 + (k // 2) % 4][:, (k % 2) * T:(k % 2 + 1) * T],
                    scalar=chan[:, V_N1 + k:V_N1 + k + 1], in1=act16[:, k, 0:T].bitcast(F32), op0=ALU.mult,
                    op1=ALU.subtract).then_inc(S["h_lo"], 1)
            v.tensor_scalar(chan[:, V_GB:V_SN], chan[:, V_GB:V_SN], 0.5, None, ALU.mult).then_inc(S["half_ready"], 1)

            a_exp, bias_b = dt_tmp[:, 64:128], dt_tmp[:, 0:64]
            val, e, sq, pol = [dt_tmp[:, 128 * n:128 * n + 128] for n in (1, 2, 3, 4)]
            v3 = lambda ap: ap.rearrange("p (t h) -> p t h", t=TT)
            for x in range(20):
                if x in (3, 7):
                    b = x // 4
                    dve.wait_ge(S["slab_used"], x + 1)
                    for par in range(2):
                        for half in range(2):
                            last = v.tensor_copy(ks[64 * half:64 * half + 64, 2 * b:2 * b + 2, par, :],
                                                 f2(ps[b][64 * par:64 * par + 64, :]))
                    last.then_inc(bank_free[b], 1)
                if x == 19:
                    dve.wait_ge(S["slab_used"], 20)
                    dve.wait_ge(S["rows_loaded"], 80)
                    for t in range(TT):
                        tt(v3(val)[:, t, :], ps[t][:, 0:64], bias_b, ALU.add).then_inc(bank_free[t], 1)
                    dve.wait_ge(bank_free[0], 2)
                    dve.wait_ge(bank_free[1], 2)
                    stt(out=e, in0=val, scalar=-1.0, in1=val, op0=ALU.mult, op1=ALU.max).then_inc(S["dt_v"], 1)
                    dve.wait_ge(S["dt_e"], 1)
                    chain.link(v.tensor_scalar(sq, e, 2.0, None, ALU.add))
                    chain.link(v.reciprocal(sq, sq))
                    chain.link(tt(e, e, sq, ALU.mult))
                    chain.link(tt(sq, e, e, ALU.mult))
                    chain.link(v.tensor_scalar(pol, sq, 1.0 / 17, None, ALU.mult))
                    for c in (15, 13, 11, 9, 7, 5, 3):
                        chain.link(stt(out=pol, in0=pol, scalar=1.0 / c, in1=sq, op0=ALU.add, op1=ALU.mult))
                    chain.link(stt(out=pol, in0=pol, scalar=1.0, in1=e, op0=ALU.add, op1=ALU.mult))
                    chain.link(v.tensor_scalar(val, val, 0.0, None, ALU.max))
                    chain.link(stt(out=dt_t[:, :, :], in0=v3(pol), scalar=2.0, in1=v3(val), op0=ALU.mult, op1=ALU.add))
                    dve.wait_ge(S["neg_a"], 1)
                    stt(out=a_t[:, :, :], in0=dt_t[:, :, :], scalar=-1.0,
                        in1=a_exp.unsqueeze(1).to_broadcast([P, TT, SSD_HEADS]), op0=ALU.mult, op1=ALU.mult) \
                        .then_inc(S["a_ready"], 1)
                split("kv", 0, x)
            attn0 = chain.n
            ATTN_STEPS = 5

            def attention(i, x):
                known = isinstance(i, int)
                if not (known and not 2 <= i < N_KV + 2):
                    j = i - 2
                    chain.at(attn0 + j * ATTN_STEPS)
                    if x == 1:
                        dve.wait_ge(S["exp_done"], j + 1)
                        chain.n = 3
                        chain.link(tt(den, rsum, es, ALU.add))
                        chain.link(v.reciprocal(rden, den))
                        tt(p0[:, :, :], p0[:, :, :], rden[:, 0:4].unsqueeze(2).to_broadcast([P, GQ, P]), ALU.mult)
                        tt(p1[:, :, :], p1[:, :, :], rden[:, 4:8].unsqueeze(2).to_broadcast([P, GQ, T]), ALU.mult) \
                            .then_inc(S["probs_ready"], 1)
                    if x == 2:
                        dve.wait_ge(S["pt_done"], j + 1)
                        v.tensor_copy(pt[:, 1, :], ps[5][:, :]).then_inc(S["pt_dve"], 1)
                    if x == 3:
                        dve.wait_ge(S["attn_hi"], j + 1)
                        tt(act32[:, bass.ds(2 * j, 2), T:2 * T], f2(ps[7][:, :]),
                           act32[:, bass.ds(2 * j, 2), 0:T].bitcast(F32), ALU.subtract).then_inc(S["attn_lo"], 1)
                if x == 3 and not (known and not 1 <= i < N_KV + 1):
                    j = i - 1
                    chain.at(attn0 + j * ATTN_STEPS)
                    dve.wait_ge(S["scores_done"], j + 1)
                    for g in range(GQ):
                        slope = const[:, bass.ds(4 * j + (C_SLOPE + g), 1)]
                        stt(out=p0[:, g, :], in0=negd[0], scalar=slope, in1=ps[4][:, g * P:(g + 1) * P],
                            op0=ALU.mult, op1=ALU.add)
                        last = stt(out=p1[:, g, :], in0=negd[1], scalar=slope,
                                   in1=ps[5 + g % 2][:, (g // 2) * T:(g // 2 + 1) * T], op0=ALU.mult, op1=ALU.add)
                    chain.link(last)
                    v.tensor_reduce(mx[:, 0:4], p0[:, :, :], AX, ALU.max)
                    chain.link(v.tensor_reduce(mx[:, 4:8], p1[:, :, :], AX, ALU.max))
                    sink = sink_b[:, bass.ds(4 * j, 4)].unsqueeze(1).to_broadcast([P, 2, 4])
                    two = lambda ap: ap.rearrange("p (t g) -> p t g", t=2)
                    chain.link(stt(out=two(mm_), in0=two(mx), scalar=0.125, in1=sink, op0=ALU.mult, op1=ALU.max))
                    tt(two(es), sink, two(mm_), ALU.subtract)
                    v.tensor_scalar(negm, mm_, -1.0, None, ALU.mult).then_inc(S["shift_ready"], 1)
                    chain.n = 0

            def q_body(i):
                for x in range(4):
                    attention(i, x)
                    if isinstance(i, int) and i == 1 and x == 0:
                        dve.wait_ge(S["cums_done"], 1)
                        v.tensor_copy(acs_t[:, :, :], ps[7][:, 0:128].rearrange("p (t h) -> p t h", t=TT)) \
                            .then_inc(S["acs_ready"], 1)
                        dve.wait_ge(S["acs_ready"], 1)
                        tt(dec_t[:, :, :], ps[7][:, 128:256].rearrange("p (t h) -> p t h", t=TT), acs_t[:, :, :],
                           ALU.subtract).then_inc(S["dec_in"], 1)
                    if x == 3:
                        dve.wait_ge(S["q_kept"], i + 1)
                        v.memset(small[:, 31:32], 0.0).then_inc(bank_free[2], 1)
                    split("q", i, x)
            loop(dve, "q", q_body, peel=2)

            def gate_a_body(i):
                for x in range(8):
                    if isinstance(i, int) and i == 0:
                        attention(N_KV + x // 4, x % 4)
                    split("gate_a", i, x)
            loop(dve, "gate_a", gate_a_body, peel=1)

            def attn_out_body(i):
                for k in range(2):
                    for x in range(4 * k, 4 * k + 4):
                        if x == 4 * k + 3:
                            bank = PLAN["attn_out"]["jobs"][k][1][0]
                            dve.wait_ge(S["slab_used"], slab_no("attn_out", i, x) + 1)
                            dst = ga_f[:, bass.ds(4 * i + 2 * k, 2), :]
                            stt(out=dst, in0=dst, scalar=1.0, in1=f2(ps[bank][:, :]), op0=ALU.add, op1=ALU.mult) \
                                .then_inc(bank_free[bank], 1)
                        split("attn_out", i, x)
            dve.wait_ge(bank_free[2], bank_use("attn_out", 0, 1, 2))
            dve.wait_ge(bank_free[3], bank_use("attn_out", 0, 0, 3))
            loop(dve, "attn_out", attn_out_body)

            v.memset(upad[:, :, 0:4], 0.0).then_inc(S["pad_zero"], 1)

            def conv(fts, cols, done, base, bank):
                step = 0
                for tap in range(CONV_K):
                    for n, f in enumerate(fts):
                        src = upad[:, f, 1 + tap:1 + tap + T]
                        w = chan[:, bass.ds(cols[n] * CONV_K + (V_CW + tap), 1)]
                        if tap == 0:
                            ins = v.tensor_scalar(cv[:, f, :], src, w, chan[:, bass.ds(cols[n] + V_CB, 1)], ALU.mult, ALU.add)
                        else:
                            dve.wait_ge(S[done], base + step - len(fts) + 1)
                            ins = stt(out=cv[:, f, :], in0=src, scalar=w, in1=cv[:, f, :], op0=ALU.mult, op1=ALU.add)
                        ins.then_inc(S[done], 1)
                        step += 1

            def conv_bc(g, n):
                dve.wait_ge(S["bc_in"], n + 1)
                v.memset(small[:, 30:31], 0.0).then_inc(bank_free[0], 1)
                conv([4, 5], [g + 32, g + 40], "conv_bc", n * 8, 0)

            def silu_bc(n):
                dve.wait_ge(S["th_bc"], n + 1)
                stt(out=cv[:, 4:6, :], in0=th[:, 4:6, :], scalar=1.0, in1=cv[:, 4:6, :], op0=ALU.add, op1=ALU.mult) \
                    .then_inc(S["silu_bc"], 1)

            def conv_x(g, which, n):
                name = "xa_in" if which == 0 else "xb_in"
                dve.wait_ge(S[name], n + 1)
                v.memset(small[:, 29:30], 0.0).then_inc(bank_free[1 if which == 0 else 0], 1)
                f = 2 * which
                conv([f, f + 1], [4 * g + f, 4 * g + (f + 1)], "conv_xa" if which == 0 else "conv_xb", n * 8, 0)

            for x in range(8):
                if x == 3:
                    conv_bc(0, 0)
                if x == 5:
                    silu_bc(0)
                if x == 7:
                    conv_x(0, 0, 0)
                split("first_group", 0, x)

            heads = lambda ap: ap.rearrange("p (h n) -> p h n", h=HPG)

            def per_head(table, t, g, rows=slice(0, P)):
                n = rows.stop - rows.start
                return table[rows, t, bass.ds(g * HPG, HPG)].unsqueeze(2).to_broadcast([n, HPG, 64])

            def ssd(g, x, phase, i, last=False):
                if x == 1 or x == 2:
                    t = x - 1
                    dve.wait_ge(S["cb_done"], g + 1)
                    tt(heads(mt[:, t, :]), heads(ps[4 + t][:, :]), per_head(acs_t, t, g), ALU.subtract) \
                        .then_inc(S["seg_out"], 1)
                if x == 2:
                    dve.wait_ge(S["btok_ready"], g + 1)
                    tt(cbm[:, :, :], ps[6][:, 0:P].rearrange("p (t l) -> p t l", t=TT),
                       tri.unsqueeze(1).to_broadcast([P, TT, 64]), ALU.mult).then_inc(S["cbm_ready"], 1)
                if x == 3:
                    conv_x(g, 1, g)
                if x == 5:
                    dve.wait_ge(S["cbm_ready"], g + 1)
                    dve.wait_ge(S["seg_exp"], g + 1)
                    for t in range(TT):
                        tt(heads(mt[:, t, :]), heads(mt[:, t, :]),
                           cbm[:, t, :].unsqueeze(1).to_broadcast([P, HPG, 64]), ALU.mult).then_inc(S["mt_ready"], 1)
                if x == 6:
                    dve.wait_ge(S["th_x"], g + 1)
                    stt(out=cv[:, 0:4, :], in0=th[:, 0:4, :], scalar=1.0, in1=cv[:, 0:4, :], op0=ALU.add, op1=ALU.mult) \
                        .then_inc(S["silu_x"], 1)
                if x == 7:
                    dve.wait_ge(S["xt_tr"], g + 1)
                    for t in range(TT):
                        src = heads(ps[7 - t][:, :])
                        tt(heads(xdt[:, t, :]), src, per_head(dt_t, t, g), ALU.mult).then_inc(S["xs_used"], 1)
                        d = dskip_b[:, bass.ds(g * HPG, HPG)].unsqueeze(2).to_broadcast([P, HPG, 64])
                        tt(heads(xd[:, t, :]), src, d, ALU.mult).then_inc(S["xs_used"], 1)
                if x == 9 or x == 10:
                    c = x - 8
                    dve.wait_ge(S["prev1"], g + 1)
                    if c == 2:
                        dve.wait_ge(S["prev2"], g + 1)
                    d = cdec[:, c, bass.ds(g * HPG, HPG)].unsqueeze(2).to_broadcast([P, HPG, 64])
                    tt(heads(prev[:, c, :]), heads(prev[:, c - 1, :]), d, ALU.mult).then_inc(S["prev_tmp"], 1)
                    dve.wait_ge(S["prev_tmp"], 2 * g + c)
                    tt(prev[:, c, :], prev[:, c, :], ps[4 + c][:, :], ALU.add).then_inc(S["prev2" if c == 1 else "prev3"], 1)
                    if c == 2:
                        dve.wait_ge(S["yd0_done"], g + 1)
                        tt(yb[:, 0, :], ps[7][:, :], xd[:, 0, :], ALU.add).then_inc(S["y_part"], 1)
                if x == 11:
                    for t in range(TT):
                        dve.wait_ge(S["tz_ready"], 2 * g + t + 1)
                        stt(out=sz[:, t, :], in0=sz[:, t, :], scalar=1.0, in1=ps[2 + t][:, :], op0=ALU.add, op1=ALU.mult) \
                            .then_inc(bank_free[2 + t], 1)
                if x == 13:
                    dve.wait_ge(S["yd1_done"], g + 1)
                    tt(yb[:, 1, :], ps[4][:, :], xd[:, 1, :], ALU.add).then_inc(S["y_part"], 1)
                    for t in range(TT):
                        rows = slice(64, P) if t == 0 else slice(0, P)
                        tt(heads(mt[rows, t, :]), heads(ps[5 + t][rows, :]), per_head(ea_t, t, g, rows), ALU.mult) \
                            .then_inc(S["y_part"], 1)
                if x == 14:
                    dve.wait_ge(S["y_part"], 4 * g + 4)
                    for t in range(TT):
                        rows = slice(64, P) if t == 0 else slice(0, P)
                        tt(yb[rows, t, :], yb[rows, t, :], mt[rows, t, :], ALU.add).then_inc(S["y_tmp"], 1)
                    for t in range(TT):
                        dve.wait_ge(S["y_tmp"], 2 * g + t + 1)
                        if t == 0:
                            dve.wait_ge(bank_free[3], sz_uses(g))
                        tt(yb[:, t, :], yb[:, t, :], sz[:, t, :], ALU.mult).then_inc(S["y_ready"], 1)
                if x == 15 and not last:
                    conv_bc(g + 1, g + 1)
                if x == 17:
                    dve.wait_ge(S["std_g"], g + 1)
                    v.reciprocal(small[:, 8:10], small[:, 6:8]).then_inc(S["rstd_g"], 1)
                    if not last:
                        silu_bc(g + 1)
                if x == 19:
                    if not last:
                        conv_x(g + 1, 0, g + 1)
                    for f in range(4):
                        dve.wait_ge(S["y_hi"], 4 * g + (2 * (f // 2) + 2))
                        ft = bass.ds(4 * g + f, 1)
                        stt(out=act32[:, ft, T:2 * T], in0=ps[6 + f // 2][:, (f % 2) * T:(f % 2 + 1) * T].unsqueeze(1),
                            scalar=chan[:, bass.ds(4 * g + (V_SN + f), 1)], in1=act32[:, ft, 0:T].bitcast(F32),
                            op0=ALU.mult, op1=ALU.subtract).then_inc(S["y_lo"], 1)

            def sz_uses(g):
                return PLAN["group"]["use0"][3] + 1 + g * PLAN["group"]["uses"][3]

            def group_body(i):
                for x in range(20):
                    ssd(i, x, "group", i)
                    split("group", i, x)
            loop(dve, "group", group_body)
            for x in range(12):
                ssd(GROUPS - 1, x, "last_group", 0, last=True)
                split("last_group", 0, x)

            def gate_s_body(i):
                for x in range(8):
                    if isinstance(i, int) and i == 0:
                        ssd(GROUPS - 1, x + 12, None, None, last=True)
                    split("gate_s", i, x)
            loop(dve, "gate_s", gate_s_body, peel=1)

            dve.wait_ge(bank_free[0], bank_use("out", 0, 0, 0))
            dve.wait_ge(bank_free[1], bank_use("out", 0, 0, 1))

            def ssd_out_body(i):
                for k in range(2):
                    for x in range(8 * k, 8 * k + 8):
                        if x == 8 * k + 7:
                            bank = 2 + k
                            n = 2 * i + k
                            ft = bass.ds(4 * i + 2 * k, 2)
                            dve.wait_ge(S["slab_used"], slab_no("ssd_out", i, x) + 1)
                            stt(out=gs[:, ft, :], in0=gs[:, ft, :], scalar=1.0, in1=f2(ps[bank][:, :]), op0=ALU.add,
                                op1=ALU.mult).then_inc(bank_free[bank], 1)
                            dve.wait_ge(bank_free[bank], bank_use("ssd_out", i, k, bank) + 1)
                            tt(ga_f[:, ft, :], ga_f[:, ft, :], gs[:, ft, :], ALU.add).then_inc(S["m_sum2"], 1)
                            dve.wait_ge(S["m_hi"], n + 1)
                            stt(out=act16[:, ft, T:2 * T], in0=ga_f[:, ft, :], scalar=0.5,
                                in1=act16[:, ft, 0:T].bitcast(F32), op0=ALU.mult, op1=ALU.subtract).then_inc(S["m_lo"], 1)
                        split("ssd_out", i, x)
            loop(dve, "ssd_out", ssd_out_body)

            def add_residual(phase, i, k, x, nb, done, n):
                dve.wait_ge(S["slab_used"], slab_no(phase, i, x) + 1)
                banks = PLAN[phase]["jobs"][k][1]
                for t in range(TT):
                    dst = x_sb[:, t, bass.ds(nb * 512, 512)]
                    tt(dst, dst, ps[banks[t]][:, :], ALU.add).then_inc(bank_free[banks[t]], 1)
                if done:
                    for t in range(TT):
                        dve.wait_ge(bank_free[banks[t]], bank_use(phase, i, k, banks[t]) + 1)
                    v.memset(small[:, 28:29], 0.0).then_inc(S[done], 1)

            def x2_side(nb):
                for k in range(4 * nb, 4 * nb + 4):
                    dve.wait_ge(S["h2_hi"], 2 * (k // 2) + 2)
                    stt(out=act32[:, k, T:2 * T], in0=ps[4 + (k // 2) % 4][:, (k % 2) * T:(k % 2 + 1) * T],
                        scalar=chan[:, V_N2 + k:V_N2 + k + 1], in1=act32[:, k, 0:T].bitcast(F32), op0=ALU.mult,
                        op1=ALU.subtract).then_inc(S["h2_lo"], 1)
            dve.wait_ge(S["x_loaded"], 32)
            dve.wait_ge(S["x_again"], 32)
            for n in range(4):
                for x in range(8 * n, 8 * n + 8):
                    if n and x == 8 * n + 1:
                        x2_side(n - 1)
                    if x == 8 * n + 7:
                        add_residual("out", 0, n, x, n, "x2_ready", n)
                    split("out", 0, x)
            x2_side(3)
            dve.wait_ge(S["sq2_ready"], 8)
            v.tensor_reduce(small[:, 10:12], ssq[:, :, :], AX, ALU.add).then_inc(S["ssq2_sum"], 1)
            dve.wait_ge(S["std2"], 1)
            v.reciprocal(small[:, 14:16], small[:, 12:14]).then_inc(S["rstd2"], 1)
            dve.wait_ge(S["rstd2"], 1)
            for t in range(TT):
                last = v.tensor_scalar(diag[:, t, :], ident, small[:, 14 + t:15 + t], None, ALU.mult)
            last.then_inc(S["diag_ready"], 1)

            def up(phase, n0, dst, ft0):
                def body(i):
                    for k in range(2):
                        for x in range(4 * k, 4 * k + 4):
                            if phase == "up_a0" and isinstance(i, int) and i == 0 and x == 1:
                                dve.wait_ge(S["rr_done"], 1)
                                v.tensor_copy(rrow, ps[4][:, 0:T]).then_inc(S["rr_ready"], 1)
                            if x == 4 * k + 3:
                                bank = PLAN[phase]["jobs"][k][1][0]
                                n = 2 * i + (n0 + k)
                                t = f2(tu[:, k, :])
                                if phase == "up_a0":
                                    dve.wait_ge(S["rr_ready"], 1)
                                dve.wait_ge(S["slab_used"], slab_no(phase, i, x) + 1)
                                stt(out=t, in0=f2(ps[bank][:, :]), scalar=0.0,
                                    in1=rrow.unsqueeze(1).to_broadcast([P, 2, T]), op0=ALU.max, op1=ALU.mult) \
                                    .then_inc(bank_free[bank], 1)
                                dve.wait_ge(bank_free[bank], bank_use(phase, i, k, bank) + 1)
                                v.memset(small[:, 27:28], 0.0).then_inc(S["u_relu"], 1)
                                dve.wait_ge(S["u_hi"], n + 1)
                                tt(t, t, t, ALU.mult).then_inc(S["u_sq"], 1)
                                dve.wait_ge(S["u_sq"], n + 1)
                                ft = bass.ds(4 * i + (ft0 + 2 * k), 2)
                                tt(dst[:, ft, T:2 * T], t, dst[:, ft, 0:T].bitcast(F32), ALU.subtract) \
                                    .then_inc(S["u_lo"], 1)
                            split(phase, i, x)
                loop(dve, phase, body, peel=1 if phase == "up_a0" else 0)

            def down_a_body(i):
                for k in range(2):
                    for x in range(16 * k, 16 * k + 16):
                        if x == 16 * k + 15:
                            add_residual("down_a", i, k, x, 2 * i + k, None, 0)
                        split("down_a", i, x)
            up("up_a0", 0, act32, 16)
            up("up_a1", 8, act16, 0)
            loop(dve, "down_a", down_a_body)
            up("up_b0", 16, act32, 16)
            up("up_b1", 24, act16, 0)
            dve.wait_ge(S["wf_loaded"], 16)
            for phase, nb0 in (("down_b", 0), ("down_end", 2)):
                for k in range(2):
                    nb = nb0 + k
                    for x in range(16 * k, 16 * k + 16):
                        if x == 16 * k + 15:
                            add_residual(phase, 0, k, x, nb, "x3_ready", nb)
                        split(phase, 0, x)
                    for t in range(TT):
                        dve.wait_ge(S["sq3_ready"], 2 * nb + t + 1)
                        blk_x = x_sb[:, t, nb * 512:(nb + 1) * 512]
                        tt(blk_x, blk_x, wf[:, nb * 512:(nb + 1) * 512], ALU.mult).then_inc(S["x3_w"], 1)
            v.tensor_reduce(small[:, 18:20], ssq[:, :, :], AX, ALU.add).then_inc(S["ssq3_sum"], 1)
            dve.wait_ge(S["std3"], 1)
            dve.wait_ge(S["x3_w"], 8)
            v.reciprocal(small[:, 22:24], small[:, 20:22]).then_inc(S["rstd3"], 1)
            dve.wait_ge(S["rstd3"], 1)
            v.tensor_scalar(x_sb[:, 1, :], x_sb[:, 1, :], small[:, 23:24], None, ALU.mult).then_inc(S["out_dve"], 1)

        @block.gpsimd
        def _(pool):
            g_ = nc.gpsimd
            ks_flat = scr[:, 0:2048].rearrange("p (j t) -> p j t", j=N_KV)
            pool.wait_ge(bank_free[0], 1)
            pool.wait_ge(bank_free[1], 1)
            pool.wait_ge(bank_free[2], 1)
            pool.wait_ge(bank_free[3], 1)

            def kv(j):
                first = isinstance(j, int) and j == 0
                if not first:
                    pool.wait_ge(S["scores_done"], j)
                g_.tensor_copy(kc.unsqueeze(1), ks_flat[:, bass.ds(j, 1), :]).then_inc(S["kc_ready"], 1)
                if not first:
                    pool.wait_ge(S["pv_done"], j)
                g_.tensor_copy(vc[:, :, :], vs[:, :, bass.ds(j * HD, HD)]).then_inc(S["vc_ready"], 1)
            kv(0)
            with pool.Fori(1, N_KV) as j:
                kv(j)

            def ssd(g):
                first = isinstance(g, int) and g == 0
                if first:
                    pool.wait_ge(S["pad_zero"], 1)
                    pool.wait_ge(S["attn_lo"], N_KV)
                else:
                    pool.wait_ge(S["y_ready"], 2 * g)
                for t in range(TT):
                    last = g_.tensor_tensor(rs[:, t, :].rearrange("p (h l) -> p h l", h=HPG),
                                            a_t[:, t, bass.ds(g * HPG, HPG)].unsqueeze(2).to_broadcast([P, HPG, 64]),
                                            tri.unsqueeze(1).to_broadcast([P, HPG, 64]), ALU.mult)
                last.then_inc(S["rs_ready"], 1)
                pool.wait_ge(S["xs_used"], 4 * g + 4)
                for t in range(TT):
                    last = g_.tensor_tensor(xdec[:, t, :].rearrange("p (h l) -> p h l", h=HPG),
                                            xdt[:, t, :].rearrange("p (h l) -> p h l", h=HPG),
                                            dec_t[:, t, bass.ds(g * HPG, HPG)].unsqueeze(2).to_broadcast([P, HPG, 64]),
                                            ALU.mult)
                last.then_inc(S["xdec_ready"], 1)
            ssd(0)
            with pool.Fori(1, GROUPS) as g:
                ssd(g)


def kernel(**inputs):
    import numpy as _np
    import concourse.bacc as _bacc
    from concourse.bass_utils import run_bass_kernel_spmd as _run

    def columns(v):
        return _np.asarray(v).reshape(-1, P).T

    taps = _np.asarray(inputs["conv_w"]).reshape(CONV_K, -1, P).transpose(2, 1, 0).reshape(P, -1)
    channel_table = _np.ascontiguousarray(_np.concatenate(
        [columns(inputs["norm1_w"]), columns(inputs["gate_bias"]), taps, columns(inputs["conv_b"]),
         columns(inputs["ssd_norm_w"]), columns(inputs["norm2_w"])], axis=1))
    k, m = _np.arange(P)[:, None], _np.arange(P)[None, :]
    same = (k // CHUNK == m // CHUNK)
    table = _np.zeros((P, C_COLS + NEG_COLS), _np.float32)
    table[:, C_ID:C_ID + P] = (k == m)
    table[:, C_TRI:C_TRI + CHUNK] = (k % CHUNK <= m[:, :CHUNK])
    table[:, C_CUM:C_CUM + P] = same & (k <= m)
    table[:, C_BLK:C_BLK + P] = same
    for t, c in ((0, C_NEG), (1, C_NEG + P)):
        q, s = _np.arange(P)[:, None] + t * P, _np.arange((t + 1) * P)[None, :]
        ahead = q // CHUNK - s // CHUNK
        table[:, c:c + (t + 1) * P] = _np.where((ahead == 0) | (ahead == 1), -_np.abs(q - s), -1e30)
    table[:, C_SLOPE:C_SLOPE + N_HEADS] = 8.0 * 2.0 ** (-8.0 * _np.arange(1, N_HEADS + 1) / N_HEADS)
    table[:, C_EPS], table[:, C_EPS4] = EPS, 4 * EPS
    table[:, C_ONE:C_ONE + P] = 1.0

    nc = _bacc.Bacc("TRN2", target_bir_lowering=False, num_devices=1)
    arrays, args = {}, []
    for name in ["x", "w_in", "w_o_attn", "w_o_ssd", "w_out", "w_up", "w_down", "attn_sinks", "dt_bias", "a_log",
                 "d_skip", "norm_final_w"]:
        arrays[f"in_{name}"] = _np.ascontiguousarray(inputs[name])
    arrays["channel_table"], arrays["shape_table"] = channel_table, table
    for name, a in arrays.items():
        args.append(nc.dram_tensor(name, a.shape, mybir.dt.from_np(a.dtype), kind="ExternalInput").ap())
    args.append(nc.dram_tensor("out", (1, T, D), F32, kind="ExternalOutput").ap())
    hybrid_block(nc, *args)
    r = _run(nc, [arrays], core_ids=[0])
    return r.results[0]["out"]
```

```python
from contextlib import ExitStack

import concourse.bass as bass
from concourse import mybir

F32 = mybir.dt.float32
F32R = mybir.dt.float32r
ALU = mybir.AluOpType
ACT = mybir.ActivationFunctionType
AX = mybir.AxisListType.X

P = 128
T = 256
TT = T // P
D = 2048
KD = D // P
CHUNK = 64
N_CHUNKS = T // CHUNK
HD = 64
N_HEADS, N_KV = 32, 8
GQ = N_HEADS // N_KV
D_INNER = 2 * D
GROUPS = 8
HPG = D_INNER // HD // GROUPS
GW = D_INNER // GROUPS
SSD_HEADS = GROUPS * HPG
STATE = 128
CONV_K = 4
D_FF = 4 * D
EPS = 1e-5

Q0 = 0
K0 = Q0 + N_HEADS * HD
V0 = K0 + N_KV * HD
Z0 = V0 + N_KV * HD
X0 = Z0 + D_INNER
B0 = X0 + D_INNER
C0 = B0 + GROUPS * STATE
DT0 = C0 + GROUPS * STATE
G0 = DT0 + SSD_HEADS
D_IN = G0 + 2 * D

PT_BANKS = (0, 1, 3)
RING = 4
SLAB = 1024

V_N1, V_GB, V_CW, V_CB, V_SN, V_N2 = 0, 16, 48, 240, 288, 320
V_COLS = 336
C_ID, C_TRI, C_CUM, C_BLK, C_SLOPE, C_EPS, C_EPS4, C_ONE = 0, 128, 192, 320, 448, 480, 481, 482
C_COLS = 610
C_NEG, NEG_COLS = C_COLS, 3 * P

PHASES = [
    ("kv", 1, [(4, [0]), (4, [1]), (8, [2, 3]), (4, [0, 1])]),
    ("q", N_KV, [(4, [2])]),
    ("gate_a", 4, [(4, [2]), (4, [3])]),
    ("attn_out", 4, [(4, [2]), (4, [3])]),
    ("first_group", 1, [(4, [0]), (4, [1])]),
    ("group", GROUPS - 1, [(4, [0]), (8, [2, 3]), (4, [0]), (4, [1])]),
    ("last_group", 1, [(4, [0]), (8, [2, 3])]),
    ("gate_s", 4, [(4, [0]), (4, [1])]),
    ("ssd_out", 4, [(8, [2]), (8, [3])]),
    ("out", 1, [(8, [0, 1]), (8, [2, 3]), (8, [0, 1]), (8, [2, 3])]),
    ("up_a0", 4, [(4, [0]), (4, [1])]),
    ("up_a1", 4, [(4, [0]), (4, [1])]),
    ("down_a", 2, [(16, [2, 3]), (16, [0, 1])]),
    ("up_b0", 4, [(4, [2]), (4, [3])]),
    ("up_b1", 4, [(4, [2]), (4, [3])]),
    ("down_b", 1, [(16, [0, 1]), (16, [2, 3])]),
    ("down_end", 1, [(16, [0, 1]), (16, [2, 3])]),
]


def make_plan():
    plan, slab, uses = {}, 0, [0] * 4
    for name, iters, jobs in PHASES:
        per = [sum(b in banks for _, banks in jobs) for b in range(4)]
        plan[name] = dict(iters=iters, jobs=jobs, slab0=slab, slabs=sum(n for n, _ in jobs), use0=list(uses), uses=per)
        slab += iters * plan[name]["slabs"]
        uses = [u + iters * p for u, p in zip(uses, per)]
    return plan, slab


PLAN, N_SLABS = make_plan()
DT_SLAB = PLAN["kv"]["slab0"] + 16


def slab_no(phase, i, x):
    return PLAN[phase]["slab0"] + i * PLAN[phase]["slabs"] + x


def slot_round(phase, i, x):
    return PLAN[phase]["slab0"] // RING + i * (PLAN[phase]["slabs"] // RING) + x // RING


def bank_use(phase, i, job, bank):
    p = PLAN[phase]
    return p["use0"][bank] + i * p["uses"][bank] + sum(bank in banks for _, banks in p["jobs"][:job])


def job_end(phase, job):
    return sum(n for n, _ in PLAN[phase]["jobs"][: job + 1]) - 1


def loop(eng, phase, body, peel=0):
    n = PLAN[phase]["iters"]
    for i in range(peel):
        body(i)
    if n - peel == 1:
        body(peel)
    elif n > peel:
        with eng.Fori(peel, n) as i:
            body(i)


def hybrid_block(nc, x, w_in, w_o_attn, w_o_ssd, w_out, w_up, w_down, sinks, dt_bias, a_log, d_skip, norm_final_w,
                 channel_table, shape_table, out):
    with ExitStack() as ctx:
        def sb(name, shape, dt=F32):
            return ctx.enter_context(nc.sbuf_tensor(name, shape, dt))

        def sem(name):
            return ctx.enter_context(nc.semaphore(name))

        ps = [ctx.enter_context(nc.psum_tensor(f"bank{b}", [P, 512], F32)) for b in range(8)]

        raw = sb("raw", [P, RING, SLAB])
        w_hi = sb("w_hi", [P, RING, SLAB], F32R)
        w_lo = sb("w_lo", [P, RING, SLAB], F32R)
        act16 = sb("act16", [P, 16, 2 * T], F32R)
        act32 = sb("act32", [P, 32, 2 * T], F32R)
        xg = sb("xg", [P, 4096])
        ga = sb("ga", [P, 4096])
        scr = sb("scr", [P, 6040])
        chan = sb("chan", [P, V_COLS])
        const = sb("const", [P, C_COLS])
        sink_b = sb("sink_b", [P, N_HEADS])
        dskip_b = sb("dskip_b", [P, SSD_HEADS])
        dt_t = sb("dt_t", [P, TT, SSD_HEADS])
        a_t = sb("a_t", [P, TT, SSD_HEADS])
        acs_t = sb("acs_t", [P, TT, SSD_HEADS])
        ea_t = sb("ea_t", [P, TT, SSD_HEADS])
        dec_t = sb("dec_t", [P, TT, SSD_HEADS])
        cdec = sb("cdec", [P, N_CHUNKS, SSD_HEADS])
        ssq = sb("ssq", [P, TT, 4])
        small = sb("small", [P, 32])

        ident = const[:, C_ID:C_ID + P]
        tri = const[:, C_TRI:C_TRI + CHUNK]
        cum = const[:, C_CUM:C_CUM + P]
        blk = const[:, C_BLK:C_BLK + P]
        ones = const[:, C_ONE:C_ONE + P]
        neg_all = scr[:, 5184:5184 + NEG_COLS]
        negd = [neg_all[:, 0:P], neg_all[:, P:NEG_COLS]]
        x_sb = xg[:, :].rearrange("p (t n) -> p t n", t=TT)
        gs = xg[:, :].rearrange("p (f n) -> p f n", f=KD)
        ga_f = ga[:, :].rearrange("p (f n) -> p f n", f=KD)

        ks = scr[:, 0:2048].rearrange("p (j c t) -> p j c t", j=4, c=2)
        vs = scr[:, 2048:3072].rearrange("p (t n) -> p t n", t=TT)
        qt = scr[:, 3072:3584].rearrange("p (f t) -> p f t", f=2)
        kc = scr[:, 3584:3840]
        vc = scr[:, 3840:3968].rearrange("p (t n) -> p t n", t=TT)
        p0 = scr[:, 3968:4480].rearrange("p (g k) -> p g k", g=GQ)
        sm = scr[:, 4480:4544]
        mx, mm_, negm, es, rsum, den, rden = [sm[:, 8 * n:8 * n + 8] for n in range(7)]
        dt_tmp = scr[:, 4544:4544 + 5 * 128]
        p1 = xg[:, 0:1024].rearrange("p (g k) -> p g k", g=GQ)
        pt = xg[:, 1024:2560].rearrange("p (b n) -> p b n", b=3)
        upad = scr[:, 0:1560].rearrange("p (f n) -> p f n", f=6)
        cv = scr[:, 1560:3096].rearrange("p (f n) -> p f n", f=6)
        th = scr[:, 3096:4632].rearrange("p (f n) -> p f n", f=6)
        prev = scr[:, 3096:4632].rearrange("p (c n) -> p c n", c=3)
        btok = scr[:, 4632:4888].rearrange("p (t n) -> p t n", t=TT)
        mt = scr[:, 4888:5912].rearrange("p (t n) -> p t n", t=TT)
        cbm = scr[:, 5912:6040].rearrange("p (t l) -> p t l", t=TT)
        rs = xg[:, 0:1024].rearrange("p (t n) -> p t n", t=TT)
        sz = rs
        yb = xg[:, 1024:2048].rearrange("p (t n) -> p t n", t=TT)
        xdt = xg[:, 2048:3072].rearrange("p (t n) -> p t n", t=TT)
        xd = xg[:, 3072:4096].rearrange("p (t n) -> p t n", t=TT)
        xdec = scr[:, 1560:2584].rearrange("p (t n) -> p t n", t=TT)
        tu = scr[:, 0:1024].rearrange("p (b n) -> p b n", b=2)
        rrow = scr[:, 1024:1280]
        diag = scr[:, 1280:1536].rearrange("p (t n) -> p t n", t=TT)
        junk = scr[:, 2048:4096]
        wf = ga[:, 0:D]

        names = """x_loaded tables_loaded rows_loaded x_again wf_loaded stored
            hi_ready lo_ready slab_used
            ssq1_act ssq1_dve std1_ready rstd1_ready xn_act xn_dve xt_done h_hi h_lo half_ready
            k_kept v_kept dt_v dt_e dt_ready a_ready neg_a cums_done acs_ready tot_copied ea_ready dec_in dec_ready tail_b
            even_scores kc_ready vc_ready scores_done biased max_done shift_ready es_ready exp_done den_ready rden_ready
            probs_ready pt_done pt_act pt_dve pv_done attn_hi attn_lo
            gate_ready ya_ready
            pad_zero conv_bc conv_xa conv_xb th_bc th_x silu_bc silu_x rs_ready cb_done bt_done seg_out seg_min
            seg_exp btok_ready cbm_ready mt_ready xt_tr xs_used xdec_ready st_done prev1 prev2 prev3 prev_tmp yd0_done yd1_done
            y_part tz_ready sz_ready yo_done y_ready ssq_g std_g rstd_g yn_ready yt_done y_hi y_lo y_tmp
            m_sum2 m_hi m_lo
            sq2_ready x2t_done h2_hi h2_lo ssq2_sum std2 rstd2 diag_ready rr_done rr_ready
            u_hi u_sq u_lo sq3_ready sq3_dve x3_w ssq3_sum std3 rstd3 out_act out_dve""".split()
        S = {n: sem(n) for n in names}
        raw_landed = [sem(f"raw_landed{s}") for s in range(RING)]
        bank_free = [sem(f"bank_free{b}") for b in range(4)]

        class Chain:
            def __init__(self, eng, s):
                self.eng, self.s, self.base, self.n = eng, s, 0, 0

            def at(self, start):
                self.base, self.n = start, 0

            def link(self, ins):
                self.n += 1
                ins.then_inc(self.s, 1)
                self.eng.wait_ge(self.s, self.base + self.n)

        def width_of(n):
            narrow = isinstance(n, int) and DT_SLAB <= n + RING < DT_SLAB + 4
            return 4 * SSD_HEADS if narrow else SLAB

        def raw_count(slot, phase, i, x):
            return (slot_round(phase, i, x) + 2) * 16

        block = ctx.enter_context(nc.Block())

        def feature_src(w, row_tile, col, width=256, kt=4):
            v = w.rearrange("(k p) n -> p k n", p=P)
            return v[:, row_tile:row_tile + kt, bass.ds(col, width)]

        @block.sync
        def _(sp):
            sp.dma_start(x_sb[:, 0, :], x[0, 0:P, :]).then_inc(S["x_loaded"], 16)
            sp.dma_start(x_sb[:, 1, :], x[0, P:T, :]).then_inc(S["x_again"], 16)

            def load(phase, i, xs, src, dst=None):
                n = slab_no(phase, i, xs)
                slot = xs % RING
                if not (isinstance(n, int) and n < RING):
                    sp.wait_ge(S["lo_ready"], n - RING + 1)
                dst = raw[:, slot, :] if dst is None else dst
                sp.dma_start(dst, src).then_inc(raw_landed[slot], 16)

            def feature_job(phase, i, x0, w, col, rows=KD):
                for s in range(rows // 4):
                    load(phase, i, x0 + s, feature_src(w, 4 * s, col),
                         raw[:, (x0 + s) % RING, :].rearrange("p (k n) -> p k n", k=4))

            def token_job(phase, i, x0, w, col, rows=KD, row0=0):
                for s in range(rows // 2):
                    load(phase, i, x0 + s, feature_src(w, row0 + 2 * s, col, 512, 2),
                         raw[:, (x0 + s) % RING, :].rearrange("p (k n) -> p k n", k=2))

            def bc_job(phase, i, x0, g):
                for s in range(4):
                    load(phase, i, x0 + s, feature_src(w_in, 8 * (s % 2), g * STATE + (B0 if s < 2 else C0), STATE, 8),
                         raw[:, (x0 + s) % RING, :].rearrange("p (k n) -> p k n", k=8))

            feature_job("kv", 0, 0, w_in, K0)
            feature_job("kv", 0, 4, w_in, K0 + 256)
            token_job("kv", 0, 8, w_in, V0)
            for s in range(4):
                load("kv", 0, 16 + s, feature_src(w_in, 4 * s, DT0, SSD_HEADS),
                     raw[:, s, 0:4 * SSD_HEADS].rearrange("p (k n) -> p k n", k=4))
            loop(sp, "q", lambda i: feature_job("q", i, 0, w_in, i * 256 + Q0))

            def gate(phase, col):
                def body(i):
                    for k in range(2):
                        feature_job(phase, i, 4 * k, w_in, i * 512 + (col + 256 * k))
                loop(sp, phase, body)

            def rows_out(phase, w, rows, col=0):
                def body(i):
                    for k in range(2):
                        feature_job(phase, i, (rows // 4) * k, w, i * 512 + (col + 256 * k), rows)
                loop(sp, phase, body)

            gate("gate_a", G0)
            rows_out("attn_out", w_o_attn, KD)
            bc_job("first_group", 0, 0, 0)
            feature_job("first_group", 0, 4, w_in, X0)

            def group(phase, g, i, last=False):
                feature_job(phase, i, 0, w_in, g * GW + (X0 + 256))
                token_job(phase, i, 4, w_in, g * GW + Z0)
                if not last:
                    bc_job(phase, i, 12, g + 1)
                    feature_job(phase, i, 16, w_in, g * GW + (X0 + GW))
            loop(sp, "group", lambda i: group("group", i, i))
            group("last_group", GROUPS - 1, 0, last=True)
            gate("gate_s", G0 + D)
            rows_out("ssd_out", w_o_ssd, 2 * KD)
            for n in range(4):
                token_job("out", 0, 8 * n, w_out, 512 * n)
                if n == 0:
                    sp.wait_ge(S["m_sum2"], 8)
                    for t in range(TT):
                        sp.dma_start(x_sb[:, t, :], x[0, t * P:(t + 1) * P, :]).then_inc(S["x_loaded" if t == 0 else "x_again"], 16)
                    sp.wait_ge(S["m_lo"], 8)
                    sp.dma_start(wf, norm_final_w.partition_broadcast(P)).then_inc(S["wf_loaded"], 16)

            def down(phase, i, half, nb0):
                for k in range(2):
                    token_job(phase, i, 16 * k, w_down, i * 1024 + (512 * k + 512 * nb0), 2 * KD, half * 2 * KD)

            for half, name in enumerate("ab"):
                for part in range(2):
                    rows_out(f"up_{name}{part}", w_up, KD, half * (D_FF // 2) + part * D)
                if half == 0:
                    loop(sp, "down_a", lambda i: down("down_a", i, 0, 0))
                else:
                    down("down_b", 0, 1, 0)
                    down("down_end", 0, 1, 2)
            for n in range(4):
                for t, name in ((0, "out_act"), (1, "out_dve")):
                    cols = slice(n * 512, (n + 1) * 512)
                    sp.wait_ge(S[name], n + 1)
                    sp.dma_start(out[0, t * P:(t + 1) * P, cols], x_sb[:, t, cols]).then_inc(S["stored"], 16)
            sp.wait_ge(S["stored"], 8 * 16)

        @block.tensor
        def _(pe):
            mm = nc.tensor.matmul

            def split3(out_ap, a_hi, a_lo, b_hi, b_lo, start, stop):
                mm(out_ap, a_hi, b_hi, start=start, stop=False, skip_group_check=True)
                mm(out_ap, a_hi, b_lo, start=False, stop=False, skip_group_check=True)
                return mm(out_ap, a_lo, b_hi, start=False, stop=stop, skip_group_check=True)

            def bank_ready(phase, i, job, bank):
                u = bank_use(phase, i, job, bank)
                if not (isinstance(u, int) and u == 0):
                    pe.wait_ge(bank_free[bank], u)

            def feature_job(phase, i, job, acts, side=None, bc=False, before=None):
                n, (bank,) = PLAN[phase]["jobs"][job]
                x0 = job_end(phase, job) - n + 1
                bank_ready(phase, i, job, bank)
                for s in range(n):
                    slot = (x0 + s) % RING
                    if before:
                        before(s)
                    pe.wait_ge(S["lo_ready"], slab_no(phase, i, x0 + s) + 1)
                    for c in range(8):
                        col, f, k = (c, s // 2, 8 * (s % 2) + c) if bc else (2 * (c % 4) + c // 4, c // 4, 4 * s + c % 4)
                        w = slice(128 * col, 128 * col + 128)
                        a = acts(k)
                        last = split3(ps[bank][:, f * T:(f + 1) * T], w_hi[:, slot, w], w_lo[:, slot, w],
                                      a[:, 0:T], a[:, T:2 * T], start=(s == 0 and c == 0),
                                      stop=(k == (KD if n == 4 else 2 * KD) - 1))
                    last.then_inc(S["slab_used"], 1)
                    if side:
                        side(x0 + s)

            def token_job(phase, i, job, acts, side=None, narrow=False, before=None):
                n, banks = PLAN[phase]["jobs"][job]
                x0 = job_end(phase, job) - n + 1
                kts, width = (4, SSD_HEADS) if narrow else (2, 512)
                for b in banks:
                    bank_ready(phase, i, job, b)
                for s in range(n):
                    slot = (x0 + s) % RING
                    if before:
                        before(s)
                    pe.wait_ge(S["lo_ready"], slab_no(phase, i, x0 + s) + 1)
                    for k in range(kts):
                        c = slice(width * k, width * (k + 1))
                        a = acts(kts * s + k)
                        for t in range(TT):
                            last = split3(ps[banks[t]][:, 0:width], a[:, t * P:(t + 1) * P],
                                          a[:, T + t * P:T + (t + 1) * P], w_hi[:, slot, c], w_lo[:, slot, c],
                                          start=(s == 0 and k == 0), stop=(s == n - 1 and k == kts - 1))
                    last.then_inc(S["slab_used"], 1)
                    if side:
                        side(x0 + s)

            h = lambda k: act16[:, k, :]
            a32 = lambda k: act32[:, k, :]

            def x_t(r):
                pe.wait_ge(S["xn_act"], r // 2 + 1)
                pe.wait_ge(S["xn_dve"], r // 2 + 1)
                if r >= 4:
                    pe.wait_ge(S["h_lo"], 2 * (r - 4) + 2)
                for k in range(2):
                    for t in range(TT):
                        last = nc.tensor.transpose(ps[4 + r % 4][:, (2 * k + t) * P:(2 * k + t + 1) * P],
                                                   x_sb[:, t, (2 * r + k) * P:(2 * r + k + 1) * P], ident)
                last.then_inc(S["xt_done"], 1)
            pe.wait_ge(S["tables_loaded"], 32)
            for r in range(4):
                x_t(r)

            def rest_of_x(x):
                if x < 2:
                    x_t(4 + 2 * x)
                    x_t(5 + 2 * x)
            feature_job("kv", 0, 0, h, rest_of_x, before=lambda s: pe.wait_ge(S["h_lo"], 4 * s + 4))
            feature_job("kv", 0, 1, h)
            token_job("kv", 0, 2, h)
            token_job("kv", 0, 3, h, narrow=True)

            def scores(j):
                pe.wait_ge(bank_free[2], bank_use("q", j, 0, 2) + 1)
                pe.wait_ge(S["kc_ready"], j + 1)
                order = [(0, 0), (2, 0), (0, 1), (2, 1), (1, 1), (3, 1), (1, 0), (3, 0)]
                for g, t in order:
                    half = slice(64 * (g % 2), 64 * (g % 2) + 64)
                    if t == 0:
                        o, keys = ps[4][:, g * P:(g + 1) * P], P
                    else:
                        o, keys = ps[5 + g % 2][:, (g // 2) * T:(g // 2 + 1) * T], T
                    if (g, t) == (1, 0):
                        pe.wait_ge(S["even_scores"], j + 1)
                    last = mm(o, qt[half, g // 2, t * P:(t + 1) * P], kc[half, 0:keys], start=True, stop=True)
                    if (g, t) == (2, 0):
                        last.then_inc(S["even_scores"], 1)
                last.then_inc(S["scores_done"], 1)

            def probs_t(j):
                pe.wait_ge(S["probs_ready"], j + 1)
                for b in range(3):
                    if b == 2 and isinstance(j, int) and j == N_KV - 1:
                        pe.wait_ge(bank_free[3], bank_use("gate_a", 0, 1, 3) + 1)
                    for g in range(GQ):
                        src = p0[:, g, :] if b == 0 else p1[:, g, (b - 1) * P:b * P]
                        last = nc.tensor.transpose(ps[PT_BANKS[b]][:, g * P:(g + 1) * P], src, ident)
                last.then_inc(S["pt_done"], 1)

            def values(j):
                pe.wait_ge(S["pt_act"], j + 1)
                pe.wait_ge(S["pt_dve"], j + 1)
                pe.wait_ge(S["vc_ready"], j + 1)
                if not (isinstance(j, int) and j == 0):
                    pe.wait_ge(S["attn_lo"], j)
                for g in range(GQ):
                    half = slice(64 * (g % 2), 64 * (g % 2) + 64)
                    for t in range(TT):
                        o = ps[7][half, (g // 2) * T + t * P:(g // 2) * T + (t + 1) * P]
                        for k in range(t + 1):
                            last = mm(o, vc[:, k, :], pt[:, t + k, g * P:(g + 1) * P],
                                      start=(g < 2 and t == 0), stop=(k == t), skip_group_check=True)
                last.then_inc(S["pv_done"], 1)

            def attention(i, x, first=0):
                known = isinstance(i, int)
                if x == 3:
                    second = not (known and not 2 <= i < N_KV + 2)
                    if second:
                        probs_t(i - 2)
                    if not (known and not 1 <= i < N_KV + 1):
                        scores(i - 1)
                    if second:
                        values(i - 2)

            def cumsums():
                pe.wait_ge(S["a_ready"], 1)
                for t in range(TT):
                    mm(ps[7][:, t * 64:(t + 1) * 64], cum, a_t[:, t, :], start=True, stop=True)
                    mm(ps[7][:, 128 + t * 64:192 + t * 64], blk, a_t[:, t, :], start=True, stop=True)
                for c in (0, 2, 1, 3):
                    rows = slice(64 * (c % 2), 64 * (c % 2) + 64)
                    last = mm(ps[5 + c % 2][:, (c // 2) * 64:(c // 2 + 1) * 64], ones[rows, :], a_t[rows, c // 2, :],
                              start=True, stop=True)
                last.then_inc(S["cums_done"], 1)

            def q_body(i):
                def side(x):
                    if isinstance(i, int) and i == 0 and x == 3:
                        cumsums()
                    if isinstance(i, int) and i == 1 and x == 3:
                        pe.wait_ge(S["dec_ready"], 2)
                        for b in PT_BANKS:
                            pe.wait_ge(bank_free[b], PLAN["q"]["use0"][b])
                    attention(i, x)
                feature_job("q", i, 0, h, side)
            loop(pe, "q", q_body, peel=2)

            def gate_a_body(i):
                for k in range(2):
                    side = (lambda x, k=k: attention(N_KV + k, x - 4 * k)) if isinstance(i, int) and i == 0 else None
                    feature_job("gate_a", i, k, h, side)
            loop(pe, "gate_a", gate_a_body, peel=1)

            pe.wait_ge(S["attn_lo"], N_KV)

            def two_jobs(phase, acts):
                def body(i):
                    for k in range(2):
                        feature_job(phase, i, k, acts)
                return body

            def last_parts(name, first, last, slab):
                def before(s):
                    if s in (0, slab):
                        pe.wait_ge(S[name], first if s == 0 else last)
                return before
            loop(pe, "attn_out", two_jobs("attn_out", a32))

            feature_job("first_group", 0, 0, h, bc=True)
            feature_job("first_group", 0, 1, h)

            def ssd(g, x):
                known0 = isinstance(g, int) and g == 0
                if x == 1:
                    pe.wait_ge(S["rs_ready"], g + 1)
                    if not known0:
                        pe.wait_ge(S["y_part"], g * 4)
                    for t in range(TT):
                        mm(ps[4 + t][:, :], blk, rs[:, t, :], start=True, stop=True)
                    pe.wait_ge(S["silu_bc"], g + 1)
                    if not known0:
                        pe.wait_ge(S["y_lo"], g * 4)
                    for c in range(N_CHUNKS):
                        rows = slice(64 * (c % 2), 64 * (c % 2) + 64)
                        tok = slice(c * CHUNK, (c + 1) * CHUNK)
                        mm(ps[6][rows, (c // 2) * 64:(c // 2 + 1) * 64], cv[:, 4, tok], cv[:, 5, tok], start=True, stop=True)
                    for t in range(TT):
                        last = nc.tensor.transpose(ps[6][:, (1 + t) * P:(2 + t) * P], cv[:, 4, t * P:(t + 1) * P], ident)
                    last.then_inc(S["cb_done"], 1)
                if x == 7:
                    pe.wait_ge(S["silu_x"], g + 1)
                    pe.wait_ge(S["cbm_ready"], g + 1)
                    pe.wait_ge(S["btok_ready"], g + 1)
                    for t in range(TT):
                        for f in range(4):
                            last = nc.tensor.transpose(ps[7 - t][:, f * P:(f + 1) * P], cv[:, f, t * P:(t + 1) * P], ident)
                    last.then_inc(S["xt_tr"], 1)
                if x == 9:
                    pe.wait_ge(S["xdec_ready"], g + 1)
                    pe.wait_ge(S["seg_out"], 2 * g + 2)
                    pe.wait_ge(S["xs_used"], 4 * g + 4)
                    pe.wait_ge(S["mt_ready"], 2 * g + 2)
                    for c in range(3):
                        rows = slice(64 * (c % 2), 64 * (c % 2) + 64)
                        last = mm(ps[4 + c][:, :], btok[rows, c // 2, :], xdec[rows, c // 2, :], start=True, stop=True)
                    last.then_inc(S["st_done"], 1)
                    y_diag(0)
                if x == 13:
                    pe.wait_ge(S["prev3"], g + 1)
                    for c in range(1, N_CHUNKS):
                        rows = slice(64 * (c % 2), 64 * (c % 2) + 64)
                        last = mm(ps[5 + c // 2][rows, :], cv[:, 5, c * CHUNK:(c + 1) * CHUNK], prev[:, c - 1, :],
                                  start=True, stop=True)
                    last.then_inc(S["yo_done"], 1)
                    y_diag(1)
                if x == 19:
                    pe.wait_ge(S["yn_ready"], 2 * g + 2)
                    for f in range(4):
                        for t in range(TT):
                            last = nc.tensor.transpose(ps[6 + f // 2][:, (f % 2) * T + t * P:(f % 2) * T + (t + 1) * P],
                                                       yb[:, t, f * P:(f + 1) * P], ident)
                    last.then_inc(S["yt_done"], 1)

            def y_diag(t):
                for c in (2 * t, 2 * t + 1):
                    rows = slice(64 * (c % 2), 64 * (c % 2) + 64)
                    for r in range(HPG):
                        cols = slice(64 * r, 64 * r + 64)
                        last = mm(ps[7 if t == 0 else 4][rows, cols], mt[rows, t, cols], xdt[rows, t, cols],
                                  start=True, stop=True)
                last.then_inc(S["yd0_done" if t == 0 else "yd1_done"], 1)

            def group(phase, g, i, last=False):
                side = lambda x: ssd(g, x)
                feature_job(phase, i, 0, h, side)
                token_job(phase, i, 1, h, side)
                if not last:
                    feature_job(phase, i, 2, h, side, bc=True)
                    feature_job(phase, i, 3, h, side)
            loop(pe, "group", lambda i: group("group", i, i))
            group("last_group", GROUPS - 1, 0, last=True)

            def gate_s_body(i):
                side = (lambda x: ssd(GROUPS - 1, x + 12)) if isinstance(i, int) and i == 0 else None
                for k in range(2):
                    feature_job("gate_s", i, k, h, side)
            loop(pe, "gate_s", gate_s_body, peel=1)

            pe.wait_ge(S["y_lo"], 4 * GROUPS)
            loop(pe, "ssd_out", two_jobs("ssd_out", a32))

            def x2_t(nb):
                for b in PLAN["out"]["jobs"][nb][1]:
                    pe.wait_ge(bank_free[b], bank_use("out", 0, nb, b) + 1)
                for q in range(2):
                    r = 2 * nb + q
                    if r >= 4:
                        pe.wait_ge(S["h2_lo"], 2 * (r - 4) + 2)
                    for k in range(2):
                        for t in range(TT):
                            last = nc.tensor.transpose(ps[4 + r % 4][:, (2 * k + t) * P:(2 * k + t + 1) * P],
                                                       x_sb[:, t, (2 * r + k) * P:(2 * r + k + 1) * P], ident)
                    last.then_inc(S["x2t_done"], 1)
            for n in range(4):
                token_job("out", 0, n, h, (lambda x, n=n: x2_t(n - 1) if n and x == 8 * n + 1 else None),
                          before=last_parts("m_lo", 7, 8, 7) if n == 0 else None)

            def end_of_norm(x):
                if x == 0:
                    x2_t(3)
                if x == 2:
                    pe.wait_ge(S["diag_ready"], 1)
                    mm(ps[4][:, 0:T], ones, diag[:, :, :], start=True, stop=True).then_inc(S["rr_done"], 1)

            def up_first(i):
                first = isinstance(i, int) and i == 0
                feature_job("up_a0", i, 0, a32, end_of_norm if first else None,
                            before=last_parts("h2_lo", 12, 16, 3) if first else None)
                feature_job("up_a0", i, 1, a32)

            def u_act(k):
                return act32[:, 16 + k, :] if k < 16 else act16[:, k - 16, :]

            def down(phase, made=None):
                def body(i):
                    for k in range(2):
                        token_job(phase, i, k, u_act,
                                  before=last_parts("u_lo", made - 1, made, 15) if made and k == 0 else None)
                return body
            loop(pe, "up_a0", up_first, peel=1)
            loop(pe, "up_a1", two_jobs("up_a1", a32))
            loop(pe, "down_a", down("down_a", 16))
            loop(pe, "up_b0", two_jobs("up_b0", a32))
            loop(pe, "up_b1", two_jobs("up_b1", a32))
            down("down_b", 32)(0)
            down("down_end")(0)

        @block.scalar
        def _(act):
            activation = nc.scalar.activation

            def split(phase, i, x):
                n = slab_no(phase, i, x)
                if isinstance(n, int) and n + RING >= N_SLABS:
                    return
                slot = x % RING
                act.wait_ge(S["slab_used"], n + 1)
                act.wait_ge(raw_landed[slot], raw_count(slot, phase, i, x))
                w = width_of(n)
                activation(w_hi[:, slot, 0:w], raw[:, slot, 0:w], ACT.Copy).then_inc(S["hi_ready"], 1)

            act.dma_start(const[:, :], shape_table[:, 0:C_COLS]).then_inc(S["tables_loaded"], 16)
            act.dma_start(neg_all, shape_table[:, C_NEG:C_NEG + NEG_COLS]).then_inc(S["rows_loaded"], 16)
            act.dma_start(chan[:, :], channel_table).then_inc(S["tables_loaded"], 16)
            act.dma_start(sink_b[:, :], sinks.partition_broadcast(P)).then_inc(S["rows_loaded"], 16)
            act.dma_start(dskip_b[:, :], d_skip.partition_broadcast(P)).then_inc(S["rows_loaded"], 16)
            act.dma_start(dt_tmp[:, 0:64], dt_bias.partition_broadcast(P)).then_inc(S["rows_loaded"], 16)
            act.dma_start(dt_tmp[:, 64:128], a_log.partition_broadcast(P)).then_inc(S["rows_loaded"], 16)

            act.wait_ge(S["x_loaded"], 16)
            activation(ga[:, 0:D], x_sb[:, 0, :], ACT.Square, accum_out=small[:, 0:1]).then_inc(S["ssq1_act"], 1)
            act.wait_ge(S["ssq1_act"], 1)
            act.wait_ge(S["ssq1_dve"], 1)
            act.wait_ge(S["tables_loaded"], 32)
            activation(small[:, 2:4], small[:, 0:2], ACT.Sqrt, scale=1.0 / D, bias=const[:, C_EPS:C_EPS + 1]) \
                .then_inc(S["std1_ready"], 1)
            act.wait_ge(S["rstd1_ready"], 1)
            for n in range(4):
                cols = slice(n * 512, (n + 1) * 512)
                activation(x_sb[:, 0, cols], x_sb[:, 0, cols], ACT.Copy, scale=small[:, 2:3]).then_inc(S["xn_act"], 1)
            for r in range(KD // 2):
                if r < RING:
                    act.wait_ge(raw_landed[r], 16)
                    activation(w_hi[:, r, :], raw[:, r, :], ACT.Copy).then_inc(S["hi_ready"], 1)
                act.wait_ge(S["xt_done"], r + 1)
                for k in (2 * r, 2 * r + 1):
                    activation(act16[:, k, 0:T], ps[4 + r % 4][:, (k % 2) * T:(k % 2 + 1) * T], ACT.Copy,
                               scale=chan[:, V_N1 + k:V_N1 + k + 1]).then_inc(S["h_hi"], 1)

            for x in range(20):
                if x == 15:
                    act.wait_ge(S["slab_used"], 16)
                    for t in range(TT):
                        activation(vs[:, t, :], ps[2 + t][:, :], ACT.Copy).then_inc(bank_free[2 + t], 1)
                if x == 19:
                    act.wait_ge(S["rows_loaded"], 80)
                    activation(dt_tmp[:, 64:128], dt_tmp[:, 64:128], ACT.Exp).then_inc(S["neg_a"], 1)
                    act.wait_ge(S["dt_v"], 1)
                    activation(dt_tmp[:, 256:384], dt_tmp[:, 256:384], ACT.Exp, scale=-1.0).then_inc(S["dt_e"], 1)
                split("kv", 0, x)

            def attention(i, x):
                known = isinstance(i, int)
                if not (known and not 2 <= i < N_KV + 2):
                    j = i - 2
                    if x == 0:
                        act.wait_ge(S["shift_ready"], j + 1)
                        for g in range(GQ):
                            activation(p0[:, g, :], p0[:, g, :], ACT.Exp, scale=0.125, bias=negm[:, g:g + 1],
                                       accum_out=rsum[:, g:g + 1])
                            activation(p1[:, g, :], p1[:, g, :], ACT.Exp, scale=0.125, bias=negm[:, 4 + g:5 + g],
                                       accum_out=rsum[:, 4 + g:5 + g])
                        activation(es, es, ACT.Exp).then_inc(S["exp_done"], 1)
                    if x == "probs":
                        act.wait_ge(S["pt_done"], j + 1)
                        activation(pt[:, 0, :], ps[PT_BANKS[0]][:, :], ACT.Copy)
                        activation(pt[:, 2, :], ps[PT_BANKS[2]][:, :], ACT.Copy).then_inc(S["pt_act"], 1)
                    if x == "values":
                        act.wait_ge(S["pv_done"], j + 1)
                        activation(act32[:, bass.ds(2 * j, 2), 0:T], ps[7][:, :].rearrange("p (f t) -> p f t", f=2),
                                   ACT.Copy).then_inc(S["attn_hi"], 1)

            def q_body(i):
                for x in range(4):
                    if x == 3:
                        attention(i, "probs")
                        act.wait_ge(S["slab_used"], slab_no("q", i, 3) + 1)
                        if not (isinstance(i, int) and i == 0):
                            act.wait_ge(S["scores_done"], i)
                        activation(qt[:, :, :], ps[2][:, :].rearrange("p (f t) -> p f t", f=2), ACT.Copy) \
                            .then_inc(bank_free[2], 1)
                        attention(i, "values")
                    attention(i, x)
                    if isinstance(i, int) and i == 1 and x == 0:
                        act.wait_ge(S["acs_ready"], 1)
                        activation(ea_t[:, :, :], acs_t[:, :, :], ACT.Exp).then_inc(S["dec_ready"], 1)
                        act.wait_ge(S["dec_in"], 1)
                        activation(dec_t[:, :, :], dec_t[:, :, :], ACT.Exp)
                        for odd in range(2):
                            last = activation(cdec[:, odd::2, :], ps[5 + odd][:, 0:128].rearrange("p (c h) -> p c h", c=2),
                                              ACT.Exp)
                        last.then_inc(S["dec_ready"], 1)
                    split("q", i, x)
            loop(act, "q", q_body, peel=2)

            def gates(phase, dst, col, peel=0, side=None, late=False):
                def body(i):
                    for k in range(2):
                        for x in range(4 * k, 4 * k + 4):
                            if side and isinstance(i, int) and i == 0 and not late:
                                side(x)
                            if x == 4 * k + 3:
                                bank = PLAN[phase]["jobs"][k][1][0]
                                if phase == "gate_s" and isinstance(i, int):
                                    act.wait_ge(S["y_ready"], 2 * GROUPS)
                                act.wait_ge(S["slab_used"], slab_no(phase, i, x) + 1)
                                for f in range(2):
                                    ft = 4 * i + (2 * k + f)
                                    last = activation(dst[:, bass.ds(ft, 1), :],
                                                      ps[bank][:, f * T:(f + 1) * T].unsqueeze(1), ACT.Tanh, scale=0.5,
                                                      bias=chan[:, bass.ds(ft + col, 1)])
                                last.then_inc(bank_free[bank], 1)
                            if side and isinstance(i, int) and i == 0 and late:
                                side(x)
                            split(phase, i, x)
                loop(act, phase, body, peel)
            act.wait_ge(S["half_ready"], 1)
            
            def attention_end(x):
                for part in (("probs", "values") if x % 4 == 3 else (x % 4,)):
                    attention(N_KV + x // 4, part)
            gates("gate_a", ga_f, V_GB, 1, attention_end, late=True)

            def only_split(phase):
                def body(i):
                    for x in range(PLAN[phase]["slabs"]):
                        split(phase, i, x)
                return body
            loop(act, "attn_out", only_split("attn_out"))

            def conv_in(phase, i, x, bank, f0):
                act.wait_ge(S["slab_used"], slab_no(phase, i, x) + 1)
                activation(upad[:, f0:f0 + 2, 4:4 + T], ps[bank][:, :].rearrange("p (f t) -> p f t", f=2), ACT.Copy) \
                    .then_inc(bank_free[bank], 1)

            act.wait_ge(S["pad_zero"], 1)
            for x in range(8):
                if x == 3:
                    conv_in("first_group", 0, 3, 0, 4)
                if x == 4:
                    act.wait_ge(S["conv_bc"], 8)
                    activation(th[:, 4:6, :], cv[:, 4:6, :], ACT.Tanh).then_inc(S["th_bc"], 1)
                if x == 7:
                    conv_in("first_group", 0, 7, 1, 0)
                split("first_group", 0, x)

            def ssd(g, x, phase, i, last=False):
                if x == 1:
                    act.wait_ge(S["cb_done"], g + 1)
                    activation(btok[:, :, :], ps[6][:, P:P + T].rearrange("p (t n) -> p t n", t=TT), ACT.Copy) \
                        .then_inc(S["btok_ready"], 1)
                if x == 3:
                    conv_in(phase, i, 3, 0, 2)
                    act.wait_ge(S["seg_out"], 2 * g + 2)
                    activation(mt[:, :, :], mt[:, :, :], ACT.Relu, scale=-1.0).then_inc(S["seg_min"], 1)
                    act.wait_ge(S["seg_min"], g + 1)
                    activation(mt[:, :, :], mt[:, :, :], ACT.Exp, scale=-1.0).then_inc(S["seg_exp"], 1)
                if x == 5:
                    act.wait_ge(S["conv_xb"], 8 * g + 8)
                    activation(th[:, 0:4, :], cv[:, 0:4, :], ACT.Tanh).then_inc(S["th_x"], 1)
                if x == 9:
                    act.wait_ge(S["st_done"], g + 1)
                    activation(prev[:, 0, :], ps[4][:, :], ACT.Copy).then_inc(S["prev1"], 1)
                if x == 11:
                    act.wait_ge(S["slab_used"], slab_no(phase, i, 11) + 1)
                    for t in range(TT):
                        activation(sz[:, t, :], ps[2 + t][:, :], ACT.Tanh, scale=0.5).then_inc(S["tz_ready"], 1)
                if x == 15 and not last:
                    conv_in(phase, i, 15, 0, 4)
                if x == 17 and not last:
                    act.wait_ge(S["conv_bc"], 8 * g + 16)
                    activation(th[:, 4:6, :], cv[:, 4:6, :], ACT.Tanh).then_inc(S["th_bc"], 1)
                if x == 16:
                    for t in range(TT):
                        act.wait_ge(S["y_ready"], 2 * g + t + 1)
                        activation(xdt[:, t, :], yb[:, t, :], ACT.Square, accum_out=small[:, 4 + t:5 + t]) \
                            .then_inc(S["ssq_g"], 1)
                    act.wait_ge(S["ssq_g"], 2 * g + 2)
                    activation(small[:, 6:8], small[:, 4:6], ACT.Sqrt, scale=1.0 / GW, bias=const[:, C_EPS4:C_EPS4 + 1]) \
                        .then_inc(S["std_g"], 1)
                if x == 18:
                    act.wait_ge(S["rstd_g"], g + 1)
                    for t in range(TT):
                        activation(yb[:, t, :], yb[:, t, :], ACT.Copy, scale=small[:, 8 + t:9 + t]).then_inc(S["yn_ready"], 1)
                if x == 19:
                    if not last:
                        conv_in(phase, i, 19, 1, 0)
                    act.wait_ge(S["yt_done"], g + 1)
                    for f in range(4):
                        activation(act32[:, bass.ds(4 * g + f, 1), 0:T],
                                   ps[6 + f // 2][:, (f % 2) * T:(f % 2 + 1) * T].unsqueeze(1), ACT.Copy,
                                   scale=chan[:, bass.ds(4 * g + (V_SN + f), 1)]).then_inc(S["y_hi"], 1)

            def group_body(i):
                for x in range(20):
                    ssd(i, x, "group", i)
                    split("group", i, x)
            loop(act, "group", group_body)
            for x in range(12):
                ssd(GROUPS - 1, x, "last_group", 0, last=True)
                split("last_group", 0, x)
            gates("gate_s", gs, V_GB + KD, 1, lambda x: (act.wait_ge(S["y_lo"], 4 * GROUPS - 4) if x == 0 else None,
                                                         ssd(GROUPS - 1, x + 12, None, None, last=True)))

            def ssd_out_body(i):
                for k in range(2):
                    for x in range(8 * k, 8 * k + 8):
                        if x == 8 * k + 7:
                            act.wait_ge(S["m_sum2"], 2 * i + (k + 1))
                            activation(act16[:, bass.ds(4 * i + 2 * k, 2), 0:T], ga_f[:, bass.ds(4 * i + 2 * k, 2), :],
                                       ACT.Copy, scale=0.5).then_inc(S["m_hi"], 1)
                        split("ssd_out", i, x)
            loop(act, "ssd_out", ssd_out_body)

            def x2_side(nb):
                for q in range(2):
                    r = 2 * nb + q
                    act.wait_ge(S["x2t_done"], r + 1)
                    for k in (2 * r, 2 * r + 1):
                        activation(act32[:, k, 0:T], ps[4 + r % 4][:, (k % 2) * T:(k % 2 + 1) * T], ACT.Copy,
                                   scale=chan[:, V_N2 + k:V_N2 + k + 1]).then_inc(S["h2_hi"], 1)

            def squares(phase, job, nb, done, tiles=TT):
                for b in PLAN[phase]["jobs"][job][1]:
                    act.wait_ge(bank_free[b], bank_use(phase, 0, job, b) + 1)
                for t in range(tiles):
                    n = 2 * nb + t
                    if n >= 4:
                        act.wait_ge(S[done], n - 3)
                    activation(junk[:, (n % 4) * 512:(n % 4 + 1) * 512], x_sb[:, t, nb * 512:(nb + 1) * 512], ACT.Square,
                               accum_out=ssq[:, t, nb:nb + 1]).then_inc(S[done], 1)
            for n in range(4):
                for x in range(8 * n, 8 * n + 8):
                    if n and x == 8 * n + 1:
                        x2_side(n - 1)
                    if x == 8 * n + 7:
                        squares("out", n, n, "sq2_ready")
                    split("out", 0, x)

            def end_of_norm():
                x2_side(3)
                act.wait_ge(S["ssq2_sum"], 1)
                activation(small[:, 12:14], small[:, 10:12], ACT.Sqrt, scale=1.0 / D, bias=const[:, C_EPS:C_EPS + 1]) \
                    .then_inc(S["std2"], 1)

            def up(phase, n0, dst, ft0):
                def body(i):
                    for k in range(2):
                        for x in range(4 * k, 4 * k + 4):
                            if phase == "up_a0" and isinstance(i, int) and i == 0 and x == 0:
                                end_of_norm()
                            if x == 4 * k + 3:
                                bank = PLAN[phase]["jobs"][k][1][0]
                                act.wait_ge(bank_free[bank], bank_use(phase, i, k, bank) + 1)
                                activation(dst[:, bass.ds(4 * i + (ft0 + 2 * k), 2), 0:T],
                                           tu[:, k, :].rearrange("p (f t) -> p f t", f=2), ACT.Square) \
                                    .then_inc(S["u_hi"], 1)
                            split(phase, i, x)
                loop(act, phase, body, peel=1 if phase == "up_a0" else 0)
            up("up_a0", 0, act32, 16)
            up("up_a1", 8, act16, 0)
            loop(act, "down_a", only_split("down_a"))
            up("up_b0", 16, act32, 16)
            up("up_b1", 24, act16, 0)
            for phase, nb0 in (("down_b", 0), ("down_end", 2)):
                for k in range(2):
                    for x in range(16 * k, 16 * k + 16):
                        if x == 16 * k + 15:
                            squares(phase, k, nb0 + k, "sq3_ready", TT if nb0 + k < 3 else 1)
                        split(phase, 0, x)
                if nb0 == 0:
                    activation(small[:, 24:25], const[:, C_EPS:C_EPS + 1], ACT.Sqrt)
            act.wait_ge(S["ssq3_sum"], 1)
            activation(small[:, 20:22], small[:, 18:20], ACT.Sqrt, scale=1.0 / D, bias=const[:, C_EPS:C_EPS + 1]) \
                .then_inc(S["std3"], 1)
            act.wait_ge(S["rstd3"], 1)
            act.wait_ge(S["x3_w"], 8)
            for n in range(4):
                cols = slice(n * 512, (n + 1) * 512)
                activation(x_sb[:, 0, cols], x_sb[:, 0, cols], ACT.Copy, scale=small[:, 22:23]).then_inc(S["out_act"], 1)

        @block.vector
        def _(dve):
            v = nc.vector
            stt = v.scalar_tensor_tensor
            tt = v.tensor_tensor

            def split(phase, i, x):
                n = slab_no(phase, i, x)
                if isinstance(n, int) and n + RING >= N_SLABS:
                    return
                w = width_of(n)
                slot = x % RING
                dve.wait_ge(S["hi_ready"], n + RING + 1)
                tt(w_lo[:, slot, 0:w], raw[:, slot, 0:w], w_hi[:, slot, 0:w].bitcast(F32), ALU.subtract) \
                    .then_inc(S["lo_ready"], 1)

            def f2(ap):
                return ap.rearrange("p (f t) -> p f t", f=2)

            chain = Chain(dve, sem("dve_step"))

            dve.wait_ge(S["x_again"], 16)
            stt(out=ga[:, D:2 * D], in0=x_sb[:, 1, :], scalar=1.0, in1=x_sb[:, 1, :], op0=ALU.mult, op1=ALU.mult,
                accum_out=small[:, 1:2]).then_inc(S["ssq1_dve"], 1)
            dve.wait_ge(S["std1_ready"], 1)
            v.reciprocal(small[:, 2:4], small[:, 2:4]).then_inc(S["rstd1_ready"], 1)
            dve.wait_ge(S["rstd1_ready"], 1)
            for n in range(4):
                cols = slice(n * 512, (n + 1) * 512)
                v.tensor_scalar(x_sb[:, 1, cols], x_sb[:, 1, cols], small[:, 3:4], None, ALU.mult).then_inc(S["xn_dve"], 1)
            for k in range(KD):
                if k % 2 == 0 and k // 2 < RING:
                    slot = k // 2
                    dve.wait_ge(S["hi_ready"], slot + 1)
                    tt(w_lo[:, slot, :], raw[:, slot, :], w_hi[:, slot, :].bitcast(F32), ALU.subtract) \
                        .then_inc(S["lo_ready"], 1)
                dve.wait_ge(S["h_hi"], 2 * (k // 2) + 2)
                stt(out=act16[:, k, T:2 * T], in0=ps[4 + (k // 2) % 4][:, (k % 2) * T:(k % 2 + 1) * T],
                    scalar=chan[:, V_N1 + k:V_N1 + k + 1], in1=act16[:, k, 0:T].bitcast(F32), op0=ALU.mult,
                    op1=ALU.subtract).then_inc(S["h_lo"], 1)
            v.tensor_scalar(chan[:, V_GB:V_SN], chan[:, V_GB:V_SN], 0.5, None, ALU.mult).then_inc(S["half_ready"], 1)

            a_exp, bias_b = dt_tmp[:, 64:128], dt_tmp[:, 0:64]
            val, e, sq, pol = [dt_tmp[:, 128 * n:128 * n + 128] for n in (1, 2, 3, 4)]
            v3 = lambda ap: ap.rearrange("p (t h) -> p t h", t=TT)
            for x in range(20):
                if x in (3, 7):
                    b = x // 4
                    dve.wait_ge(S["slab_used"], x + 1)
                    for par in range(2):
                        for half in range(2):
                            last = v.tensor_copy(ks[64 * half:64 * half + 64, 2 * b:2 * b + 2, par, :],
                                                 f2(ps[b][64 * par:64 * par + 64, :]))
                    last.then_inc(bank_free[b], 1)
                if x == 19:
                    dve.wait_ge(S["slab_used"], 20)
                    dve.wait_ge(S["rows_loaded"], 80)
                    for t in range(TT):
                        tt(v3(val)[:, t, :], ps[t][:, 0:64], bias_b, ALU.add).then_inc(bank_free[t], 1)
                    dve.wait_ge(bank_free[0], 2)
                    dve.wait_ge(bank_free[1], 2)
                    stt(out=e, in0=val, scalar=-1.0, in1=val, op0=ALU.mult, op1=ALU.max).then_inc(S["dt_v"], 1)
                    dve.wait_ge(S["dt_e"], 1)
                    chain.link(v.tensor_scalar(sq, e, 2.0, None, ALU.add))
                    chain.link(v.reciprocal(sq, sq))
                    chain.link(tt(e, e, sq, ALU.mult))
                    chain.link(tt(sq, e, e, ALU.mult))
                    chain.link(v.tensor_scalar(pol, sq, 1.0 / 17, None, ALU.mult))
                    for c in (15, 13, 11, 9, 7, 5, 3):
                        chain.link(stt(out=pol, in0=pol, scalar=1.0 / c, in1=sq, op0=ALU.add, op1=ALU.mult))
                    chain.link(stt(out=pol, in0=pol, scalar=1.0, in1=e, op0=ALU.add, op1=ALU.mult))
                    chain.link(v.tensor_scalar(val, val, 0.0, None, ALU.max))
                    chain.link(stt(out=dt_t[:, :, :], in0=v3(pol), scalar=2.0, in1=v3(val), op0=ALU.mult, op1=ALU.add))
                    dve.wait_ge(S["neg_a"], 1)
                    stt(out=a_t[:, :, :], in0=dt_t[:, :, :], scalar=-1.0,
                        in1=a_exp.unsqueeze(1).to_broadcast([P, TT, SSD_HEADS]), op0=ALU.mult, op1=ALU.mult) \
                        .then_inc(S["a_ready"], 1)
                split("kv", 0, x)
            attn0 = chain.n
            ATTN_STEPS = 5

            def attention(i, x):
                known = isinstance(i, int)
                if not (known and not 2 <= i < N_KV + 2):
                    j = i - 2
                    chain.at(attn0 + j * ATTN_STEPS)
                    if x == 2:
                        dve.wait_ge(S["exp_done"], j + 1)
                        chain.n = 3
                        chain.link(tt(den, rsum, es, ALU.add))
                        chain.link(v.reciprocal(rden, den))
                        tt(p0[:, :, :], p0[:, :, :], rden[:, 0:4].unsqueeze(2).to_broadcast([P, GQ, P]), ALU.mult)
                        tt(p1[:, :, :], p1[:, :, :], rden[:, 4:8].unsqueeze(2).to_broadcast([P, GQ, T]), ALU.mult) \
                            .then_inc(S["probs_ready"], 1)
                    if x == 3:
                        dve.wait_ge(S["pt_done"], j + 1)
                        v.tensor_copy(pt[:, 1, :], ps[PT_BANKS[1]][:, :]).then_inc(S["pt_dve"], 1)
                if x == 3 and not (known and not 1 <= i < N_KV + 1):
                    j = i - 1
                    chain.at(attn0 + j * ATTN_STEPS)
                    dve.wait_ge(S["scores_done"], j + 1)
                    for g in range(GQ):
                        slope = const[:, bass.ds(4 * j + (C_SLOPE + g), 1)]
                        stt(out=p0[:, g, :], in0=negd[0], scalar=slope, in1=ps[4][:, g * P:(g + 1) * P],
                            op0=ALU.mult, op1=ALU.add)
                        last = stt(out=p1[:, g, :], in0=negd[1], scalar=slope,
                                   in1=ps[5 + g % 2][:, (g // 2) * T:(g // 2 + 1) * T], op0=ALU.mult, op1=ALU.add)
                    chain.link(last)
                    v.tensor_reduce(mx[:, 0:4], p0[:, :, :], AX, ALU.max)
                    chain.link(v.tensor_reduce(mx[:, 4:8], p1[:, :, :], AX, ALU.max))
                    sink = sink_b[:, bass.ds(4 * j, 4)].unsqueeze(1).to_broadcast([P, 2, 4])
                    two = lambda ap: ap.rearrange("p (t g) -> p t g", t=2)
                    chain.link(stt(out=two(mm_), in0=two(mx), scalar=0.125, in1=sink, op0=ALU.mult, op1=ALU.max))
                    tt(two(es), sink, two(mm_), ALU.subtract)
                    v.tensor_scalar(negm, mm_, -1.0, None, ALU.mult).then_inc(S["shift_ready"], 1)
                    chain.n = 0
                if x == 3 and not (known and not 2 <= i < N_KV + 2):
                    j = i - 2
                    dve.wait_ge(S["attn_hi"], j + 1)
                    tt(act32[:, bass.ds(2 * j, 2), T:2 * T], f2(ps[7][:, :]),
                       act32[:, bass.ds(2 * j, 2), 0:T].bitcast(F32), ALU.subtract).then_inc(S["attn_lo"], 1)

            def q_body(i):
                for x in range(4):
                    attention(i, x)
                    if isinstance(i, int) and i == 1 and x == 0:
                        dve.wait_ge(S["cums_done"], 1)
                        v.tensor_copy(acs_t[:, :, :], ps[7][:, 0:128].rearrange("p (t h) -> p t h", t=TT)) \
                            .then_inc(S["acs_ready"], 1)
                        dve.wait_ge(S["acs_ready"], 1)
                        tt(dec_t[:, :, :], ps[7][:, 128:256].rearrange("p (t h) -> p t h", t=TT), acs_t[:, :, :],
                           ALU.subtract).then_inc(S["dec_in"], 1)
                    split("q", i, x)
            loop(dve, "q", q_body, peel=2)

            def gate_a_body(i):
                for x in range(8):
                    if isinstance(i, int) and i == 0:
                        attention(N_KV + x // 4, x % 4)
                    split("gate_a", i, x)
            loop(dve, "gate_a", gate_a_body, peel=1)

            def attn_out_body(i):
                for k in range(2):
                    for x in range(4 * k, 4 * k + 4):
                        if x == 4 * k + 3:
                            bank = PLAN["attn_out"]["jobs"][k][1][0]
                            dve.wait_ge(S["slab_used"], slab_no("attn_out", i, x) + 1)
                            dst = ga_f[:, bass.ds(4 * i + 2 * k, 2), :]
                            stt(out=dst, in0=dst, scalar=1.0, in1=f2(ps[bank][:, :]), op0=ALU.add, op1=ALU.mult) \
                                .then_inc(bank_free[bank], 1)
                        split("attn_out", i, x)
            dve.wait_ge(bank_free[2], bank_use("attn_out", 0, 0, 2))
            dve.wait_ge(bank_free[3], bank_use("attn_out", 0, 1, 3))
            loop(dve, "attn_out", attn_out_body)

            v.memset(upad[:, :, 0:4], 0.0).then_inc(S["pad_zero"], 1)

            def conv(fts, cols, done, base, bank):
                step = 0
                for tap in range(CONV_K):
                    for n, f in enumerate(fts):
                        src = upad[:, f, 1 + tap:1 + tap + T]
                        w = chan[:, bass.ds(cols[n] * CONV_K + (V_CW + tap), 1)]
                        if tap == 0:
                            ins = v.tensor_scalar(cv[:, f, :], src, w, chan[:, bass.ds(cols[n] + V_CB, 1)], ALU.mult, ALU.add)
                        else:
                            dve.wait_ge(S[done], base + step - len(fts) + 1)
                            ins = stt(out=cv[:, f, :], in0=src, scalar=w, in1=cv[:, f, :], op0=ALU.mult, op1=ALU.add)
                        ins.then_inc(S[done], 1)
                        step += 1

            def conv_bc(g, n, phase, i, job):
                dve.wait_ge(bank_free[0], bank_use(phase, i, job, 0) + 1)
                conv([4, 5], [g + 32, g + 40], "conv_bc", n * 8, 0)

            def silu_bc(n):
                dve.wait_ge(S["th_bc"], n + 1)
                stt(out=cv[:, 4:6, :], in0=th[:, 4:6, :], scalar=1.0, in1=cv[:, 4:6, :], op0=ALU.add, op1=ALU.mult) \
                    .then_inc(S["silu_bc"], 1)

            def conv_x(g, which, n, phase, i, job):
                bank = 1 - which
                dve.wait_ge(bank_free[bank], bank_use(phase, i, job, bank) + 1)
                f = 2 * which
                conv([f, f + 1], [4 * g + f, 4 * g + (f + 1)], "conv_xa" if which == 0 else "conv_xb", n * 8, 0)

            for x in range(8):
                if x == 3:
                    conv_bc(0, 0, "first_group", 0, 0)
                if x == 5:
                    silu_bc(0)
                if x == 7:
                    conv_x(0, 0, 0, "first_group", 0, 1)
                split("first_group", 0, x)

            heads = lambda ap: ap.rearrange("p (h n) -> p h n", h=HPG)

            def per_head(table, t, g, rows=slice(0, P)):
                n = rows.stop - rows.start
                return table[rows, t, bass.ds(g * HPG, HPG)].unsqueeze(2).to_broadcast([n, HPG, 64])

            def ssd(g, x, phase, i, last=False):
                if x == 1 or x == 2:
                    t = x - 1
                    dve.wait_ge(S["cb_done"], g + 1)
                    tt(heads(mt[:, t, :]), heads(ps[4 + t][:, :]), per_head(acs_t, t, g), ALU.subtract) \
                        .then_inc(S["seg_out"], 1)
                if x == 2:
                    dve.wait_ge(S["btok_ready"], g + 1)
                    tt(cbm[:, :, :], ps[6][:, 0:P].rearrange("p (t l) -> p t l", t=TT),
                       tri.unsqueeze(1).to_broadcast([P, TT, 64]), ALU.mult).then_inc(S["cbm_ready"], 1)
                if x == 3:
                    conv_x(g, 1, g, phase, i, 0)
                if x == 5:
                    dve.wait_ge(S["cbm_ready"], g + 1)
                    dve.wait_ge(S["seg_exp"], g + 1)
                    for t in range(TT):
                        tt(heads(mt[:, t, :]), heads(mt[:, t, :]),
                           cbm[:, t, :].unsqueeze(1).to_broadcast([P, HPG, 64]), ALU.mult).then_inc(S["mt_ready"], 1)
                if x == 6:
                    dve.wait_ge(S["th_x"], g + 1)
                    stt(out=cv[:, 0:4, :], in0=th[:, 0:4, :], scalar=1.0, in1=cv[:, 0:4, :], op0=ALU.add, op1=ALU.mult) \
                        .then_inc(S["silu_x"], 1)
                if x == 7:
                    dve.wait_ge(S["xt_tr"], g + 1)
                    for t in range(TT):
                        src = heads(ps[7 - t][:, :])
                        tt(heads(xdt[:, t, :]), src, per_head(dt_t, t, g), ALU.mult).then_inc(S["xs_used"], 1)
                        d = dskip_b[:, bass.ds(g * HPG, HPG)].unsqueeze(2).to_broadcast([P, HPG, 64])
                        tt(heads(xd[:, t, :]), src, d, ALU.mult).then_inc(S["xs_used"], 1)
                if x == 9 or x == 10:
                    c = x - 8
                    dve.wait_ge(S["prev1"], g + 1)
                    if c == 2:
                        dve.wait_ge(S["prev2"], g + 1)
                    d = cdec[:, c, bass.ds(g * HPG, HPG)].unsqueeze(2).to_broadcast([P, HPG, 64])
                    tt(heads(prev[:, c, :]), heads(prev[:, c - 1, :]), d, ALU.mult).then_inc(S["prev_tmp"], 1)
                    dve.wait_ge(S["prev_tmp"], 2 * g + c)
                    tt(prev[:, c, :], prev[:, c, :], ps[4 + c][:, :], ALU.add).then_inc(S["prev2" if c == 1 else "prev3"], 1)
                    if c == 2:
                        dve.wait_ge(S["yd0_done"], g + 1)
                        tt(yb[:, 0, :], ps[7][:, :], xd[:, 0, :], ALU.add).then_inc(S["y_part"], 1)
                if x == 11:
                    for t in range(TT):
                        dve.wait_ge(S["tz_ready"], 2 * g + t + 1)
                        stt(out=sz[:, t, :], in0=sz[:, t, :], scalar=1.0, in1=ps[2 + t][:, :], op0=ALU.add, op1=ALU.mult) \
                            .then_inc(bank_free[2 + t], 1)
                if x == 13:
                    dve.wait_ge(S["yd1_done"], g + 1)
                    tt(yb[:, 1, :], ps[4][:, :], xd[:, 1, :], ALU.add).then_inc(S["y_part"], 1)
                    for t in range(TT):
                        rows = slice(64, P) if t == 0 else slice(0, P)
                        tt(heads(mt[rows, t, :]), heads(ps[5 + t][rows, :]), per_head(ea_t, t, g, rows), ALU.mult) \
                            .then_inc(S["y_part"], 1)
                if x == 14:
                    dve.wait_ge(S["y_part"], 4 * g + 4)
                    for t in range(TT):
                        rows = slice(64, P) if t == 0 else slice(0, P)
                        tt(yb[rows, t, :], yb[rows, t, :], mt[rows, t, :], ALU.add).then_inc(S["y_tmp"], 1)
                    for t in range(TT):
                        dve.wait_ge(S["y_tmp"], 2 * g + t + 1)
                        if t == 0:
                            dve.wait_ge(bank_free[3], sz_uses(g))
                        tt(yb[:, t, :], yb[:, t, :], sz[:, t, :], ALU.mult).then_inc(S["y_ready"], 1)
                if x == 15 and not last:
                    conv_bc(g + 1, g + 1, phase, i, 2)
                if x == 17:
                    dve.wait_ge(S["std_g"], g + 1)
                    v.reciprocal(small[:, 8:10], small[:, 6:8]).then_inc(S["rstd_g"], 1)
                    if not last:
                        silu_bc(g + 1)
                if x == 19:
                    if not last:
                        conv_x(g + 1, 0, g + 1, phase, i, 3)
                    for f in range(4):
                        dve.wait_ge(S["y_hi"], 4 * g + (2 * (f // 2) + 2))
                        ft = bass.ds(4 * g + f, 1)
                        stt(out=act32[:, ft, T:2 * T], in0=ps[6 + f // 2][:, (f % 2) * T:(f % 2 + 1) * T].unsqueeze(1),
                            scalar=chan[:, bass.ds(4 * g + (V_SN + f), 1)], in1=act32[:, ft, 0:T].bitcast(F32),
                            op0=ALU.mult, op1=ALU.subtract).then_inc(S["y_lo"], 1)

            def sz_uses(g):
                return PLAN["group"]["use0"][3] + 1 + g * PLAN["group"]["uses"][3]

            def group_body(i):
                for x in range(20):
                    ssd(i, x, "group", i)
                    split("group", i, x)
            loop(dve, "group", group_body)
            for x in range(12):
                ssd(GROUPS - 1, x, "last_group", 0, last=True)
                split("last_group", 0, x)

            def gate_s_body(i):
                for x in range(8):
                    if isinstance(i, int) and i == 0:
                        ssd(GROUPS - 1, x + 12, None, None, last=True)
                    split("gate_s", i, x)
            loop(dve, "gate_s", gate_s_body, peel=1)

            dve.wait_ge(bank_free[0], bank_use("out", 0, 0, 0))
            dve.wait_ge(bank_free[1], bank_use("out", 0, 0, 1))

            def ssd_out_body(i):
                for k in range(2):
                    for x in range(8 * k, 8 * k + 8):
                        if x == 8 * k + 7:
                            bank = 2 + k
                            n = 2 * i + k
                            ft = bass.ds(4 * i + 2 * k, 2)
                            dve.wait_ge(S["slab_used"], slab_no("ssd_out", i, x) + 1)
                            stt(out=gs[:, ft, :], in0=gs[:, ft, :], scalar=1.0, in1=f2(ps[bank][:, :]), op0=ALU.add,
                                op1=ALU.mult).then_inc(bank_free[bank], 1)
                            dve.wait_ge(bank_free[bank], bank_use("ssd_out", i, k, bank) + 1)
                            tt(ga_f[:, ft, :], ga_f[:, ft, :], gs[:, ft, :], ALU.add).then_inc(S["m_sum2"], 1)
                            dve.wait_ge(S["m_hi"], n + 1)
                            stt(out=act16[:, ft, T:2 * T], in0=ga_f[:, ft, :], scalar=0.5,
                                in1=act16[:, ft, 0:T].bitcast(F32), op0=ALU.mult, op1=ALU.subtract).then_inc(S["m_lo"], 1)
                        split("ssd_out", i, x)
            loop(dve, "ssd_out", ssd_out_body)

            def add_residual(phase, i, k, x, nb):
                dve.wait_ge(S["slab_used"], slab_no(phase, i, x) + 1)
                banks = PLAN[phase]["jobs"][k][1]
                for t in range(TT):
                    dst = x_sb[:, t, bass.ds(nb * 512, 512)]
                    tt(dst, dst, ps[banks[t]][:, :], ALU.add).then_inc(bank_free[banks[t]], 1)

            def x2_side(nb):
                for k in range(4 * nb, 4 * nb + 4):
                    dve.wait_ge(S["h2_hi"], 2 * (k // 2) + 2)
                    stt(out=act32[:, k, T:2 * T], in0=ps[4 + (k // 2) % 4][:, (k % 2) * T:(k % 2 + 1) * T],
                        scalar=chan[:, V_N2 + k:V_N2 + k + 1], in1=act32[:, k, 0:T].bitcast(F32), op0=ALU.mult,
                        op1=ALU.subtract).then_inc(S["h2_lo"], 1)
            dve.wait_ge(S["x_loaded"], 32)
            dve.wait_ge(S["x_again"], 32)
            for n in range(4):
                for x in range(8 * n, 8 * n + 8):
                    if n and x == 8 * n + 1:
                        x2_side(n - 1)
                    if x == 8 * n + 7:
                        add_residual("out", 0, n, x, n)
                    split("out", 0, x)

            def end_of_norm():
                x2_side(3)
                dve.wait_ge(S["sq2_ready"], 8)
                v.tensor_reduce(small[:, 10:12], ssq[:, :, :], AX, ALU.add).then_inc(S["ssq2_sum"], 1)
                dve.wait_ge(S["std2"], 1)
                v.reciprocal(small[:, 14:16], small[:, 12:14]).then_inc(S["rstd2"], 1)
                dve.wait_ge(S["rstd2"], 1)
                for t in range(TT):
                    last = v.tensor_scalar(diag[:, t, :], ident, small[:, 14 + t:15 + t], None, ALU.mult)
                last.then_inc(S["diag_ready"], 1)

            def up(phase, n0, dst, ft0):
                def body(i):
                    for k in range(2):
                        for x in range(4 * k, 4 * k + 4):
                            if phase == "up_a0" and isinstance(i, int) and i == 0 and x == 0:
                                end_of_norm()
                            if phase == "up_a0" and isinstance(i, int) and i == 0 and x == 2:
                                dve.wait_ge(S["rr_done"], 1)
                                v.tensor_copy(rrow, ps[4][:, 0:T]).then_inc(S["rr_ready"], 1)
                            if x == 4 * k + 3:
                                bank = PLAN[phase]["jobs"][k][1][0]
                                n = 2 * i + (n0 + k)
                                t = f2(tu[:, k, :])
                                if phase == "up_a0":
                                    dve.wait_ge(S["rr_ready"], 1)
                                dve.wait_ge(S["slab_used"], slab_no(phase, i, x) + 1)
                                stt(out=t, in0=f2(ps[bank][:, :]), scalar=0.0,
                                    in1=rrow.unsqueeze(1).to_broadcast([P, 2, T]), op0=ALU.max, op1=ALU.mult) \
                                    .then_inc(bank_free[bank], 1)
                                dve.wait_ge(bank_free[bank], bank_use(phase, i, k, bank) + 1)
                                dve.wait_ge(S["u_hi"], n + 1)
                                tt(t, t, t, ALU.mult).then_inc(S["u_sq"], 1)
                                dve.wait_ge(S["u_sq"], n + 1)
                                ft = bass.ds(4 * i + (ft0 + 2 * k), 2)
                                tt(dst[:, ft, T:2 * T], t, dst[:, ft, 0:T].bitcast(F32), ALU.subtract) \
                                    .then_inc(S["u_lo"], 1)
                            split(phase, i, x)
                loop(dve, phase, body, peel=1 if phase == "up_a0" else 0)

            def down_a_body(i):
                for k in range(2):
                    for x in range(16 * k, 16 * k + 16):
                        if x == 16 * k + 15:
                            add_residual("down_a", i, k, x, 2 * i + k)
                        split("down_a", i, x)
            up("up_a0", 0, act32, 16)
            up("up_a1", 8, act16, 0)
            loop(dve, "down_a", down_a_body)
            up("up_b0", 16, act32, 16)
            up("up_b1", 24, act16, 0)
            dve.wait_ge(S["wf_loaded"], 16)
            for phase, nb0 in (("down_b", 0), ("down_end", 2)):
                for k in range(2):
                    nb = nb0 + k
                    for x in range(16 * k, 16 * k + 16):
                        if x == 16 * k + 15:
                            add_residual(phase, 0, k, x, nb)
                        split(phase, 0, x)
                    cols = slice(nb * 512, (nb + 1) * 512)
                    if nb < 3:
                        for t in range(TT):
                            dve.wait_ge(S["sq3_ready"], 2 * nb + t + 1)
                            tt(x_sb[:, t, cols], x_sb[:, t, cols], wf[:, cols], ALU.mult).then_inc(S["x3_w"], 1)
                    else:
                        bank = PLAN[phase]["jobs"][k][1][1]
                        dve.wait_ge(bank_free[bank], bank_use(phase, 0, k, bank) + 1)
                        stt(out=junk[:, 1536:2048], in0=x_sb[:, 1, cols], scalar=1.0, in1=x_sb[:, 1, cols],
                            op0=ALU.mult, op1=ALU.mult, accum_out=ssq[:, 1, 3:4]).then_inc(S["sq3_dve"], 1)
                        dve.wait_ge(S["sq3_ready"], 7)
                        dve.wait_ge(S["sq3_dve"], 1)
            v.tensor_reduce(small[:, 18:20], ssq[:, :, :], AX, ALU.add).then_inc(S["ssq3_sum"], 1)
            for t in range(TT):
                tt(x_sb[:, t, cols], x_sb[:, t, cols], wf[:, cols], ALU.mult).then_inc(S["x3_w"], 1)
            dve.wait_ge(S["std3"], 1)
            v.reciprocal(small[:, 22:24], small[:, 20:22]).then_inc(S["rstd3"], 1)
            dve.wait_ge(S["x3_w"], 8)
            dve.wait_ge(S["rstd3"], 1)
            for n in range(4):
                cols = slice(n * 512, (n + 1) * 512)
                v.tensor_scalar(x_sb[:, 1, cols], x_sb[:, 1, cols], small[:, 23:24], None, ALU.mult) \
                    .then_inc(S["out_dve"], 1)

        @block.gpsimd
        def _(pool):
            g_ = nc.gpsimd
            ks_flat = scr[:, 0:2048].rearrange("p (j t) -> p j t", j=N_KV)
            pool.wait_ge(bank_free[0], 1)
            pool.wait_ge(bank_free[1], 1)
            pool.wait_ge(bank_free[2], 1)
            pool.wait_ge(bank_free[3], 1)

            def kv(j):
                first = isinstance(j, int) and j == 0
                if not first:
                    pool.wait_ge(S["scores_done"], j)
                g_.tensor_copy(kc.unsqueeze(1), ks_flat[:, bass.ds(j, 1), :]).then_inc(S["kc_ready"], 1)
                if not first:
                    pool.wait_ge(S["pv_done"], j)
                g_.tensor_copy(vc[:, :, :], vs[:, :, bass.ds(j * HD, HD)]).then_inc(S["vc_ready"], 1)
            kv(0)
            with pool.Fori(1, N_KV) as j:
                kv(j)

            def ssd(g):
                first = isinstance(g, int) and g == 0
                if first:
                    pool.wait_ge(S["pad_zero"], 1)
                    pool.wait_ge(S["attn_lo"], N_KV)
                else:
                    pool.wait_ge(S["y_ready"], 2 * g)
                for t in range(TT):
                    last = g_.tensor_tensor(rs[:, t, :].rearrange("p (h l) -> p h l", h=HPG),
                                            a_t[:, t, bass.ds(g * HPG, HPG)].unsqueeze(2).to_broadcast([P, HPG, 64]),
                                            tri.unsqueeze(1).to_broadcast([P, HPG, 64]), ALU.mult)
                last.then_inc(S["rs_ready"], 1)
                pool.wait_ge(S["xs_used"], 4 * g + 4)
                for t in range(TT):
                    last = g_.tensor_tensor(xdec[:, t, :].rearrange("p (h l) -> p h l", h=HPG),
                                            xdt[:, t, :].rearrange("p (h l) -> p h l", h=HPG),
                                            dec_t[:, t, bass.ds(g * HPG, HPG)].unsqueeze(2).to_broadcast([P, HPG, 64]),
                                            ALU.mult)
                last.then_inc(S["xdec_ready"], 1)
            ssd(0)
            with pool.Fori(1, GROUPS) as g:
                ssd(g)


def kernel(**inputs):
    import numpy as _np
    import concourse.bacc as _bacc
    from concourse.bass_utils import run_bass_kernel_spmd as _run

    def columns(v):
        return _np.asarray(v).reshape(-1, P).T

    taps = _np.asarray(inputs["conv_w"]).reshape(CONV_K, -1, P).transpose(2, 1, 0).reshape(P, -1)
    channel_table = _np.ascontiguousarray(_np.concatenate(
        [columns(inputs["norm1_w"]), columns(inputs["gate_bias"]), taps, columns(inputs["conv_b"]),
         columns(inputs["ssd_norm_w"]), columns(inputs["norm2_w"])], axis=1))
    k, m = _np.arange(P)[:, None], _np.arange(P)[None, :]
    same = (k // CHUNK == m // CHUNK)
    table = _np.zeros((P, C_COLS + NEG_COLS), _np.float32)
    table[:, C_ID:C_ID + P] = (k == m)
    table[:, C_TRI:C_TRI + CHUNK] = (k % CHUNK <= m[:, :CHUNK])
    table[:, C_CUM:C_CUM + P] = same & (k <= m)
    table[:, C_BLK:C_BLK + P] = same
    for t, c in ((0, C_NEG), (1, C_NEG + P)):
        q, s = _np.arange(P)[:, None] + t * P, _np.arange((t + 1) * P)[None, :]
        ahead = q // CHUNK - s // CHUNK
        table[:, c:c + (t + 1) * P] = _np.where((ahead == 0) | (ahead == 1), -_np.abs(q - s), -1e30)
    table[:, C_SLOPE:C_SLOPE + N_HEADS] = 8.0 * 2.0 ** (-8.0 * _np.arange(1, N_HEADS + 1) / N_HEADS)
    table[:, C_EPS], table[:, C_EPS4] = EPS, 4 * EPS
    table[:, C_ONE:C_ONE + P] = 1.0

    nc = _bacc.Bacc("TRN2", target_bir_lowering=False, num_devices=1)
    arrays, args = {}, []
    for name in ["x", "w_in", "w_o_attn", "w_o_ssd", "w_out", "w_up", "w_down", "attn_sinks", "dt_bias", "a_log",
                 "d_skip", "norm_final_w"]:
        arrays[f"in_{name}"] = _np.ascontiguousarray(inputs[name])
    arrays["channel_table"], arrays["shape_table"] = channel_table, table
    for name, a in arrays.items():
        args.append(nc.dram_tensor(name, a.shape, mybir.dt.from_np(a.dtype), kind="ExternalInput").ap())
    args.append(nc.dram_tensor("out", (1, T, D), F32, kind="ExternalOutput").ap())
    hybrid_block(nc, *args)
    r = _run(nc, [arrays], core_ids=[0])
    return r.results[0]["out"]
```

```python
from contextlib import ExitStack

import concourse.bass as bass
from concourse import mybir

F32 = mybir.dt.float32
F32R = mybir.dt.float32r
ALU = mybir.AluOpType
ACT = mybir.ActivationFunctionType
AX = mybir.AxisListType.X

P = 128
T = 256
TT = T // P
D = 2048
KD = D // P
CHUNK = 64
N_CHUNKS = T // CHUNK
HD = 64
N_HEADS, N_KV = 32, 8
GQ = N_HEADS // N_KV
D_INNER = 2 * D
GROUPS = 8
HPG = D_INNER // HD // GROUPS
GW = D_INNER // GROUPS
SSD_HEADS = GROUPS * HPG
STATE = 128
CONV_K = 4
D_FF = 4 * D
EPS = 1e-5

Q0 = 0
K0 = Q0 + N_HEADS * HD
V0 = K0 + N_KV * HD
Z0 = V0 + N_KV * HD
X0 = Z0 + D_INNER
B0 = X0 + D_INNER
C0 = B0 + GROUPS * STATE
DT0 = C0 + GROUPS * STATE
G0 = DT0 + SSD_HEADS

PT_BANKS = (0, 1, 3)
WARM_UP = 5
RING = 4
SLAB = 1024

V_N1, V_GB, V_CW, V_CB, V_SN, V_N2 = 0, 16, 48, 240, 288, 320
V_COLS = 336
C_ID, C_TRI, C_CUM, C_BLK, C_SLOPE, C_EPS, C_EPS4, C_ONE = 0, 128, 192, 320, 448, 480, 481, 482
C_COLS = 610
C_NEG, NEG_COLS = C_COLS, 3 * P

PHASES = [
    ("kv", 1, [(4, [0]), (4, [1]), (8, [2, 3]), (4, [0, 1])]),
    ("q", N_KV, [(4, [2])]),
    ("gate_a", 4, [(4, [2]), (4, [3])]),
    ("attn_out", 4, [(4, [2]), (4, [3])]),
    ("first_group", 1, [(4, [0]), (4, [1])]),
    ("group", GROUPS - 1, [(4, [0]), (8, [2, 3]), (4, [0]), (4, [1])]),
    ("last_group", 1, [(4, [0]), (8, [2, 3])]),
    ("gate_s", 4, [(4, [0]), (4, [1])]),
    ("ssd_out", 4, [(8, [2]), (8, [3])]),
    ("out", 1, [(8, [0, 1]), (8, [2, 3]), (8, [0, 1]), (8, [2, 3])]),
    ("up_a0", 4, [(4, [0]), (4, [1])]),
    ("up_a1", 4, [(4, [0]), (4, [1])]),
    ("down_a", 2, [(16, [2, 3]), (16, [0, 1])]),
    ("up_b0", 4, [(4, [2]), (4, [3])]),
    ("up_b1", 4, [(4, [2]), (4, [3])]),
    ("down_b", 1, [(16, [0, 1]), (16, [2, 3])]),
    ("down_end", 1, [(16, [0, 1]), (16, [2, 3])]),
]


def make_plan():
    plan, slab, uses = {}, 0, [0] * 4
    for name, iters, jobs in PHASES:
        per = [sum(b in banks for _, banks in jobs) for b in range(4)]
        plan[name] = dict(iters=iters, jobs=jobs, slab0=slab, slabs=sum(n for n, _ in jobs), use0=list(uses), uses=per)
        slab += iters * plan[name]["slabs"]
        uses = [u + iters * p for u, p in zip(uses, per)]
    return plan, slab


PLAN, N_SLABS = make_plan()
DT_SLAB = PLAN["kv"]["slab0"] + 16


def slab_no(phase, i, x):
    return PLAN[phase]["slab0"] + i * PLAN[phase]["slabs"] + x


def slot_round(phase, i, x):
    return PLAN[phase]["slab0"] // RING + i * (PLAN[phase]["slabs"] // RING) + x // RING


def bank_use(phase, i, job, bank):
    p = PLAN[phase]
    return p["use0"][bank] + i * p["uses"][bank] + sum(bank in banks for _, banks in p["jobs"][:job])


def job_end(phase, job):
    return sum(n for n, _ in PLAN[phase]["jobs"][: job + 1]) - 1


def loop(eng, phase, body, peel=0):
    n = PLAN[phase]["iters"]
    for i in range(peel):
        body(i)
    if n - peel == 1:
        body(peel)
    elif n > peel:
        with eng.Fori(peel, n) as i:
            body(i)


def is_step(i, n):
    return isinstance(i, int) and i == n


def out_of(i, low, high):
    return isinstance(i, int) and not low <= i < high


def hybrid_block(nc, x, w_in, w_o_attn, w_o_ssd, w_out, w_up, w_down, sinks, dt_bias, a_log, d_skip, norm_final_w,
                 channel_table, shape_table, acs_dram, out):
    with ExitStack() as ctx:
        def sb(name, shape, dt=F32):
            return ctx.enter_context(nc.sbuf_tensor(name, shape, dt))

        def sem(name):
            return ctx.enter_context(nc.semaphore(name))

        ps = [ctx.enter_context(nc.psum_tensor(f"bank{b}", [P, 512], F32)) for b in range(8)]

        raw = sb("raw", [P, RING, SLAB])
        w_hi = sb("w_hi", [P, RING, SLAB], F32R)
        w_lo = sb("w_lo", [P, RING, SLAB], F32R)
        act16 = sb("act16", [P, 16, 2 * T], F32R)
        act32 = sb("act32", [P, 32, 2 * T], F32R)
        xg = sb("xg", [P, 4096])
        ga = sb("ga", [P, 4096])
        b2_last = sb("b2_last", [P, 2 * STATE], F32R)
        scr = sb("scr", [P, 5784])
        chan = sb("chan", [P, V_COLS])
        const = sb("const", [P, C_COLS])
        sink_b = sb("sink_b", [P, N_HEADS])
        dskip_b = sb("dskip_b", [P, SSD_HEADS])
        dt_t = sb("dt_t", [P, TT, SSD_HEADS])
        a_t = sb("a_t", [P, TT, SSD_HEADS])
        acs_t = sb("acs_t", [P, TT, SSD_HEADS])
        ea_t = sb("ea_t", [P, TT, SSD_HEADS])
        dec_t = sb("dec_t", [P, TT, SSD_HEADS])
        cdec = sb("cdec", [P, N_CHUNKS, SSD_HEADS])
        ssq = sb("ssq", [P, TT, 4])
        small = sb("small", [P, 32])

        ident = const[:, C_ID:C_ID + P]
        tri = const[:, C_TRI:C_TRI + CHUNK]
        cum = const[:, C_CUM:C_CUM + P]
        blk = const[:, C_BLK:C_BLK + P]
        ones = const[:, C_ONE:C_ONE + P]
        neg_all = scr[:, 5184:5184 + NEG_COLS]
        negd = [neg_all[:, 0:P], neg_all[:, P:NEG_COLS]]
        x_sb = xg[:, :].rearrange("p (t n) -> p t n", t=TT)
        gs = xg[:, :].rearrange("p (f n) -> p f n", f=KD)
        ga_f = ga[:, :].rearrange("p (f n) -> p f n", f=KD)

        ks = scr[:, 0:2048].rearrange("p (j c t) -> p j c t", j=4, c=2)
        vs = scr[:, 2048:3072].rearrange("p (t n) -> p t n", t=TT)
        qt = scr[:, 3072:3584].rearrange("p (f t) -> p f t", f=2)
        vc = scr[:, 3840:3968].rearrange("p (t n) -> p t n", t=TT)
        p0 = scr[:, 3968:4480].rearrange("p (g k) -> p g k", g=GQ)
        sm = scr[:, 4480:4544]
        mx, mm_, negm, es, rsum, den, rden = [sm[:, 8 * n:8 * n + 8] for n in range(7)]
        dt_tmp = scr[:, 4544:4544 + 5 * 128]
        p1 = xg[:, 0:1024].rearrange("p (g k) -> p g k", g=GQ)
        pt = xg[:, 1024:2560].rearrange("p (b n) -> p b n", b=3)
        q2 = act32[:, 16:18, :].rearrange("p f (c t) -> p f c t", c=2)
        kc = act32[:, 18, :].rearrange("p (s t) -> p s t", s=2)
        upad = scr[:, 0:1560].rearrange("p (f n) -> p f n", f=6)
        cv = scr[:, 1560:3096].rearrange("p (f n) -> p f n", f=6)
        th = scr[:, 3096:4632].rearrange("p (f n) -> p f n", f=6)
        prev = scr[:, 3096:4632].rearrange("p (c n) -> p c n", c=3)
        mt = scr[:, 4632:5656].rearrange("p (t n) -> p t n", t=TT)
        cbm = scr[:, 5656:5784].rearrange("p (t l) -> p t l", t=TT)
        x2 = act32[:, 28:31, :]
        b2_of = [act32[:, 31, 0:2 * P], act32[:, 31, 2 * P:4 * P], b2_last]
        b2 = [ap.rearrange("p (s n) -> p s n", s=2) for ap in b2_of]
        acs_rows = xg[:, 0:1024].rearrange("p (t n) -> p t n", t=TT)
        sz = acs_rows
        acs_h = ga[0:SSD_HEADS, 0:T]
        yb = xg[:, 1024:2048].rearrange("p (t n) -> p t n", t=TT)
        xdt = xg[:, 2048:3072].rearrange("p (t n) -> p t n", t=TT)
        xd = xg[:, 3072:4096].rearrange("p (t n) -> p t n", t=TT)
        xdec = scr[:, 1560:2584].rearrange("p (t n) -> p t n", t=TT)
        tu = scr[:, 0:1024].rearrange("p (b n) -> p b n", b=2)
        rrow = scr[:, 1024:1280]
        diag = scr[:, 1280:1536].rearrange("p (t n) -> p t n", t=TT)
        junk = scr[:, 2048:4096]
        wf = ga[:, 0:D]

        names = """
            x_loaded x1_left x1_right tables_loaded rows_loaded wf_loaded acs_stored rows_landed stored
            hi_ready lo_ready slab_used
            one_set ssq1_act ssq1_part ssq1_dve std1_ready rstd1_ready xn_act xn_dve xt_done h_hi h_lo half_ready
            dt_v dt_e a_ready neg_a cums_done acs_ready dec_in dec_ready acs_tr acs_copied
            kc_ready vc_ready q_hi q_lo kc_hi scores_done shift_ready exp_done probs_ready pt_done pt_act pt_dve
            pv_done attn_hi attn_lo
            pad_zero conv_bc conv_xa conv_xb th_bc th_x silu_bc silu_x cb_done b_hi b_lo cbm_ready seg_out seg_min
            seg_exp mt_ready xt_tr xs_used xdec_ready x_hi x_lo st_done prev1 prev_tmp prev2 prev3 yd0_done yd1_done y_part
            tz_ready y_tmp y_ready ssq_g std_g rstd_g yn_ready yt_done y_hi y_lo
            m_sum m_hi m_lo
            x2t_done h2_hi h2_lo sq2_ready ssq2_sum std2 rstd2 diag_ready rr_done rr_ready
            u_hi u_sq u_lo
            sq3_ready sq3_dve x3_w ssq3_sum std3 rstd3 out_act out_dve""".split()
        S = {n: sem(n) for n in names}
        raw_landed = [sem(f"raw_landed{s}") for s in range(RING)]
        bank_free = [sem(f"bank_free{b}") for b in range(4)]

        class Chain:
            def __init__(self, eng, s):
                self.eng, self.s, self.base, self.n = eng, s, 0, 0

            def at(self, start):
                self.base, self.n = start, 0

            def link(self, ins):
                self.n += 1
                ins.then_inc(self.s, 1)
                self.eng.wait_ge(self.s, self.base + self.n)

        def width_of(n):
            narrow = isinstance(n, int) and DT_SLAB <= n + RING < DT_SLAB + 4
            return 4 * SSD_HEADS if narrow else SLAB

        def raw_count(slot, phase, i, x):
            return (slot_round(phase, i, x) + 2) * 16

        block = ctx.enter_context(nc.Block())

        def feature_src(w, row_tile, col, width=256, kt=4):
            v = w.rearrange("(k p) n -> p k n", p=P)
            return v[:, row_tile:row_tile + kt, bass.ds(col, width)]

        @block.sync
        def _(sp):
            sp.dma_start(x_sb[:, 0, :], x[0, 0:P, :]).then_inc(S["x_loaded"], 16)
            for n in range(2):
                cols = slice(n * D // 2, (n + 1) * D // 2)
                sp.dma_start(x_sb[:, 1, cols], x[0, P:T, cols]).then_inc(S["x1_left" if n == 0 else "x1_right"], 16)

            def load(phase, i, xs, src, dst=None):
                n = slab_no(phase, i, xs)
                slot = xs % RING
                if not (isinstance(n, int) and n < RING):
                    sp.wait_ge(S["lo_ready"], n - RING + 1)
                dst = raw[:, slot, :] if dst is None else dst
                sp.dma_start(dst, src).then_inc(raw_landed[slot], 16)

            def feature_job(phase, i, x0, w, col, rows=KD):
                for s in range(rows // 4):
                    load(phase, i, x0 + s, feature_src(w, 4 * s, col),
                         raw[:, (x0 + s) % RING, :].rearrange("p (k n) -> p k n", k=4))

            def token_job(phase, i, x0, w, col, rows=KD, row0=0):
                for s in range(rows // 2):
                    load(phase, i, x0 + s, feature_src(w, row0 + 2 * s, col, 512, 2),
                         raw[:, (x0 + s) % RING, :].rearrange("p (k n) -> p k n", k=2))

            def bc_job(phase, i, x0, g):
                for s in range(4):
                    load(phase, i, x0 + s, feature_src(w_in, 8 * (s % 2), g * STATE + (B0 if s < 2 else C0), STATE, 8),
                         raw[:, (x0 + s) % RING, :].rearrange("p (k n) -> p k n", k=8))

            feature_job("kv", 0, 0, w_in, K0)
            feature_job("kv", 0, 4, w_in, K0 + 256)
            token_job("kv", 0, 8, w_in, V0)
            for s in range(4):
                load("kv", 0, 16 + s, feature_src(w_in, 4 * s, DT0, SSD_HEADS),
                     raw[:, s, 0:4 * SSD_HEADS].rearrange("p (k n) -> p k n", k=4))
            loop(sp, "q", lambda i: feature_job("q", i, 0, w_in, i * 256 + Q0))

            def gate(phase, col):
                def body(i):
                    for k in range(2):
                        feature_job(phase, i, 4 * k, w_in, i * 512 + (col + 256 * k))
                loop(sp, phase, body)

            def rows_out(phase, w, rows, col=0):
                def body(i):
                    for k in range(2):
                        feature_job(phase, i, (rows // 4) * k, w, i * 512 + (col + 256 * k), rows)
                loop(sp, phase, body)

            gate("gate_a", G0)
            rows_out("attn_out", w_o_attn, KD)
            bc_job("first_group", 0, 0, 0)
            feature_job("first_group", 0, 4, w_in, X0)

            def group(phase, g, i, last=False):
                feature_job(phase, i, 0, w_in, g * GW + (X0 + 256))
                token_job(phase, i, 4, w_in, g * GW + Z0)
                if not last:
                    bc_job(phase, i, 12, g + 1)
                    feature_job(phase, i, 16, w_in, g * GW + (X0 + GW))
            loop(sp, "group", lambda i: group("group", i, i))
            group("last_group", GROUPS - 1, 0, last=True)
            gate("gate_s", G0 + D)
            rows_out("ssd_out", w_o_ssd, 2 * KD)
            for n in range(4):
                token_job("out", 0, 8 * n, w_out, 512 * n)
                if n == 0:
                    sp.wait_ge(S["m_sum"], 8)
                    for t in range(TT):
                        sp.dma_start(x_sb[:, t, :], x[0, t * P:(t + 1) * P, :]) \
                            .then_inc(S["x_loaded" if t == 0 else "x1_left"], 16)
                    sp.wait_ge(S["m_lo"], 8)
                    sp.dma_start(wf, norm_final_w.partition_broadcast(P)).then_inc(S["wf_loaded"], 16)

            def down(phase, i, half, nb0):
                for k in range(2):
                    token_job(phase, i, 16 * k, w_down, i * 1024 + (512 * k + 512 * nb0), 2 * KD, half * 2 * KD)

            for half, name in enumerate("ab"):
                for part in range(2):
                    rows_out(f"up_{name}{part}", w_up, KD, half * (D_FF // 2) + part * D)
                if half == 0:
                    loop(sp, "down_a", lambda i: down("down_a", i, 0, 0))
                else:
                    down("down_b", 0, 1, 0)
                    down("down_end", 0, 1, 2)
            for n in range(4):
                for t, name in ((0, "out_act"), (1, "out_dve")):
                    cols = slice(n * 512, (n + 1) * 512)
                    sp.wait_ge(S[name], n + 1)
                    sp.dma_start(out[0, t * P:(t + 1) * P, cols], x_sb[:, t, cols]).then_inc(S["stored"], 16)
            sp.wait_ge(S["stored"], 8 * 16)

        @block.tensor
        def _(pe):
            mm = nc.tensor.matmul

            def split3(out_ap, a_hi, a_lo, b_hi, b_lo, start, stop):
                mm(out_ap, a_hi, b_hi, start=start, stop=False, skip_group_check=True)
                mm(out_ap, a_hi, b_lo, start=False, stop=False, skip_group_check=True)
                return mm(out_ap, a_lo, b_hi, start=False, stop=stop, skip_group_check=True)

            def bank_ready(phase, i, job, bank):
                u = bank_use(phase, i, job, bank)
                if not (isinstance(u, int) and u == 0):
                    pe.wait_ge(bank_free[bank], u)

            def feature_job(phase, i, job, acts, side=None, bc=False, before=None):
                n, (bank,) = PLAN[phase]["jobs"][job]
                x0 = job_end(phase, job) - n + 1
                bank_ready(phase, i, job, bank)
                for s in range(n):
                    slot = (x0 + s) % RING
                    if before:
                        before(s)
                    pe.wait_ge(S["lo_ready"], slab_no(phase, i, x0 + s) + 1)
                    for c in range(8):
                        col, f, k = (c, s // 2, 8 * (s % 2) + c) if bc else (2 * (c % 4) + c // 4, c // 4, 4 * s + c % 4)
                        w = slice(128 * col, 128 * col + 128)
                        a = acts(k)
                        last = split3(ps[bank][:, f * T:(f + 1) * T], w_hi[:, slot, w], w_lo[:, slot, w],
                                      a[:, 0:T], a[:, T:2 * T], start=(s == 0 and c == 0),
                                      stop=(k == (KD if n == 4 else 2 * KD) - 1))
                    last.then_inc(S["slab_used"], 1)
                    if side:
                        side(x0 + s)

            def token_job(phase, i, job, acts, side=None, narrow=False, before=None):
                n, banks = PLAN[phase]["jobs"][job]
                x0 = job_end(phase, job) - n + 1
                kts, width = (4, SSD_HEADS) if narrow else (2, 512)
                for b in banks:
                    bank_ready(phase, i, job, b)
                for s in range(n):
                    slot = (x0 + s) % RING
                    if before:
                        before(s)
                    pe.wait_ge(S["lo_ready"], slab_no(phase, i, x0 + s) + 1)
                    for k in range(kts):
                        c = slice(width * k, width * (k + 1))
                        a = acts(kts * s + k)
                        for t in range(TT):
                            last = split3(ps[banks[t]][:, 0:width], a[:, t * P:(t + 1) * P],
                                          a[:, T + t * P:T + (t + 1) * P], w_hi[:, slot, c], w_lo[:, slot, c],
                                          start=(s == 0 and k == 0), stop=(s == n - 1 and k == kts - 1))
                    last.then_inc(S["slab_used"], 1)
                    if side:
                        side(x0 + s)

            h = lambda k: act16[:, k, :]
            a32 = lambda k: act32[:, k, :]

            def x_t(r):
                pe.wait_ge(S["xn_act"], r // 2 + 1)
                pe.wait_ge(S["xn_dve"], r // 2 + 1)
                if r >= 4:
                    pe.wait_ge(S["h_lo"], 2 * (r - 4) + 2)
                for k in range(2):
                    for t in range(TT):
                        last = nc.tensor.transpose(ps[4 + r % 4][:, (2 * k + t) * P:(2 * k + t + 1) * P],
                                                   x_sb[:, t, (2 * r + k) * P:(2 * r + k + 1) * P], ident)
                last.then_inc(S["xt_done"], 1)
            pe.wait_ge(S["tables_loaded"], 32)
            for _ in range(WARM_UP):
                mm(ps[7][:, 0:P], ident, ident, start=True, stop=True)
            for r in range(4):
                x_t(r)

            def rest_of_x(x):
                if x < 2:
                    x_t(4 + 2 * x)
                    x_t(5 + 2 * x)
            feature_job("kv", 0, 0, h, rest_of_x, before=lambda s: pe.wait_ge(S["h_lo"], 4 * s + 4))
            feature_job("kv", 0, 1, h)
            token_job("kv", 0, 2, h)
            token_job("kv", 0, 3, h, narrow=True)

            def scores(j):
                pe.wait_ge(S["q_lo"], j + 1)
                pe.wait_ge(S["kc_ready"], j + 1)
                for g in range(GQ):
                    for t in range(TT):
                        if t == 0:
                            o, keys, first = ps[4][:, g * P:(g + 1) * P], P, g == 0
                        else:
                            o, keys, first = ps[5 + g % 2][:, (g // 2) * T:(g // 2 + 1) * T], T, g < 2
                        for part in range(2):
                            last = mm(o, q2[:, g // 2, g % 2, t * P:(t + 1) * P], kc[:, part, 0:keys],
                                      start=(first and part == 0), stop=(part == 1), skip_group_check=True)
                last.then_inc(S["scores_done"], 1)

            def probs_t(j):
                pe.wait_ge(S["probs_ready"], j + 1)
                for b in range(3):
                    if b == 2 and is_step(j, N_KV - 1):
                        pe.wait_ge(bank_free[3], bank_use("gate_a", 0, 1, 3) + 1)
                    for g in range(GQ):
                        src = p0[:, g, :] if b == 0 else p1[:, g, (b - 1) * P:b * P]
                        last = nc.tensor.transpose(ps[PT_BANKS[b]][:, g * P:(g + 1) * P], src, ident)
                last.then_inc(S["pt_done"], 1)

            def values(j):
                pe.wait_ge(S["pt_act"], j + 1)
                pe.wait_ge(S["pt_dve"], j + 1)
                pe.wait_ge(S["vc_ready"], j + 1)
                if not is_step(j, 0):
                    pe.wait_ge(S["attn_lo"], j)
                for g in range(GQ):
                    half = slice(64 * (g % 2), 64 * (g % 2) + 64)
                    for t in range(TT):
                        o = ps[7][half, (g // 2) * T + t * P:(g // 2) * T + (t + 1) * P]
                        for k in range(t + 1):
                            last = mm(o, vc[:, k, :], pt[:, t + k, g * P:(g + 1) * P],
                                      start=(g < 2 and t == 0), stop=(k == t), skip_group_check=True)
                last.then_inc(S["pv_done"], 1)

            def attention(i, x):
                if x == 3:
                    if not out_of(i, 2, N_KV + 2):
                        probs_t(i - 2)
                    if not out_of(i, 1, N_KV + 1):
                        scores(i - 1)
                    if not out_of(i, 2, N_KV + 2):
                        values(i - 2)

            def cumsums():
                pe.wait_ge(S["a_ready"], 1)
                for t in range(TT):
                    mm(ps[7][:, t * 64:(t + 1) * 64], cum, a_t[:, t, :], start=True, stop=True)
                    mm(ps[7][:, 128 + t * 64:192 + t * 64], blk, a_t[:, t, :], start=True, stop=True)
                for c in (0, 2, 1, 3):
                    rows = slice(64 * (c % 2), 64 * (c % 2) + 64)
                    last = mm(ps[5 + c % 2][:, (c // 2) * 64:(c // 2 + 1) * 64], ones[rows, :], a_t[rows, c // 2, :],
                              start=True, stop=True)
                last.then_inc(S["cums_done"], 1)

            def q_body(i):
                def side(x):
                    if is_step(i, 0) and x == 3:
                        cumsums()
                    if is_step(i, 1) and x == 1:
                        pe.wait_ge(S["acs_ready"], 1)
                        for t in range(TT):
                            last = nc.tensor.transpose(ps[4][0:SSD_HEADS, t * P:(t + 1) * P], acs_t[:, t, :], ident)
                        last.then_inc(S["acs_tr"], 1)
                    if is_step(i, 1) and x == 3:
                        pe.wait_ge(S["acs_copied"], 1)
                        pe.wait_ge(S["dec_ready"], 2)
                        for b in PT_BANKS:
                            pe.wait_ge(bank_free[b], PLAN["q"]["use0"][b])
                    attention(i, x)
                feature_job("q", i, 0, h, side)
            loop(pe, "q", q_body, peel=2)

            def gate_a_body(i):
                for k in range(2):
                    side = (lambda x, k=k: attention(N_KV + k, x - 4 * k)) if is_step(i, 0) else None
                    feature_job("gate_a", i, k, h, side)
            loop(pe, "gate_a", gate_a_body, peel=1)

            pe.wait_ge(S["attn_lo"], N_KV)

            def two_jobs(phase, acts):
                def body(i):
                    for k in range(2):
                        feature_job(phase, i, k, acts)
                return body

            def last_parts(name, first, last, slab):
                def before(s):
                    if s in (0, slab):
                        pe.wait_ge(S[name], first if s == 0 else last)
                return before
            loop(pe, "attn_out", two_jobs("attn_out", a32))

            feature_job("first_group", 0, 0, h, bc=True)
            feature_job("first_group", 0, 1, h)

            def ssd(g, x):
                first = is_step(g, 0)
                if x == 1:
                    pe.wait_ge(S["silu_bc"], g + 1)
                    if not first:
                        pe.wait_ge(S["y_lo"], g * 4)
                    for c in range(N_CHUNKS):
                        rows = slice(64 * (c % 2), 64 * (c % 2) + 64)
                        tok = slice(c * CHUNK, (c + 1) * CHUNK)
                        mm(ps[6][rows, (c // 2) * 64:(c // 2 + 1) * 64], cv[:, 4, tok], cv[:, 5, tok], start=True, stop=True)
                    for t in range(TT):
                        last = nc.tensor.transpose(ps[6][:, (1 + t) * P:(2 + t) * P], cv[:, 4, t * P:(t + 1) * P], ident)
                    last.then_inc(S["cb_done"], 1)
                if x == 7:
                    pe.wait_ge(S["silu_x"], g + 1)
                    pe.wait_ge(S["cbm_ready"], g + 1)
                    pe.wait_ge(S["b_lo"], g + 1)
                    for t in range(TT):
                        for f in range(4):
                            last = nc.tensor.transpose(ps[7 - t][:, f * P:(f + 1) * P], cv[:, f, t * P:(t + 1) * P], ident)
                    last.then_inc(S["xt_tr"], 1)
                if x == 11:
                    pe.wait_ge(S["xs_used"], 4 * g + 4)
                    pe.wait_ge(S["mt_ready"], 2 * g + 2)
                    pe.wait_ge(S["x_lo"], g + 1)
                    for c in range(3):
                        mm(ps[4 + c][:, :], b2[c][:, 0, :], x2[:, c, :], start=True, stop=False, skip_group_check=True)
                        last = mm(ps[4 + c][:, :], b2[c][:, 1, :], x2[:, c, :], start=False, stop=True,
                                  skip_group_check=True)
                    last.then_inc(S["st_done"], 1)
                    y_diag(0)
                if x == 13:
                    pe.wait_ge(S["prev3"], g + 1)
                    for c in range(1, N_CHUNKS):
                        rows = slice(64 * (c % 2), 64 * (c % 2) + 64)
                        mm(ps[5 + c // 2][rows, :], cv[:, 5, c * CHUNK:(c + 1) * CHUNK], prev[:, c - 1, :],
                                  start=True, stop=True)
                    y_diag(1)
                if x == 19:
                    pe.wait_ge(S["yn_ready"], 2 * g + 2)
                    for f in range(4):
                        for t in range(TT):
                            last = nc.tensor.transpose(ps[6 + f // 2][:, (f % 2) * T + t * P:(f % 2) * T + (t + 1) * P],
                                                       yb[:, t, f * P:(f + 1) * P], ident)
                    last.then_inc(S["yt_done"], 1)

            def y_diag(t):
                for r in range(HPG):
                    cols = slice(64 * r, 64 * r + 64)
                    for c in (2 * t, 2 * t + 1):
                        rows = slice(64 * (c % 2), 64 * (c % 2) + 64)
                        last = mm(ps[7 if t == 0 else 4][rows, cols], mt[rows, t, cols], xdt[rows, t, cols],
                                  start=True, stop=True)
                last.then_inc(S["yd0_done" if t == 0 else "yd1_done"], 1)

            def group(phase, g, i, last=False):
                side = lambda x: ssd(g, x)
                feature_job(phase, i, 0, h, side)
                token_job(phase, i, 1, h, side)
                if not last:
                    feature_job(phase, i, 2, h, side, bc=True)
                    feature_job(phase, i, 3, h, side)
            loop(pe, "group", lambda i: group("group", i, i))
            group("last_group", GROUPS - 1, 0, last=True)

            def gate_s_body(i):
                side = (lambda x: ssd(GROUPS - 1, x + 12)) if is_step(i, 0) else None
                for k in range(2):
                    feature_job("gate_s", i, k, h, side)
            loop(pe, "gate_s", gate_s_body, peel=1)

            pe.wait_ge(S["y_lo"], 4 * GROUPS)
            loop(pe, "ssd_out", two_jobs("ssd_out", a32))

            def x2_t(nb):
                for b in PLAN["out"]["jobs"][nb][1]:
                    pe.wait_ge(bank_free[b], bank_use("out", 0, nb, b) + 1)
                for q in range(2):
                    r = 2 * nb + q
                    if r >= 4:
                        pe.wait_ge(S["h2_lo"], 2 * (r - 4) + 2)
                    for k in range(2):
                        for t in range(TT):
                            last = nc.tensor.transpose(ps[4 + r % 4][:, (2 * k + t) * P:(2 * k + t + 1) * P],
                                                       x_sb[:, t, (2 * r + k) * P:(2 * r + k + 1) * P], ident)
                    last.then_inc(S["x2t_done"], 1)
            for n in range(4):
                token_job("out", 0, n, h, (lambda x, n=n: x2_t(n - 1) if n and x == 8 * n + 1 else None),
                          before=last_parts("m_lo", 7, 8, 7) if n == 0 else None)

            def end_of_norm(x):
                if x == 0:
                    x2_t(3)
                if x == 2:
                    pe.wait_ge(S["diag_ready"], 1)
                    mm(ps[4][:, 0:T], ones, diag[:, :, :], start=True, stop=True).then_inc(S["rr_done"], 1)

            def up_first(i):
                first = is_step(i, 0)
                feature_job("up_a0", i, 0, a32, end_of_norm if first else None,
                            before=last_parts("h2_lo", 12, 16, 3) if first else None)
                feature_job("up_a0", i, 1, a32)

            def u_act(k):
                return act32[:, 16 + k, :] if k < 16 else act16[:, k - 16, :]

            def down(phase, made=None):
                def body(i):
                    for k in range(2):
                        token_job(phase, i, k, u_act,
                                  before=last_parts("u_lo", made - 1, made, 15) if made and k == 0 else None)
                return body
            loop(pe, "up_a0", up_first, peel=1)
            loop(pe, "up_a1", two_jobs("up_a1", a32))
            loop(pe, "down_a", down("down_a", 16))
            loop(pe, "up_b0", two_jobs("up_b0", a32))
            loop(pe, "up_b1", two_jobs("up_b1", a32))
            down("down_b", 32)(0)
            down("down_end")(0)

        @block.scalar
        def _(act):
            activation = nc.scalar.activation

            def split(phase, i, x):
                n = slab_no(phase, i, x)
                if isinstance(n, int) and n + RING >= N_SLABS:
                    return
                slot = x % RING
                act.wait_ge(S["slab_used"], n + 1)
                act.wait_ge(raw_landed[slot], raw_count(slot, phase, i, x))
                w = width_of(n)
                activation(w_hi[:, slot, 0:w], raw[:, slot, 0:w], ACT.Copy).then_inc(S["hi_ready"], 1)

            act.dma_start(const[:, :], shape_table[:, 0:C_COLS]).then_inc(S["tables_loaded"], 16)
            act.wait_ge(S["one_set"], 1)
            activation(small[:, 25:26], small[:, 26:27], ACT.Sqrt)
            act.dma_start(neg_all, shape_table[:, C_NEG:C_NEG + NEG_COLS]).then_inc(S["rows_loaded"], 16)
            act.dma_start(chan[:, :], channel_table).then_inc(S["tables_loaded"], 16)
            act.dma_start(sink_b[:, :], sinks.partition_broadcast(P)).then_inc(S["rows_loaded"], 16)
            act.dma_start(dskip_b[:, :], d_skip.partition_broadcast(P)).then_inc(S["rows_loaded"], 16)
            act.dma_start(dt_tmp[:, 0:64], dt_bias.partition_broadcast(P)).then_inc(S["rows_loaded"], 16)
            act.dma_start(dt_tmp[:, 64:128], a_log.partition_broadcast(P)).then_inc(S["rows_loaded"], 16)

            def first_slab(slot):
                act.wait_ge(raw_landed[slot], 16)
                activation(w_hi[:, slot, :], raw[:, slot, :], ACT.Copy).then_inc(S["hi_ready"], 1)

            act.wait_ge(S["x_loaded"], 16)
            activation(ga[:, 0:D], x_sb[:, 0, :], ACT.Square, accum_out=small[:, 0:1]).then_inc(S["ssq1_act"], 1)
            act.wait_ge(S["ssq1_act"], 1)
            act.wait_ge(S["ssq1_dve"], 1)
            act.wait_ge(S["tables_loaded"], 32)
            activation(small[:, 2:4], small[:, 0:2], ACT.Sqrt, scale=1.0 / D, bias=const[:, C_EPS:C_EPS + 1]) \
                .then_inc(S["std1_ready"], 1)
            act.wait_ge(S["rstd1_ready"], 1)

            def norm_piece(n):
                cols = slice(n * 512, (n + 1) * 512)
                activation(x_sb[:, 0, cols], x_sb[:, 0, cols], ACT.Copy, scale=small[:, 2:3]).then_inc(S["xn_act"], 1)

            def h_pair(r):
                act.wait_ge(S["xt_done"], r + 1)
                for k in (2 * r, 2 * r + 1):
                    activation(act16[:, k, 0:T], ps[4 + r % 4][:, (k % 2) * T:(k % 2 + 1) * T], ACT.Copy,
                               scale=chan[:, V_N1 + k:V_N1 + k + 1]).then_inc(S["h_hi"], 1)

            norm_piece(0)
            first_slab(0)
            norm_piece(1)
            for n in range(4):
                h_pair(2 * n)
                h_pair(2 * n + 1)
                if n + 1 < RING:
                    first_slab(n + 1)
                if n + 2 < 4:
                    norm_piece(n + 2)

            for x in range(20):
                if x == 15:
                    act.wait_ge(S["slab_used"], 16)
                    for t in range(TT):
                        activation(vs[:, t, :], ps[2 + t][:, :], ACT.Copy).then_inc(bank_free[2 + t], 1)
                if x == 19:
                    act.wait_ge(S["rows_loaded"], 80)
                    activation(dt_tmp[:, 64:128], dt_tmp[:, 64:128], ACT.Exp).then_inc(S["neg_a"], 1)
                    act.wait_ge(S["dt_v"], 1)
                    activation(dt_tmp[:, 256:384], dt_tmp[:, 256:384], ACT.Exp, scale=-1.0).then_inc(S["dt_e"], 1)
                split("kv", 0, x)

            def attention(i, x):
                if not out_of(i, 2, N_KV + 2):
                    j = i - 2
                    if x == 1:
                        act.wait_ge(S["shift_ready"], j + 1)
                        for g in range(GQ):
                            activation(p0[:, g, :], p0[:, g, :], ACT.Exp, scale=0.125, bias=negm[:, g:g + 1],
                                       accum_out=rsum[:, g:g + 1])
                            activation(p1[:, g, :], p1[:, g, :], ACT.Exp, scale=0.125, bias=negm[:, 4 + g:5 + g],
                                       accum_out=rsum[:, 4 + g:5 + g])
                        activation(es, es, ACT.Exp).then_inc(S["exp_done"], 1)
                    if x == "probs":
                        act.wait_ge(S["pt_done"], j + 1)
                        activation(pt[:, 0, :], ps[PT_BANKS[0]][:, :], ACT.Copy)
                        activation(pt[:, 2, :], ps[PT_BANKS[2]][:, :], ACT.Copy).then_inc(S["pt_act"], 1)
                    if x == "values":
                        act.wait_ge(S["pv_done"], j + 1)
                        activation(act32[:, bass.ds(2 * j, 2), 0:T], ps[7][:, :].rearrange("p (f t) -> p f t", f=2),
                                   ACT.Copy).then_inc(S["attn_hi"], 1)

            def q_body(i):
                for x in range(4):
                    if x == 3:
                        attention(i, "probs")
                        act.wait_ge(S["slab_used"], slab_no("q", i, 3) + 1)
                        if not is_step(i, 0):
                            act.wait_ge(S["scores_done"], i)
                        activation(qt[:, :, :], ps[2][:, :].rearrange("p (f t) -> p f t", f=2), ACT.Copy) \
                            .then_inc(bank_free[2], 1)
                        attention(i, "values")
                        act.wait_ge(bank_free[2], bank_use("q", i, 0, 2) + 1)
                        for c in range(2):
                            half = slice(64 * c, 64 * c + 64)
                            last = activation(q2[half, :, c, :], qt[half, :, :], ACT.Copy)
                        last.then_inc(S["q_hi"], 1)
                    attention(i, x)
                    if is_step(i, 1) and x == 2:
                        act.wait_ge(S["acs_copied"], 1)
                        act.dma_start(acs_dram.rearrange("c (h l) -> h c l", h=SSD_HEADS),
                                      acs_h.rearrange("h (c l) -> h c l", c=N_CHUNKS)).then_inc(S["acs_stored"], 16)
                    if is_step(i, 1) and x == 0:
                        act.wait_ge(S["acs_ready"], 1)
                        activation(ea_t[:, :, :], acs_t[:, :, :], ACT.Exp).then_inc(S["dec_ready"], 1)
                        act.wait_ge(S["dec_in"], 1)
                        activation(dec_t[:, :, :], dec_t[:, :, :], ACT.Exp)
                        for odd in range(2):
                            last = activation(cdec[:, odd::2, :], ps[5 + odd][:, 0:128].rearrange("p (c h) -> p c h", c=2),
                                              ACT.Exp)
                        last.then_inc(S["dec_ready"], 1)
                    split("q", i, x)
            loop(act, "q", q_body, peel=2)

            def gates(phase, dst, col, side, late=False):
                def body(i):
                    for k in range(2):
                        for x in range(4 * k, 4 * k + 4):
                            if is_step(i, 0) and not late:
                                side(x)
                            if x == 4 * k + 3:
                                bank = PLAN[phase]["jobs"][k][1][0]
                                if phase == "gate_s" and isinstance(i, int):
                                    act.wait_ge(S["y_ready"], 2 * GROUPS)
                                act.wait_ge(S["slab_used"], slab_no(phase, i, x) + 1)
                                for f in range(2):
                                    ft = 4 * i + (2 * k + f)
                                    last = activation(dst[:, bass.ds(ft, 1), :],
                                                      ps[bank][:, f * T:(f + 1) * T].unsqueeze(1), ACT.Tanh, scale=0.5,
                                                      bias=chan[:, bass.ds(ft + col, 1)])
                                last.then_inc(bank_free[bank], 1)
                            if is_step(i, 0) and late:
                                side(x)
                            split(phase, i, x)
                loop(act, phase, body, peel=1)
            act.wait_ge(S["half_ready"], 1)
            act.wait_ge(S["acs_stored"], 16)

            def attention_end(x):
                for part in (("probs", "values") if x % 4 == 3 else (x % 4,)):
                    attention(N_KV + x // 4, part)
            gates("gate_a", ga_f, V_GB, attention_end, late=True)

            def splits(phase):
                def body(i):
                    for x in range(PLAN[phase]["slabs"]):
                        split(phase, i, x)
                return body
            def load_rows(g):
                for c in range(N_CHUNKS):
                    act.dma_start(acs_rows[64 * (c % 2):64 * (c % 2) + 64, c // 2, :],
                                  acs_dram[c, bass.ds(g * GW, GW)].partition_broadcast(64)).then_inc(S["rows_landed"], 16)

            act.wait_ge(S["pt_done"], N_KV)
            load_rows(0)
            loop(act, "attn_out", splits("attn_out"))

            def conv_in(phase, i, x, bank, f0):
                act.wait_ge(S["slab_used"], slab_no(phase, i, x) + 1)
                activation(upad[:, f0:f0 + 2, 4:4 + T], ps[bank][:, :].rearrange("p (f t) -> p f t", f=2), ACT.Copy) \
                    .then_inc(bank_free[bank], 1)

            act.wait_ge(S["pad_zero"], 1)
            for x in range(8):
                if x == 3:
                    conv_in("first_group", 0, 3, 0, 4)
                if x == 4:
                    act.wait_ge(S["conv_bc"], 8)
                    activation(th[:, 4:6, :], cv[:, 4:6, :], ACT.Tanh).then_inc(S["th_bc"], 1)
                if x == 7:
                    conv_in("first_group", 0, 7, 1, 0)
                split("first_group", 0, x)

            def ssd(g, x, phase, i, last=False):
                if x == 1:
                    act.wait_ge(S["cb_done"], g + 1)
                    for c in range(3):
                        rows = slice(64 * (c % 2), 64 * (c % 2) + 64)
                        for half in (slice(0, 64), slice(64, P)):
                            last = activation(b2[c][half, 0, :], ps[6][rows, (1 + c // 2) * P:(2 + c // 2) * P], ACT.Copy)
                    last.then_inc(S["b_hi"], 1)
                if x == 9:
                    act.wait_ge(S["xdec_ready"], g + 1)
                    for c in range(3):
                        rows = slice(64 * (c % 2), 64 * (c % 2) + 64)
                        last = activation(x2[rows, c, :], xdec[rows, c // 2, :], ACT.Copy)
                    last.then_inc(S["x_hi"], 1)
                if x == 3:
                    conv_in(phase, i, 3, 0, 2)
                    act.wait_ge(S["seg_out"], 2 * g + 2)
                    activation(mt[:, :, :], mt[:, :, :], ACT.Relu, scale=-1.0).then_inc(S["seg_min"], 1)
                    act.wait_ge(S["seg_min"], g + 1)
                    activation(mt[:, :, :], mt[:, :, :], ACT.Exp, scale=-1.0).then_inc(S["seg_exp"], 1)
                if x == 5:
                    act.wait_ge(S["conv_xb"], 8 * g + 8)
                    activation(th[:, 0:4, :], cv[:, 0:4, :], ACT.Tanh).then_inc(S["th_x"], 1)
                if x == 11:
                    act.wait_ge(S["st_done"], g + 1)
                    activation(prev[:, 0, :], ps[4][:, :], ACT.Copy).then_inc(S["prev1"], 1)
                    act.wait_ge(S["slab_used"], slab_no(phase, i, 11) + 1)
                    for t in range(TT):
                        activation(sz[:, t, :], ps[2 + t][:, :], ACT.Tanh, scale=0.5).then_inc(S["tz_ready"], 1)
                if x == 15 and not last:
                    conv_in(phase, i, 15, 0, 4)
                if x == 17:
                    act.wait_ge(S["rstd_g"], g + 1)
                    for t in range(TT):
                        activation(yb[:, t, :], yb[:, t, :], ACT.Copy, scale=small[:, 8 + t:9 + t]).then_inc(S["yn_ready"], 1)
                if x == 17 and not last:
                    act.wait_ge(S["conv_bc"], 8 * g + 16)
                    activation(th[:, 4:6, :], cv[:, 4:6, :], ACT.Tanh).then_inc(S["th_bc"], 1)
                if x == 16:
                    for t in range(TT):
                        act.wait_ge(S["y_ready"], 2 * g + t + 1)
                        activation(xdt[:, t, :], yb[:, t, :], ACT.Square, accum_out=small[:, 4 + t:5 + t]) \
                            .then_inc(S["ssq_g"], 1)
                    act.wait_ge(S["ssq_g"], 2 * g + 2)
                    activation(small[:, 6:8], small[:, 4:6], ACT.Sqrt, scale=1.0 / GW, bias=const[:, C_EPS4:C_EPS4 + 1]) \
                        .then_inc(S["std_g"], 1)
                    if not last:
                        load_rows(g + 1)
                if x == 19:
                    act.wait_ge(S["yt_done"], g + 1)
                    for f in range(4):
                        activation(act32[:, bass.ds(4 * g + f, 1), 0:T],
                                   ps[6 + f // 2][:, (f % 2) * T:(f % 2 + 1) * T].unsqueeze(1), ACT.Copy,
                                   scale=chan[:, bass.ds(4 * g + (V_SN + f), 1)]).then_inc(S["y_hi"], 1)
                    if not last:
                        conv_in(phase, i, 19, 1, 0)

            def group_body(i):
                for x in range(20):
                    ssd(i, x, "group", i)
                    split("group", i, x)
            loop(act, "group", group_body)
            for x in range(12):
                ssd(GROUPS - 1, x, "last_group", 0, last=True)
                split("last_group", 0, x)
            gates("gate_s", gs, V_GB + KD, lambda x: ssd(GROUPS - 1, x + 12, None, None, last=True))

            def ssd_out_body(i):
                for k in range(2):
                    for x in range(8 * k, 8 * k + 8):
                        if x == 8 * k + 7:
                            act.wait_ge(S["m_sum"], 2 * i + (k + 1))
                            activation(act16[:, bass.ds(4 * i + 2 * k, 2), 0:T], ga_f[:, bass.ds(4 * i + 2 * k, 2), :],
                                       ACT.Copy, scale=0.5).then_inc(S["m_hi"], 1)
                        split("ssd_out", i, x)
            loop(act, "ssd_out", ssd_out_body)

            def x2_side(nb):
                for q in range(2):
                    r = 2 * nb + q
                    act.wait_ge(S["x2t_done"], r + 1)
                    for k in (2 * r, 2 * r + 1):
                        activation(act32[:, k, 0:T], ps[4 + r % 4][:, (k % 2) * T:(k % 2 + 1) * T], ACT.Copy,
                                   scale=chan[:, V_N2 + k:V_N2 + k + 1]).then_inc(S["h2_hi"], 1)

            def squares(phase, job, nb, done, tiles=TT):
                for b in PLAN[phase]["jobs"][job][1]:
                    act.wait_ge(bank_free[b], bank_use(phase, 0, job, b) + 1)
                for t in range(tiles):
                    n = 2 * nb + t
                    if n >= 4:
                        act.wait_ge(S[done], n - 3)
                    activation(junk[:, (n % 4) * 512:(n % 4 + 1) * 512], x_sb[:, t, nb * 512:(nb + 1) * 512], ACT.Square,
                               accum_out=ssq[:, t, nb:nb + 1]).then_inc(S[done], 1)
            for n in range(4):
                for x in range(8 * n, 8 * n + 8):
                    if n and x == 8 * n + 1:
                        x2_side(n - 1)
                    if x == 8 * n + 7:
                        squares("out", n, n, "sq2_ready")
                    split("out", 0, x)

            def end_of_norm():
                x2_side(3)
                act.wait_ge(S["ssq2_sum"], 1)
                activation(small[:, 12:14], small[:, 10:12], ACT.Sqrt, scale=1.0 / D, bias=const[:, C_EPS:C_EPS + 1]) \
                    .then_inc(S["std2"], 1)

            def up(phase, dst, ft0):
                def body(i):
                    for k in range(2):
                        for x in range(4 * k, 4 * k + 4):
                            if phase == "up_a0" and is_step(i, 0) and x == 0:
                                end_of_norm()
                            if x == 4 * k + 3:
                                bank = PLAN[phase]["jobs"][k][1][0]
                                act.wait_ge(bank_free[bank], bank_use(phase, i, k, bank) + 1)
                                activation(dst[:, bass.ds(4 * i + (ft0 + 2 * k), 2), 0:T],
                                           tu[:, k, :].rearrange("p (f t) -> p f t", f=2), ACT.Square) \
                                    .then_inc(S["u_hi"], 1)
                            split(phase, i, x)
                loop(act, phase, body, peel=1 if phase == "up_a0" else 0)
            up("up_a0", act32, 16)
            up("up_a1", act16, 0)
            loop(act, "down_a", splits("down_a"))
            up("up_b0", act32, 16)
            up("up_b1", act16, 0)
            for phase, nb0 in (("down_b", 0), ("down_end", 2)):
                for k in range(2):
                    for x in range(16 * k, 16 * k + 16):
                        if x == 16 * k + 15:
                            squares(phase, k, nb0 + k, "sq3_ready", TT if nb0 + k < 3 else 1)
                        split(phase, 0, x)
                if nb0 == 0:
                    activation(small[:, 24:25], const[:, C_EPS:C_EPS + 1], ACT.Sqrt)
            act.wait_ge(S["ssq3_sum"], 1)
            activation(small[:, 20:22], small[:, 18:20], ACT.Sqrt, scale=1.0 / D, bias=const[:, C_EPS:C_EPS + 1]) \
                .then_inc(S["std3"], 1)
            act.wait_ge(S["rstd3"], 1)
            act.wait_ge(S["x3_w"], 8)
            for n in range(4):
                cols = slice(n * 512, (n + 1) * 512)
                activation(x_sb[:, 0, cols], x_sb[:, 0, cols], ACT.Copy, scale=small[:, 22:23]).then_inc(S["out_act"], 1)

        @block.vector
        def _(dve):
            v = nc.vector
            stt = v.scalar_tensor_tensor
            tt = v.tensor_tensor

            def split(phase, i, x):
                n = slab_no(phase, i, x)
                if isinstance(n, int) and n + RING >= N_SLABS:
                    return
                w = width_of(n)
                slot = x % RING
                dve.wait_ge(S["hi_ready"], n + RING + 1)
                tt(w_lo[:, slot, 0:w], raw[:, slot, 0:w], w_hi[:, slot, 0:w].bitcast(F32), ALU.subtract) \
                    .then_inc(S["lo_ready"], 1)

            def f2(ap):
                return ap.rearrange("p (f t) -> p f t", f=2)

            chain = Chain(dve, sem("dve_step"))

            def first_slab(slot):
                dve.wait_ge(S["hi_ready"], slot + 1)
                tt(w_lo[:, slot, :], raw[:, slot, :], w_hi[:, slot, :].bitcast(F32), ALU.subtract) \
                    .then_inc(S["lo_ready"], 1)

            v.memset(small[:, 26:27], 1.0).then_inc(S["one_set"], 1)
            for n in range(2):
                dve.wait_ge(S["x1_left" if n == 0 else "x1_right"], 16)
                stt(out=ga[:, D + n * D // 2:D + (n + 1) * D // 2], in0=x_sb[:, 1, n * D // 2:(n + 1) * D // 2],
                    scalar=1.0, in1=x_sb[:, 1, n * D // 2:(n + 1) * D // 2], op0=ALU.mult, op1=ALU.mult,
                    accum_out=small[:, 16 + n:17 + n]).then_inc(S["ssq1_part"], 1)
            dve.wait_ge(S["ssq1_part"], 2)
            tt(small[:, 1:2], small[:, 16:17], small[:, 17:18], ALU.add).then_inc(S["ssq1_dve"], 1)
            dve.wait_ge(S["std1_ready"], 1)
            v.reciprocal(small[:, 2:4], small[:, 2:4]).then_inc(S["rstd1_ready"], 1)
            dve.wait_ge(S["rstd1_ready"], 1)

            def norm_piece(n):
                cols = slice(n * 512, (n + 1) * 512)
                v.tensor_scalar(x_sb[:, 1, cols], x_sb[:, 1, cols], small[:, 3:4], None, ALU.mult).then_inc(S["xn_dve"], 1)

            def h_pair(r):
                dve.wait_ge(S["h_hi"], 2 * r + 2)
                for k in (2 * r, 2 * r + 1):
                    stt(out=act16[:, k, T:2 * T], in0=ps[4 + r % 4][:, (k % 2) * T:(k % 2 + 1) * T],
                        scalar=chan[:, V_N1 + k:V_N1 + k + 1], in1=act16[:, k, 0:T].bitcast(F32), op0=ALU.mult,
                        op1=ALU.subtract).then_inc(S["h_lo"], 1)

            norm_piece(0)
            first_slab(0)
            norm_piece(1)
            for n in range(4):
                h_pair(2 * n)
                h_pair(2 * n + 1)
                if n + 1 < RING:
                    first_slab(n + 1)
                if n + 2 < 4:
                    norm_piece(n + 2)
            v.tensor_scalar(chan[:, V_GB:V_SN], chan[:, V_GB:V_SN], 0.5, None, ALU.mult).then_inc(S["half_ready"], 1)

            a_exp, bias_b = dt_tmp[:, 64:128], dt_tmp[:, 0:64]
            val, e, sq, pol = [dt_tmp[:, 128 * n:128 * n + 128] for n in (1, 2, 3, 4)]
            v3 = lambda ap: ap.rearrange("p (t h) -> p t h", t=TT)
            for x in range(20):
                if x in (3, 7):
                    b = x // 4
                    dve.wait_ge(S["slab_used"], x + 1)
                    for par in range(2):
                        for half in range(2):
                            last = v.tensor_copy(ks[64 * half:64 * half + 64, 2 * b:2 * b + 2, par, :],
                                                 f2(ps[b][64 * par:64 * par + 64, :]))
                    last.then_inc(bank_free[b], 1)
                if x == 19:
                    dve.wait_ge(S["slab_used"], 20)
                    dve.wait_ge(S["rows_loaded"], 80)
                    for t in range(TT):
                        tt(v3(val)[:, t, :], ps[t][:, 0:64], bias_b, ALU.add).then_inc(bank_free[t], 1)
                    dve.wait_ge(bank_free[0], 2)
                    dve.wait_ge(bank_free[1], 2)
                    stt(out=e, in0=val, scalar=-1.0, in1=val, op0=ALU.mult, op1=ALU.max).then_inc(S["dt_v"], 1)
                    dve.wait_ge(S["dt_e"], 1)
                    chain.link(v.tensor_scalar(sq, e, 2.0, None, ALU.add))
                    chain.link(v.reciprocal(sq, sq))
                    chain.link(tt(e, e, sq, ALU.mult))
                    chain.link(tt(sq, e, e, ALU.mult))
                    chain.link(v.tensor_scalar(pol, sq, 1.0 / 17, None, ALU.mult))
                    for c in (15, 13, 11, 9, 7, 5, 3):
                        chain.link(stt(out=pol, in0=pol, scalar=1.0 / c, in1=sq, op0=ALU.add, op1=ALU.mult))
                    chain.link(stt(out=pol, in0=pol, scalar=1.0, in1=e, op0=ALU.add, op1=ALU.mult))
                    chain.link(v.tensor_scalar(val, val, 0.0, None, ALU.max))
                    chain.link(stt(out=dt_t[:, :, :], in0=v3(pol), scalar=2.0, in1=v3(val), op0=ALU.mult, op1=ALU.add))
                    dve.wait_ge(S["neg_a"], 1)
                    stt(out=a_t[:, :, :], in0=dt_t[:, :, :], scalar=-1.0,
                        in1=a_exp.unsqueeze(1).to_broadcast([P, TT, SSD_HEADS]), op0=ALU.mult, op1=ALU.mult) \
                        .then_inc(S["a_ready"], 1)
                split("kv", 0, x)
            attn0 = chain.n
            ATTN_STEPS = 5

            def attention(i, x):
                if x == 1 and not out_of(i, 1, N_KV + 1):
                    dve.wait_ge(S["q_hi"], i)
                    for c in range(2):
                        half, other = slice(64 * c, 64 * c + 64), slice(64 - 64 * c, 128 - 64 * c)
                        last = tt(q2[other, :, c, :], qt[half, :, :], q2[half, :, c, :].bitcast(F32), ALU.subtract)
                    last.then_inc(S["q_lo"], 1)
                    dve.wait_ge(S["kc_hi"], i)
                    tt(kc[:, 1:2, :], scr[:, 0:2048].rearrange("p (j t) -> p j t", j=N_KV)[:, bass.ds(i - 1, 1), :],
                       kc[:, 0:1, :].bitcast(F32), ALU.subtract).then_inc(S["kc_ready"], 1)
                if not out_of(i, 2, N_KV + 2):
                    j = i - 2
                    chain.at(attn0 + j * ATTN_STEPS)
                    if x == 1:
                        dve.wait_ge(S["exp_done"], j + 1)
                        chain.n = 3
                        chain.link(tt(den, rsum, es, ALU.add))
                        chain.link(v.reciprocal(rden, den))
                        tt(p0[:, :, :], p0[:, :, :], rden[:, 0:4].unsqueeze(2).to_broadcast([P, GQ, P]), ALU.mult)
                        tt(p1[:, :, :], p1[:, :, :], rden[:, 4:8].unsqueeze(2).to_broadcast([P, GQ, T]), ALU.mult) \
                            .then_inc(S["probs_ready"], 1)
                    if x == 3:
                        dve.wait_ge(S["pt_done"], j + 1)
                        v.tensor_copy(pt[:, 1, :], ps[PT_BANKS[1]][:, :]).then_inc(S["pt_dve"], 1)
                if x == 3 and not out_of(i, 1, N_KV + 1):
                    j = i - 1
                    chain.at(attn0 + j * ATTN_STEPS)
                    dve.wait_ge(S["scores_done"], j + 1)
                    for g in range(GQ):
                        slope = const[:, bass.ds(4 * j + (C_SLOPE + g), 1)]
                        stt(out=p0[:, g, :], in0=negd[0], scalar=slope, in1=ps[4][:, g * P:(g + 1) * P],
                            op0=ALU.mult, op1=ALU.add)
                        last = stt(out=p1[:, g, :], in0=negd[1], scalar=slope,
                                   in1=ps[5 + g % 2][:, (g // 2) * T:(g // 2 + 1) * T], op0=ALU.mult, op1=ALU.add)
                    chain.link(last)
                    v.tensor_reduce(mx[:, 0:4], p0[:, :, :], AX, ALU.max)
                    chain.link(v.tensor_reduce(mx[:, 4:8], p1[:, :, :], AX, ALU.max))
                    sink = sink_b[:, bass.ds(4 * j, 4)].unsqueeze(1).to_broadcast([P, 2, 4])
                    two = lambda ap: ap.rearrange("p (t g) -> p t g", t=2)
                    chain.link(stt(out=two(mm_), in0=two(mx), scalar=0.125, in1=sink, op0=ALU.mult, op1=ALU.max))
                    tt(two(es), sink, two(mm_), ALU.subtract)
                    v.tensor_scalar(negm, mm_, -1.0, None, ALU.mult).then_inc(S["shift_ready"], 1)
                    chain.n = 0
                if x == 3 and not out_of(i, 2, N_KV + 2):
                    j = i - 2
                    dve.wait_ge(S["attn_hi"], j + 1)
                    tt(act32[:, bass.ds(2 * j, 2), T:2 * T], f2(ps[7][:, :]),
                       act32[:, bass.ds(2 * j, 2), 0:T].bitcast(F32), ALU.subtract).then_inc(S["attn_lo"], 1)

            def q_body(i):
                for x in range(4):
                    attention(i, x)
                    if is_step(i, 1) and x == 0:
                        dve.wait_ge(S["cums_done"], 1)
                        v.tensor_copy(acs_t[:, :, :], ps[7][:, 0:128].rearrange("p (t h) -> p t h", t=TT)) \
                            .then_inc(S["acs_ready"], 1)
                        dve.wait_ge(S["acs_ready"], 1)
                        tt(dec_t[:, :, :], ps[7][:, 128:256].rearrange("p (t h) -> p t h", t=TT), acs_t[:, :, :],
                           ALU.subtract).then_inc(S["dec_in"], 1)
                    if is_step(i, 1) and x == 1:
                        dve.wait_ge(S["acs_tr"], 1)
                        v.tensor_copy(acs_h, ps[4][0:SSD_HEADS, 0:T]).then_inc(S["acs_copied"], 1)
                    split("q", i, x)
            loop(dve, "q", q_body, peel=2)

            def gate_a_body(i):
                for x in range(8):
                    if is_step(i, 0):
                        attention(N_KV + x // 4, x % 4)
                    split("gate_a", i, x)
            loop(dve, "gate_a", gate_a_body, peel=1)

            def attn_out_body(i):
                for k in range(2):
                    for x in range(4 * k, 4 * k + 4):
                        if x == 4 * k + 3:
                            bank = PLAN["attn_out"]["jobs"][k][1][0]
                            dve.wait_ge(S["slab_used"], slab_no("attn_out", i, x) + 1)
                            dst = ga_f[:, bass.ds(4 * i + 2 * k, 2), :]
                            stt(out=dst, in0=dst, scalar=1.0, in1=f2(ps[bank][:, :]), op0=ALU.add, op1=ALU.mult) \
                                .then_inc(bank_free[bank], 1)
                        split("attn_out", i, x)
            dve.wait_ge(bank_free[2], bank_use("attn_out", 0, 0, 2))
            dve.wait_ge(bank_free[3], bank_use("attn_out", 0, 1, 3))
            loop(dve, "attn_out", attn_out_body)

            v.memset(upad[:, :, 0:4], 0.0).then_inc(S["pad_zero"], 1)

            def conv(fts, cols, done, base):
                step = 0
                for tap in range(CONV_K):
                    for n, f in enumerate(fts):
                        src = upad[:, f, 1 + tap:1 + tap + T]
                        w = chan[:, bass.ds(cols[n] * CONV_K + (V_CW + tap), 1)]
                        if tap == 0:
                            ins = v.tensor_scalar(cv[:, f, :], src, w, chan[:, bass.ds(cols[n] + V_CB, 1)], ALU.mult, ALU.add)
                        else:
                            dve.wait_ge(S[done], base + step - len(fts) + 1)
                            ins = stt(out=cv[:, f, :], in0=src, scalar=w, in1=cv[:, f, :], op0=ALU.mult, op1=ALU.add)
                        ins.then_inc(S[done], 1)
                        step += 1

            def conv_bc(g, n, phase, i, job):
                dve.wait_ge(bank_free[0], bank_use(phase, i, job, 0) + 1)
                conv([4, 5], [g + 32, g + 40], "conv_bc", n * 8)

            def silu_bc(n):
                dve.wait_ge(S["th_bc"], n + 1)
                stt(out=cv[:, 4:6, :], in0=th[:, 4:6, :], scalar=1.0, in1=cv[:, 4:6, :], op0=ALU.add, op1=ALU.mult) \
                    .then_inc(S["silu_bc"], 1)

            def conv_x(g, which, n, phase, i, job):
                bank = 1 - which
                dve.wait_ge(bank_free[bank], bank_use(phase, i, job, bank) + 1)
                f = 2 * which
                conv([f, f + 1], [4 * g + f, 4 * g + (f + 1)], "conv_xa" if which == 0 else "conv_xb", n * 8)

            for x in range(8):
                if x == 3:
                    conv_bc(0, 0, "first_group", 0, 0)
                if x == 5:
                    silu_bc(0)
                if x == 7:
                    conv_x(0, 0, 0, "first_group", 0, 1)
                split("first_group", 0, x)

            heads = lambda ap: ap.rearrange("p (h n) -> p h n", h=HPG)

            def per_head(table, t, g, rows=slice(0, P)):
                n = rows.stop - rows.start
                return table[rows, t, bass.ds(g * HPG, HPG)].unsqueeze(2).to_broadcast([n, HPG, 64])

            def ssd(g, x, phase, i, last=False):
                if x == 1 or x == 2:
                    t = x - 1
                    dve.wait_ge(S["cb_done"], g + 1)
                    dve.wait_ge(S["rows_landed"], 64 * (g + 1))
                    tt(heads(mt[:, t, :]), heads(acs_rows[:, t, :]), per_head(acs_t, t, g), ALU.subtract) \
                        .then_inc(S["seg_out"], 1)
                if x == 2:
                    dve.wait_ge(S["b_hi"], g + 1)
                    for c in range(3):
                        rows = slice(64 * (c % 2), 64 * (c % 2) + 64)
                        for half in (slice(0, 64), slice(64, P)):
                            last = tt(b2[c][half, 1, :], ps[6][rows, (1 + c // 2) * P:(2 + c // 2) * P],
                                      b2[c][rows, 0, :].bitcast(F32), ALU.subtract)
                    last.then_inc(S["b_lo"], 1)
                    tt(cbm[:, :, :], ps[6][:, 0:P].rearrange("p (t l) -> p t l", t=TT),
                       tri.unsqueeze(1).to_broadcast([P, TT, 64]), ALU.mult).then_inc(S["cbm_ready"], 1)
                if x == 3:
                    conv_x(g, 1, g, phase, i, 0)
                if x == 6:
                    dve.wait_ge(S["th_x"], g + 1)
                    stt(out=cv[:, 0:4, :], in0=th[:, 0:4, :], scalar=1.0, in1=cv[:, 0:4, :], op0=ALU.add, op1=ALU.mult) \
                        .then_inc(S["silu_x"], 1)
                if x == 7:
                    dve.wait_ge(S["xt_tr"], g + 1)
                    for t in range(TT):
                        src = heads(ps[7 - t][:, :])
                        tt(heads(xdt[:, t, :]), src, per_head(dt_t, t, g), ALU.mult).then_inc(S["xs_used"], 1)
                        d = dskip_b[:, bass.ds(g * HPG, HPG)].unsqueeze(2).to_broadcast([P, HPG, 64])
                        tt(heads(xd[:, t, :]), src, d, ALU.mult).then_inc(S["xs_used"], 1)
                if x == 8:
                    dve.wait_ge(S["cbm_ready"], g + 1)
                    dve.wait_ge(S["seg_exp"], g + 1)
                    for t in range(TT):
                        tt(heads(mt[:, t, :]), heads(mt[:, t, :]),
                           cbm[:, t, :].unsqueeze(1).to_broadcast([P, HPG, 64]), ALU.mult).then_inc(S["mt_ready"], 1)
                if x == 9:
                    dve.wait_ge(S["x_hi"], g + 1)
                    for c in range(3):
                        rows = slice(64 * (c % 2), 64 * (c % 2) + 64)
                        other = slice(64 - rows.start, P - rows.start)
                        last = tt(x2[other, c, :], xdec[rows, c // 2, :], x2[rows, c, :].bitcast(F32), ALU.subtract)
                    last.then_inc(S["x_lo"], 1)
                if x == 11 or x == 12:
                    c = x - 10
                    dve.wait_ge(S["prev1"], g + 1)
                    if c == 2:
                        dve.wait_ge(S["prev2"], g + 1)
                    d = cdec[:, c, bass.ds(g * HPG, HPG)].unsqueeze(2).to_broadcast([P, HPG, 64])
                    tt(heads(prev[:, c, :]), heads(prev[:, c - 1, :]), d, ALU.mult).then_inc(S["prev_tmp"], 1)
                    dve.wait_ge(S["prev_tmp"], 2 * g + c)
                    tt(prev[:, c, :], prev[:, c, :], ps[4 + c][:, :], ALU.add).then_inc(S["prev2" if c == 1 else "prev3"], 1)
                if x == 12:
                    dve.wait_ge(S["yd0_done"], g + 1)
                    tt(yb[:, 0, :], ps[7][:, :], xd[:, 0, :], ALU.add).then_inc(S["y_part"], 1)
                if x == 11:
                    for t in range(TT):
                        dve.wait_ge(S["tz_ready"], 2 * g + t + 1)
                        stt(out=sz[:, t, :], in0=sz[:, t, :], scalar=1.0, in1=ps[2 + t][:, :], op0=ALU.add, op1=ALU.mult) \
                            .then_inc(bank_free[2 + t], 1)
                if x == 13:
                    dve.wait_ge(S["yd1_done"], g + 1)
                    tt(yb[:, 1, :], ps[4][:, :], xd[:, 1, :], ALU.add).then_inc(S["y_part"], 1)
                    for t in range(TT):
                        rows = slice(64, P) if t == 0 else slice(0, P)
                        tt(heads(mt[rows, t, :]), heads(ps[5 + t][rows, :]), per_head(ea_t, t, g, rows), ALU.mult) \
                            .then_inc(S["y_part"], 1)
                if x == 14:
                    dve.wait_ge(S["y_part"], 4 * g + 4)
                    for t in range(TT):
                        rows = slice(64, P) if t == 0 else slice(0, P)
                        tt(yb[rows, t, :], yb[rows, t, :], mt[rows, t, :], ALU.add).then_inc(S["y_tmp"], 1)
                    for t in range(TT):
                        dve.wait_ge(S["y_tmp"], 2 * g + t + 1)
                        if t == 0:
                            dve.wait_ge(bank_free[3], sz_uses(g))
                        tt(yb[:, t, :], yb[:, t, :], sz[:, t, :], ALU.mult).then_inc(S["y_ready"], 1)
                if x == 15 and not last:
                    conv_bc(g + 1, g + 1, phase, i, 2)
                if x == 16:
                    dve.wait_ge(S["std_g"], g + 1)
                    v.reciprocal(small[:, 8:10], small[:, 6:8]).then_inc(S["rstd_g"], 1)
                if x == 17 and not last:
                    silu_bc(g + 1)
                if x == 19:
                    for f in range(4):
                        dve.wait_ge(S["y_hi"], 4 * g + (2 * (f // 2) + 2))
                        ft = bass.ds(4 * g + f, 1)
                        stt(out=act32[:, ft, T:2 * T], in0=ps[6 + f // 2][:, (f % 2) * T:(f % 2 + 1) * T].unsqueeze(1),
                            scalar=chan[:, bass.ds(4 * g + (V_SN + f), 1)], in1=act32[:, ft, 0:T].bitcast(F32),
                            op0=ALU.mult, op1=ALU.subtract).then_inc(S["y_lo"], 1)
                    if not last:
                        conv_x(g + 1, 0, g + 1, phase, i, 3)

            def sz_uses(g):
                return PLAN["group"]["use0"][3] + 1 + g * PLAN["group"]["uses"][3]

            def group_body(i):
                for x in range(20):
                    ssd(i, x, "group", i)
                    split("group", i, x)
            loop(dve, "group", group_body)
            for x in range(12):
                ssd(GROUPS - 1, x, "last_group", 0, last=True)
                split("last_group", 0, x)

            def gate_s_body(i):
                for x in range(8):
                    if is_step(i, 0):
                        ssd(GROUPS - 1, x + 12, None, None, last=True)
                    split("gate_s", i, x)
            loop(dve, "gate_s", gate_s_body, peel=1)

            dve.wait_ge(bank_free[0], bank_use("out", 0, 0, 0))
            dve.wait_ge(bank_free[1], bank_use("out", 0, 0, 1))

            def ssd_out_body(i):
                for k in range(2):
                    for x in range(8 * k, 8 * k + 8):
                        if x == 8 * k + 7:
                            bank = 2 + k
                            n = 2 * i + k
                            ft = bass.ds(4 * i + 2 * k, 2)
                            dve.wait_ge(S["slab_used"], slab_no("ssd_out", i, x) + 1)
                            stt(out=gs[:, ft, :], in0=gs[:, ft, :], scalar=1.0, in1=f2(ps[bank][:, :]), op0=ALU.add,
                                op1=ALU.mult).then_inc(bank_free[bank], 1)
                            dve.wait_ge(bank_free[bank], bank_use("ssd_out", i, k, bank) + 1)
                            tt(ga_f[:, ft, :], ga_f[:, ft, :], gs[:, ft, :], ALU.add).then_inc(S["m_sum"], 1)
                            dve.wait_ge(S["m_hi"], n + 1)
                            stt(out=act16[:, ft, T:2 * T], in0=ga_f[:, ft, :], scalar=0.5,
                                in1=act16[:, ft, 0:T].bitcast(F32), op0=ALU.mult, op1=ALU.subtract).then_inc(S["m_lo"], 1)
                        split("ssd_out", i, x)
            loop(dve, "ssd_out", ssd_out_body)

            def add_residual(phase, i, k, x, nb):
                dve.wait_ge(S["slab_used"], slab_no(phase, i, x) + 1)
                banks = PLAN[phase]["jobs"][k][1]
                for t in range(TT):
                    dst = x_sb[:, t, bass.ds(nb * 512, 512)]
                    tt(dst, dst, ps[banks[t]][:, :], ALU.add).then_inc(bank_free[banks[t]], 1)

            def x2_side(nb):
                for k in range(4 * nb, 4 * nb + 4):
                    dve.wait_ge(S["h2_hi"], 2 * (k // 2) + 2)
                    stt(out=act32[:, k, T:2 * T], in0=ps[4 + (k // 2) % 4][:, (k % 2) * T:(k % 2 + 1) * T],
                        scalar=chan[:, V_N2 + k:V_N2 + k + 1], in1=act32[:, k, 0:T].bitcast(F32), op0=ALU.mult,
                        op1=ALU.subtract).then_inc(S["h2_lo"], 1)
            for n in range(4):
                for x in range(8 * n, 8 * n + 8):
                    if n and x == 8 * n + 1:
                        x2_side(n - 1)
                    if x == 7:
                        dve.wait_ge(S["x_loaded"], 32)
                        dve.wait_ge(S["x1_left"], 32)
                    if x == 8 * n + 7:
                        add_residual("out", 0, n, x, n)
                    split("out", 0, x)

            def end_of_norm():
                x2_side(3)
                dve.wait_ge(S["sq2_ready"], 8)
                v.tensor_reduce(small[:, 10:12], ssq[:, :, :], AX, ALU.add).then_inc(S["ssq2_sum"], 1)
                dve.wait_ge(S["std2"], 1)
                v.reciprocal(small[:, 14:16], small[:, 12:14]).then_inc(S["rstd2"], 1)
                dve.wait_ge(S["rstd2"], 1)
                for t in range(TT):
                    last = v.tensor_scalar(diag[:, t, :], ident, small[:, 14 + t:15 + t], None, ALU.mult)
                last.then_inc(S["diag_ready"], 1)

            def up(phase, n0, dst, ft0):
                def body(i):
                    for k in range(2):
                        for x in range(4 * k, 4 * k + 4):
                            if phase == "up_a0" and is_step(i, 0) and x == 0:
                                end_of_norm()
                            if phase == "up_a0" and is_step(i, 0) and x == 2:
                                dve.wait_ge(S["rr_done"], 1)
                                v.tensor_copy(rrow, ps[4][:, 0:T]).then_inc(S["rr_ready"], 1)
                            if x == 4 * k + 3:
                                bank = PLAN[phase]["jobs"][k][1][0]
                                n = 2 * i + (n0 + k)
                                t = f2(tu[:, k, :])
                                if phase == "up_a0":
                                    dve.wait_ge(S["rr_ready"], 1)
                                dve.wait_ge(S["slab_used"], slab_no(phase, i, x) + 1)
                                stt(out=t, in0=f2(ps[bank][:, :]), scalar=0.0,
                                    in1=rrow.unsqueeze(1).to_broadcast([P, 2, T]), op0=ALU.max, op1=ALU.mult) \
                                    .then_inc(bank_free[bank], 1)
                                dve.wait_ge(bank_free[bank], bank_use(phase, i, k, bank) + 1)
                                dve.wait_ge(S["u_hi"], n + 1)
                                tt(t, t, t, ALU.mult).then_inc(S["u_sq"], 1)
                                dve.wait_ge(S["u_sq"], n + 1)
                                ft = bass.ds(4 * i + (ft0 + 2 * k), 2)
                                tt(dst[:, ft, T:2 * T], t, dst[:, ft, 0:T].bitcast(F32), ALU.subtract) \
                                    .then_inc(S["u_lo"], 1)
                            split(phase, i, x)
                loop(dve, phase, body, peel=1 if phase == "up_a0" else 0)

            def down_a_body(i):
                for k in range(2):
                    for x in range(16 * k, 16 * k + 16):
                        if x == 16 * k + 15:
                            add_residual("down_a", i, k, x, 2 * i + k)
                        split("down_a", i, x)
            up("up_a0", 0, act32, 16)
            up("up_a1", 8, act16, 0)
            loop(dve, "down_a", down_a_body)
            up("up_b0", 16, act32, 16)
            up("up_b1", 24, act16, 0)
            dve.wait_ge(S["wf_loaded"], 16)
            for phase, nb0 in (("down_b", 0), ("down_end", 2)):
                for k in range(2):
                    nb = nb0 + k
                    for x in range(16 * k, 16 * k + 16):
                        if x == 16 * k + 15:
                            add_residual(phase, 0, k, x, nb)
                        split(phase, 0, x)
                    cols = slice(nb * 512, (nb + 1) * 512)
                    if nb < 3:
                        for t in range(TT):
                            dve.wait_ge(S["sq3_ready"], 2 * nb + t + 1)
                            tt(x_sb[:, t, cols], x_sb[:, t, cols], wf[:, cols], ALU.mult).then_inc(S["x3_w"], 1)
                    else:
                        bank = PLAN[phase]["jobs"][k][1][1]
                        dve.wait_ge(bank_free[bank], bank_use(phase, 0, k, bank) + 1)
                        stt(out=junk[:, 1536:2048], in0=x_sb[:, 1, cols], scalar=1.0, in1=x_sb[:, 1, cols],
                            op0=ALU.mult, op1=ALU.mult, accum_out=ssq[:, 1, 3:4]).then_inc(S["sq3_dve"], 1)
                        dve.wait_ge(S["sq3_ready"], 7)
                        dve.wait_ge(S["sq3_dve"], 1)
            v.tensor_reduce(small[:, 18:20], ssq[:, :, :], AX, ALU.add).then_inc(S["ssq3_sum"], 1)
            for t in range(TT):
                tt(x_sb[:, t, cols], x_sb[:, t, cols], wf[:, cols], ALU.mult).then_inc(S["x3_w"], 1)
            dve.wait_ge(S["std3"], 1)
            v.reciprocal(small[:, 22:24], small[:, 20:22]).then_inc(S["rstd3"], 1)
            dve.wait_ge(S["x3_w"], 8)
            dve.wait_ge(S["rstd3"], 1)
            for n in range(4):
                cols = slice(n * 512, (n + 1) * 512)
                v.tensor_scalar(x_sb[:, 1, cols], x_sb[:, 1, cols], small[:, 23:24], None, ALU.mult) \
                    .then_inc(S["out_dve"], 1)

        @block.gpsimd
        def _(pool):
            g_ = nc.gpsimd
            ks_flat = scr[:, 0:2048].rearrange("p (j t) -> p j t", j=N_KV)
            pool.wait_ge(bank_free[0], 1)
            pool.wait_ge(bank_free[1], 1)
            pool.wait_ge(bank_free[2], 1)
            pool.wait_ge(bank_free[3], 1)

            def kv(j):
                first = is_step(j, 0)
                if not first:
                    pool.wait_ge(S["scores_done"], j)
                g_.tensor_copy(kc[:, 0:1, :], ks_flat[:, bass.ds(j, 1), :]).then_inc(S["kc_hi"], 1)
                if not first:
                    pool.wait_ge(S["pv_done"], j)
                g_.tensor_copy(vc[:, :, :], vs[:, :, bass.ds(j * HD, HD)]).then_inc(S["vc_ready"], 1)
            kv(0)
            with pool.Fori(1, N_KV) as j:
                kv(j)

            def ssd(g):
                pool.wait_ge(S["xs_used"], 4 * g + 4)
                for t in range(TT):
                    last = g_.tensor_tensor(xdec[:, t, :].rearrange("p (h l) -> p h l", h=HPG),
                                            xdt[:, t, :].rearrange("p (h l) -> p h l", h=HPG),
                                            dec_t[:, t, bass.ds(g * HPG, HPG)].unsqueeze(2).to_broadcast([P, HPG, 64]),
                                            ALU.mult)
                last.then_inc(S["xdec_ready"], 1)
            with pool.Fori(0, GROUPS) as g:
                ssd(g)


def kernel(**inputs):
    import numpy as _np
    import concourse.bacc as _bacc
    from concourse.bass_utils import run_bass_kernel_spmd as _run

    def columns(v):
        return _np.asarray(v).reshape(-1, P).T

    taps = _np.asarray(inputs["conv_w"]).reshape(CONV_K, -1, P).transpose(2, 1, 0).reshape(P, -1)
    channel_table = _np.ascontiguousarray(_np.concatenate(
        [columns(inputs["norm1_w"]), columns(inputs["gate_bias"]), taps, columns(inputs["conv_b"]),
         columns(inputs["ssd_norm_w"]), columns(inputs["norm2_w"])], axis=1))
    k, m = _np.arange(P)[:, None], _np.arange(P)[None, :]
    same = (k // CHUNK == m // CHUNK)
    table = _np.zeros((P, C_COLS + NEG_COLS), _np.float32)
    table[:, C_ID:C_ID + P] = (k == m)
    table[:, C_TRI:C_TRI + CHUNK] = (k % CHUNK <= m[:, :CHUNK])
    table[:, C_CUM:C_CUM + P] = same & (k <= m)
    table[:, C_BLK:C_BLK + P] = same
    for t, c in ((0, C_NEG), (1, C_NEG + P)):
        q, s = _np.arange(P)[:, None] + t * P, _np.arange((t + 1) * P)[None, :]
        ahead = q // CHUNK - s // CHUNK
        table[:, c:c + (t + 1) * P] = _np.where((ahead == 0) | (ahead == 1), -_np.abs(q - s), -1e30)
    table[:, C_SLOPE:C_SLOPE + N_HEADS] = 8.0 * 2.0 ** (-8.0 * _np.arange(1, N_HEADS + 1) / N_HEADS)
    table[:, C_EPS], table[:, C_EPS4] = EPS, 4 * EPS
    table[:, C_ONE:C_ONE + P] = 1.0

    nc = _bacc.Bacc("TRN2", target_bir_lowering=False, num_devices=1)
    arrays, args = {}, []
    for name in ["x", "w_in", "w_o_attn", "w_o_ssd", "w_out", "w_up", "w_down", "attn_sinks", "dt_bias", "a_log",
                 "d_skip", "norm_final_w"]:
        arrays[f"in_{name}"] = _np.ascontiguousarray(inputs[name])
    arrays["channel_table"], arrays["shape_table"] = channel_table, table
    for name, a in arrays.items():
        args.append(nc.dram_tensor(name, a.shape, mybir.dt.from_np(a.dtype), kind="ExternalInput").ap())
    args.append(nc.dram_tensor("acs_dram", (N_CHUNKS, SSD_HEADS * CHUNK), F32, kind="Internal").ap())
    args.append(nc.dram_tensor("out", (1, T, D), F32, kind="ExternalOutput").ap())
    hybrid_block(nc, *args)
    r = _run(nc, [arrays], core_ids=[0])
    return r.results[0]["out"]
```
